# Optimizing a Trainium2 kernel written in Bass

```python
import math
import jax, jax.numpy as jnp
from jax import lax
import numpy as np

D_MODEL = 1024
BATCH = 1
SEQ = 256
DEPTH = 1

D_RNN = D_MODEL
RNN_BLOCKS = 8
RNN_BLOCK_W = D_RNN // RNN_BLOCKS
CONV_RNN = 4
RG_LRU_C = 8.0
DIFF_HEADS = 4
DIFF_HEAD_DIM = 64
DIFF_QK = DIFF_HEADS * 2 * DIFF_HEAD_DIM
DIFF_WIDTH = DIFF_HEADS * 2 * DIFF_HEAD_DIM
FOX_HEADS = 8
FOX_HEAD_DIM = 64
FOX_WIDTH = FOX_HEADS * FOX_HEAD_DIM
N_BUCKETS = 32
MAX_EXACT = N_BUCKETS // 2
MAX_DISTANCE = 128
Q_BLOCK = 128
D_FF = ((8 * D_MODEL // 3 + 127) // 128) * 128
CONV_FFN = 3
N_BRANCH = 3
EPS = 1e-6

IN_WIDTHS = (D_RNN, D_RNN, DIFF_QK, DIFF_QK, DIFF_WIDTH, FOX_WIDTH, FOX_WIDTH, FOX_WIDTH, FOX_HEADS, N_BRANCH * D_MODEL)
N_IN = int(sum(IN_WIDTHS))
IN_SPLITS = tuple(int(v) for v in np.cumsum(IN_WIDTHS)[:-1])


def rmsnorm(x, g):
    xf = x.astype(jnp.float32)
    y = xf * lax.rsqrt(jnp.mean(xf * xf, axis=-1, keepdims=True) + EPS)
    return (y * g.astype(jnp.float32)).astype(x.dtype)

def causal_dwconv(x, w, b):
    k = w.shape[0]
    s = x.shape[1]
    xp = jnp.pad(x, ((0, 0), (k - 1, 0), (0, 0)))
    y = b + xp[:, 0:s] * w[0]
    for j in range(1, k):
        y = y + xp[:, j:j + s] * w[j]
    return y

def _to_blocks(t):
    b, s = t.shape[:2]
    return jnp.moveaxis(t.reshape(b, s // Q_BLOCK, Q_BLOCK, *t.shape[2:]), 1, 0)

def _from_blocks(t):
    nb, b = t.shape[:2]
    t = jnp.moveaxis(t, 0, 1)
    return t.reshape(b, nb * Q_BLOCK, *t.shape[3:])

def t5_bucket(dist):
    n = jnp.maximum(dist, 0)
    nf = jnp.maximum(n, 1).astype(jnp.float32)
    large = MAX_EXACT + (jnp.log(nf / MAX_EXACT) / math.log(MAX_DISTANCE / MAX_EXACT)
                         * (N_BUCKETS - MAX_EXACT)).astype(jnp.int32)
    large = jnp.minimum(large, N_BUCKETS - 1)
    return jnp.where(n < MAX_EXACT, n, large)

def rg_lru(x, w_r, b_r, w_i, b_i, a_param):
    bsz, s, c = x.shape
    xb = x.reshape(bsz, s, RNN_BLOCKS, RNN_BLOCK_W)
    r = jax.nn.sigmoid(jnp.einsum('bsnc,ncd->bsnd', xb, w_r).reshape(bsz, s, c) + b_r)
    i = jax.nn.sigmoid(jnp.einsum('bsnc,ncd->bsnd', xb, w_i).reshape(bsz, s, c) + b_i)
    log_a = (-RG_LRU_C * r.astype(jnp.float32)) * jax.nn.softplus(-a_param.astype(jnp.float32))
    a = jnp.exp(log_a)
    u = jnp.sqrt(-jnp.expm1(2.0 * log_a)) * (i * x).astype(jnp.float32)

    def combine(left, right):
        a1, b1 = left
        a2, b2 = right
        return a1 * a2, a2 * b1 + b2

    _, h = lax.associative_scan(combine, (a, u), axis=1)
    return h.astype(x.dtype)

def diff_attention(q, k, v, lam, rel_table):
    s_len = q.shape[1]
    scale = DIFF_HEAD_DIM ** -0.5
    k_pos = jnp.arange(s_len)

    def one_block(args):
        qb, blk = args
        q_pos = blk * Q_BLOCK + jnp.arange(Q_BLOCK)
        dist = q_pos[:, None] - k_pos[None, :]
        bias = jnp.moveaxis(rel_table[t5_bucket(dist)], -1, 0)
        sc = jnp.einsum('bqhcd,bkhcd->bchqk', qb, k).astype(jnp.float32) * scale + bias.astype(jnp.float32)
        sc = jnp.where(dist >= 0, sc, -jnp.inf)
        p = jax.nn.softmax(sc, axis=-1)
        w = p[:, 0] - lam * p[:, 1]
        return jnp.einsum('bhqk,bkhd->bqhd', w.astype(v.dtype), v)

    out = lax.map(one_block, (_to_blocks(q), jnp.arange(s_len // Q_BLOCK)))
    return _from_blocks(out)

def forgetting_attention(q, k, v, log_f):
    s_len = q.shape[1]
    scale = FOX_HEAD_DIM ** -0.5
    k_pos = jnp.arange(s_len)
    c = jnp.cumsum(log_f.astype(jnp.float32), axis=1)
    ck = jnp.moveaxis(c, -1, 1)

    def one_block(args):
        qb, cq, blk = args
        q_pos = blk * Q_BLOCK + jnp.arange(Q_BLOCK)
        dist = q_pos[:, None] - k_pos[None, :]
        decay = jnp.moveaxis(cq, -1, 1)[..., None] - ck[:, :, None, :]
        sc = jnp.einsum('bqhd,bkhd->bhqk', qb, k).astype(jnp.float32) * scale + decay
        sc = jnp.where(dist >= 0, sc, -jnp.inf)
        p = jax.nn.softmax(sc, axis=-1)
        return jnp.einsum('bhqk,bkhd->bqhd', p.astype(v.dtype), v)

    out = lax.map(one_block, (_to_blocks(q), _to_blocks(c), jnp.arange(s_len // Q_BLOCK)))
    return _from_blocks(out)

def first_inputs(seed: int = 0) -> dict:
    key = jax.random.key(seed)
    ks = jax.random.split(key, 32)
    L = DEPTH

    def nrm(k, shape, scale):
        return jax.random.normal(k, shape, jnp.float32) * scale

    a_target = jax.random.uniform(ks[9], (L, D_RNN), jnp.float32, 0.9, 0.999)
    sig = a_target ** (1.0 / RG_LRU_C)
    return {
        "x": nrm(ks[0], (BATCH, SEQ, D_MODEL), 1.0),
        "norm1_g": 1.0 + nrm(ks[1], (L, D_MODEL), 0.02),
        "w_in": nrm(ks[2], (L, D_MODEL, N_IN), D_MODEL ** -0.5),
        "rnn_conv_w": nrm(ks[3], (L, CONV_RNN, D_RNN), CONV_RNN ** -0.5),
        "rnn_conv_b": nrm(ks[4], (L, D_RNN), 0.02),
        "rg_w_r": nrm(ks[5], (L, RNN_BLOCKS, RNN_BLOCK_W, RNN_BLOCK_W), RNN_BLOCK_W ** -0.5),
        "rg_b_r": nrm(ks[6], (L, D_RNN), 0.02),
        "rg_w_i": nrm(ks[7], (L, RNN_BLOCKS, RNN_BLOCK_W, RNN_BLOCK_W), RNN_BLOCK_W ** -0.5),
        "rg_b_i": nrm(ks[8], (L, D_RNN), 0.02),
        "rg_a": jnp.log(sig) - jnp.log1p(-sig),
        "diff_lq1": nrm(ks[10], (L, DIFF_HEAD_DIM), 0.1),
        "diff_lk1": nrm(ks[11], (L, DIFF_HEAD_DIM), 0.1),
        "diff_lq2": nrm(ks[12], (L, DIFF_HEAD_DIM), 0.1),
        "diff_lk2": nrm(ks[13], (L, DIFF_HEAD_DIM), 0.1),
        "diff_subln_g": 1.0 + nrm(ks[14], (L, 2 * DIFF_HEAD_DIM), 0.02),
        "rel_bias": nrm(ks[15], (N_BUCKETS, DIFF_HEADS), 0.5),
        "fox_b_f": 3.0 + nrm(ks[16], (L, FOX_HEADS), 0.5),
        "gate_b": nrm(ks[17], (L, N_BRANCH, D_MODEL), 0.02),
        "w_br_rnn": nrm(ks[18], (L, D_RNN, D_MODEL), D_RNN ** -0.5),
        "w_br_diff": nrm(ks[19], (L, DIFF_WIDTH, D_MODEL), DIFF_WIDTH ** -0.5),
        "w_br_fox": nrm(ks[20], (L, FOX_WIDTH, D_MODEL), FOX_WIDTH ** -0.5),
        "w_out": nrm(ks[21], (L, D_MODEL, D_MODEL), D_MODEL ** -0.5),
        "norm2_g": 1.0 + nrm(ks[22], (L, D_MODEL), 0.02),
        "ffn_up": nrm(ks[23], (L, D_MODEL, 2 * D_FF), D_MODEL ** -0.5),
        "ffn_conv_w": nrm(ks[24], (L, CONV_FFN, 2 * D_FF), CONV_FFN ** -0.5),
        "ffn_conv_b": nrm(ks[25], (L, 2 * D_FF), 0.02),
        "ffn_down": nrm(ks[26], (L, D_FF, D_MODEL), D_FF ** -0.5),
        "final_g": 1.0 + nrm(ks[27], (D_MODEL,), 0.02),
    }

def first_block(x, norm1_g, w_in, rnn_conv_w, rnn_conv_b, rg_w_r, rg_b_r, rg_w_i, rg_b_i, rg_a,
              diff_lq1, diff_lk1, diff_lq2, diff_lk2, diff_subln_g, rel_bias, fox_b_f, gate_b,
              w_br_rnn, w_br_diff, w_br_fox, w_out, norm2_g, ffn_up, ffn_conv_w, ffn_conv_b,
              ffn_down, final_g):
    bsz, s_len, _ = x.shape
    for l in range(DEPTH):
        h = rmsnorm(x, norm1_g[l])
        proj = h @ w_in[l]
        (x_rnn, g_rnn, dq, dk, dv, fq, fk, fv, f_logit, gates) = jnp.split(proj, IN_SPLITS, axis=-1)

        x_rnn = causal_dwconv(x_rnn, rnn_conv_w[l], rnn_conv_b[l])
        y_rnn = jax.nn.gelu(g_rnn) * rg_lru(x_rnn, rg_w_r[l], rg_b_r[l], rg_w_i[l], rg_b_i[l], rg_a[l])

        lam_init = 0.8 - 0.6 * math.exp(-0.3 * l)
        lam = (jnp.exp(jnp.sum(diff_lq1[l] * diff_lk1[l]).astype(jnp.float32))
               - jnp.exp(jnp.sum(diff_lq2[l] * diff_lk2[l]).astype(jnp.float32)) + lam_init)
        o_diff = diff_attention(dq.reshape(bsz, s_len, DIFF_HEADS, 2, DIFF_HEAD_DIM),
                                dk.reshape(bsz, s_len, DIFF_HEADS, 2, DIFF_HEAD_DIM),
                                dv.reshape(bsz, s_len, DIFF_HEADS, 2 * DIFF_HEAD_DIM), lam, rel_bias)
        y_diff = (rmsnorm(o_diff, diff_subln_g[l]) * (1.0 - lam_init)).reshape(bsz, s_len, DIFF_WIDTH)

        log_f = jax.nn.log_sigmoid((f_logit + fox_b_f[l]).astype(jnp.float32))
        o_fox = forgetting_attention(fq.reshape(bsz, s_len, FOX_HEADS, FOX_HEAD_DIM),
                                     fk.reshape(bsz, s_len, FOX_HEADS, FOX_HEAD_DIM),
                                     fv.reshape(bsz, s_len, FOX_HEADS, FOX_HEAD_DIM), log_f)
        y_fox = o_fox.reshape(bsz, s_len, FOX_WIDTH)

        g = jax.nn.sigmoid(gates.reshape(bsz, s_len, N_BRANCH, D_MODEL) + gate_b[l])
        m = (g[:, :, 0] * (y_rnn @ w_br_rnn[l])
             + g[:, :, 1] * (y_diff @ w_br_diff[l])
             + g[:, :, 2] * (y_fox @ w_br_fox[l]))
        x = x + m @ w_out[l]

        h = rmsnorm(x, norm2_g[l])
        u = causal_dwconv(h @ ffn_up[l], ffn_conv_w[l], ffn_conv_b[l])
        u_gate, u_val = jnp.split(u, 2, axis=-1)
        x = x + (jax.nn.gelu(u_gate) * u_val) @ ffn_down[l]
    return rmsnorm(x, final_g)


DEPTH_2 = 2

HEAD_DIM = 64
DIL_PATTERNS = ((128, 1), (512, 4), (2048, 16))
DIL_HEADS = 4
N_DIL_SUB = DIL_HEADS * len(DIL_PATTERNS)
DIL_QKV = N_DIL_SUB * HEAD_DIM
DIL_OUT = DIL_HEADS * HEAD_DIM
DIL_BLOCK = 64
WIN_HALF = 128
WIN_BLOCK = 128
WIN_Q = D_MODEL
WIN_Q_HEADS = WIN_Q // HEAD_DIM
WIN_KV_HEADS = 4
WIN_KV = WIN_KV_HEADS * HEAD_DIM
N_BRANCH_2 = 2
SPLITS = (DIL_QKV, 2 * DIL_QKV, 3 * DIL_QKV,
          3 * DIL_QKV + WIN_Q, 3 * DIL_QKV + WIN_Q + WIN_KV, 3 * DIL_QKV + WIN_Q + 2 * WIN_KV)
IN_COLS = 3 * DIL_QKV + WIN_Q + 2 * WIN_KV + N_BRANCH_2 * D_MODEL
N_EXPERTS = 16
CAPACITY_FACTOR = 2
D_EXPERT = 1024
RMS_EPS = 1e-6
NEG_INF = -1e30


def rmsnorm_2(x, g):
    xf = x.astype(jnp.float32)
    y = xf * lax.rsqrt(jnp.mean(xf * xf, axis=-1, keepdims=True) + RMS_EPS)
    return (y * g.astype(jnp.float32)).astype(x.dtype)

def alibi_slopes(n):
    return 2.0 ** (-8.0 * jnp.arange(1, n + 1, dtype=jnp.float32) / n)

def banded_attention(q, k, v, half, blk, slopes, pos_scale, sink=None):
    N, L, H, dh = q.shape
    Hk = k.shape[2]
    G = H // Hk
    nb = -(-L // blk)
    Lp = nb * blk
    pad = Lp - L
    qb = jnp.pad(q, ((0, 0), (0, pad), (0, 0), (0, 0))).reshape(N, nb, blk, Hk, G, dh)

    def key_blocks(t):
        tp = jnp.pad(t, ((0, 0), (blk, pad + blk), (0, 0), (0, 0)))
        return jnp.concatenate([
            tp[:, :Lp].reshape(N, nb, blk, Hk, dh),
            tp[:, blk:blk + Lp].reshape(N, nb, blk, Hk, dh),
            tp[:, 2 * blk:].reshape(N, nb, blk, Hk, dh)], axis=2)

    kb = key_blocks(k)
    vb = key_blocks(v)
    a = jnp.arange(blk)[:, None]
    b = jnp.arange(3 * blk)[None, :]
    rel = b - blk - a
    kpos = (jnp.arange(nb)[:, None, None] - 1) * blk + b[None]
    mask = (jnp.abs(rel) <= half)[None] & (kpos >= 0) & (kpos < L)
    bias = -slopes.astype(jnp.float32).reshape(Hk, G)[:, :, None, None] * \
        (pos_scale * jnp.abs(rel)).astype(jnp.float32)[None, None]
    s = jnp.einsum('nibkgd,nijkd->nikgbj', qb, kb).astype(jnp.float32) * (dh ** -0.5) + bias
    s = jnp.where(mask[None, :, None, None], s, NEG_INF)
    m = jnp.max(s, axis=-1)
    if sink is not None:
        sk = sink.astype(jnp.float32).reshape(Hk, G)[:, :, None]
        m = jnp.maximum(m, sk)
    p = jnp.exp(s - m[..., None])
    denom = jnp.sum(p, axis=-1)
    if sink is not None:
        denom = denom + jnp.exp(sk - m)
    p = p / denom[..., None]
    o = jnp.einsum('nikgbj,nijkd->nibkgd', p.astype(v.dtype), vb)
    o = o.reshape(N, Lp, H, dh)[:, :L]
    lse = jnp.moveaxis(m + jnp.log(denom), -1, 2).reshape(N, Lp, H)[:, :L]
    return o, lse

def dilated_mixture(q, k, v):
    B, S = q.shape[:2]
    slopes = alibi_slopes(N_DIL_SUB)
    outs, lses = [], []
    for g, (w, r) in enumerate(DIL_PATTERNS):
        sl = slice(g * DIL_HEADS, (g + 1) * DIL_HEADS)

        def strided(t):
            return t[:, :, sl].reshape(B, S // r, r, DIL_HEADS, HEAD_DIM).transpose(0, 2, 1, 3, 4) \
                .reshape(B * r, S // r, DIL_HEADS, HEAD_DIM)

        o, lse = banded_attention(strided(q), strided(k), strided(v), w // (2 * r), DIL_BLOCK,
                                  slopes[sl], r)
        outs.append(o.reshape(B, r, S // r, DIL_HEADS, HEAD_DIM).transpose(0, 2, 1, 3, 4)
                    .reshape(B, S, DIL_HEADS, HEAD_DIM))
        lses.append(lse.reshape(B, r, S // r, DIL_HEADS).transpose(0, 2, 1, 3).reshape(B, S, DIL_HEADS))
    wts = jax.nn.softmax(jnp.stack(lses, axis=0), axis=0)
    return jnp.sum(wts[..., None].astype(q.dtype) * jnp.stack(outs, axis=0), axis=0)

def hybrid_mixer(h, w_in, w_branch_a, w_branch_b, b_gate, sink_logit, w_out):
    B, S, D = h.shape
    proj = jnp.einsum('bsd,dc->bsc', h, w_in)
    qa, ka, va, qw, kw, vw, gates = jnp.split(proj, SPLITS, axis=-1)
    oa = dilated_mixture(qa.reshape(B, S, N_DIL_SUB, HEAD_DIM),
                         ka.reshape(B, S, N_DIL_SUB, HEAD_DIM),
                         va.reshape(B, S, N_DIL_SUB, HEAD_DIM))
    ya = jnp.einsum('bsc,cd->bsd', oa.reshape(B, S, DIL_OUT), w_branch_a)
    ob, _ = banded_attention(qw.reshape(B, S, WIN_Q_HEADS, HEAD_DIM),
                             kw.reshape(B, S, WIN_KV_HEADS, HEAD_DIM),
                             vw.reshape(B, S, WIN_KV_HEADS, HEAD_DIM),
                             WIN_HALF, WIN_BLOCK, alibi_slopes(WIN_Q_HEADS), 1, sink_logit)
    yb = jnp.einsum('bsc,cd->bsd', ob.reshape(B, S, WIN_Q), w_branch_b)
    g = jax.nn.sigmoid((gates + b_gate).astype(jnp.float32)).astype(h.dtype).reshape(B, S, N_BRANCH_2, D)
    merged = g[:, :, 0] * ya + g[:, :, 1] * yb
    return jnp.einsum('bsd,de->bse', merged, w_out)

def expert_choice_ffn(h, w_router, w_gate, w_up, w_down):
    B, S, D = h.shape
    cap = CAPACITY_FACTOR * S // N_EXPERTS
    aff = jax.nn.softmax(jnp.einsum('bsd,de->bse', h, w_router).astype(jnp.float32), axis=-1)
    gate, idx = lax.top_k(jnp.swapaxes(aff, 1, 2), cap)
    bidx = jnp.arange(B)[:, None, None]
    xe = h[bidx, idx]
    a = jnp.einsum('becd,edf->becf', xe, w_gate)
    u = jnp.einsum('becd,edf->becf', xe, w_up)
    ye = jnp.einsum('becf,efd->becd', jax.nn.silu(a) * u, w_down)
    return jnp.zeros_like(h).at[bidx, idx].add(gate[..., None].astype(h.dtype) * ye)

def second_inputs(seed: int = 0) -> dict:
    key = jax.random.key(seed)
    ks = jax.random.split(key, 14)
    f = jnp.float32
    return {
        "x": jax.random.normal(ks[0], (BATCH, SEQ, D_MODEL), f),
        "norm_mix": 1.0 + 0.02 * jax.random.normal(ks[1], (DEPTH_2, D_MODEL), f),
        "w_in": jax.random.normal(ks[2], (DEPTH_2, D_MODEL, IN_COLS), f) * D_MODEL ** -0.5,
        "w_branch_a": jax.random.normal(ks[3], (DEPTH_2, DIL_OUT, D_MODEL), f) * DIL_OUT ** -0.5,
        "w_branch_b": jax.random.normal(ks[4], (DEPTH_2, WIN_Q, D_MODEL), f) * WIN_Q ** -0.5,
        "b_gate": 0.1 * jax.random.normal(ks[5], (DEPTH_2, N_BRANCH_2 * D_MODEL), f),
        "sink_logit": 0.5 * jax.random.normal(ks[6], (DEPTH_2, WIN_Q_HEADS), f),
        "w_out": jax.random.normal(ks[7], (DEPTH_2, D_MODEL, D_MODEL), f) * D_MODEL ** -0.5,
        "norm_ffn": 1.0 + 0.02 * jax.random.normal(ks[8], (DEPTH_2, D_MODEL), f),
        "w_router": jax.random.normal(ks[9], (DEPTH_2, D_MODEL, N_EXPERTS), f) * D_MODEL ** -0.5,
        "w_expert_gate": jax.random.normal(ks[10], (DEPTH_2, N_EXPERTS, D_MODEL, D_EXPERT), f) * D_MODEL ** -0.5,
        "w_expert_up": jax.random.normal(ks[11], (DEPTH_2, N_EXPERTS, D_MODEL, D_EXPERT), f) * D_MODEL ** -0.5,
        "w_expert_down": jax.random.normal(ks[12], (DEPTH_2, N_EXPERTS, D_EXPERT, D_MODEL), f) * D_EXPERT ** -0.5,
        "norm_final": 1.0 + 0.02 * jax.random.normal(ks[13], (D_MODEL,), f),
    }

def second_block(x, norm_mix, w_in, w_branch_a, w_branch_b, b_gate, sink_logit, w_out,
              norm_ffn, w_router, w_expert_gate, w_expert_up, w_expert_down, norm_final):
    h = x
    for l in range(DEPTH_2):
        h = h + hybrid_mixer(rmsnorm_2(h, norm_mix[l]), w_in[l], w_branch_a[l], w_branch_b[l],
                             b_gate[l], sink_logit[l], w_out[l])
        h = h + expert_choice_ffn(rmsnorm_2(h, norm_ffn[l]), w_router[l], w_expert_gate[l],
                                  w_expert_up[l], w_expert_down[l])
    return rmsnorm_2(h, norm_final)


def setup_inputs(seed=0):
    out = dict(first_inputs(seed))
    for name, value in second_inputs(seed + 1).items():
        if name != "x":
            out[name + "_2"] = value
    return out


def reference(
    x, norm1_g, w_in, rnn_conv_w, rnn_conv_b, rg_w_r, rg_b_r, rg_w_i, rg_b_i, rg_a, diff_lq1,
    diff_lk1, diff_lq2, diff_lk2, diff_subln_g, rel_bias, fox_b_f, gate_b, w_br_rnn, w_br_diff,
    w_br_fox, w_out, norm2_g, ffn_up, ffn_conv_w, ffn_conv_b, ffn_down, final_g, norm_mix_2,
    w_in_2, w_branch_a_2, w_branch_b_2, b_gate_2, sink_logit_2, w_out_2, norm_ffn_2, w_router_2,
    w_expert_gate_2, w_expert_up_2, w_expert_down_2, norm_final_2,
):
    x = first_block(
        x, norm1_g, w_in, rnn_conv_w, rnn_conv_b, rg_w_r, rg_b_r, rg_w_i, rg_b_i, rg_a,
        diff_lq1, diff_lk1, diff_lq2, diff_lk2, diff_subln_g, rel_bias, fox_b_f, gate_b,
        w_br_rnn, w_br_diff, w_br_fox, w_out, norm2_g, ffn_up, ffn_conv_w, ffn_conv_b, ffn_down,
        final_g,
    )
    return second_block(
        x, norm_mix_2, w_in_2, w_branch_a_2, w_branch_b_2, b_gate_2, sink_logit_2, w_out_2,
        norm_ffn_2, w_router_2, w_expert_gate_2, w_expert_up_2, w_expert_down_2, norm_final_2,
    )


_drawn_inputs = setup_inputs


def setup_inputs(seed=0):
    import zlib

    import numpy as np

    out = dict(_drawn_inputs(seed))
    spreads = {}
    factors = {'rg_b_r': 8.0,
     'rg_b_i': 8.0,
     'diff_lq1': 6.818,
     'diff_subln_g': 3.142,
     'gate_b': 5.478,
     'norm_mix_2': 2.96,
     'b_gate_2': 2.991,
     'sink_logit_2': 22.264,
     'norm_final_2': 7.691}
    for name, (base, spread) in spreads.items():
        noise = np.random.default_rng([zlib.crc32(name.encode()), seed]).standard_normal(out[name].shape)
        drawn = base * np.exp(spread * noise) if base else spread * noise
        out[name] = __import__('jax').numpy.asarray(drawn.astype(out[name].dtype))
    for name, factor in factors.items():
        out[name] = (out[name] * factor).astype(out[name].dtype)
    return out
```

```python
import math
import numpy as np
import concourse.bass as bass
from concourse import mybir

F32 = mybir.dt.float32
ACT = mybir.ActivationFunctionType
ALU = mybir.AluOpType
AX = mybir.AxisListType.X

KS, CS = 4096, 256
BIG = -1.0e30
SLOPES_A = [float(np.float32(2.0) ** np.float32(-8.0 * i / 12)) for i in range(1, 13)]
SLOPES_W = [float(np.float32(2.0) ** np.float32(-8.0 * i / 16)) for i in range(1, 17)]



def slab_list():
    s = []

    def add(name, n, cols=KS, extra=False):
        for i in range(n):
            s.append((name, i, cols, extra))
    add("xrnn", 2)
    add("grnn", 2)
    add("dq", 1)
    add("dk", 1)
    add("rg", 1, 2048)
    add("dv", 1)
    add("fq", 1)
    add("fk", 1)
    add("fv", 1)
    add("gates", 6)
    add("brr", 2)
    add("brd", 1)
    add("brf", 1)
    add("wout", 2)
    add("up", 11)
    add("down", 5)
    add("down5", 1, 2048)
    for l in range(2):
        add(f"qka{l}", 3)
        add(f"va{l}", 1)
        add(f"vb{l}", 1, 2048)
        add(f"qw{l}", 2)
        add(f"kvw{l}", 1)
        add(f"bias{l}_", 2, 3840)
        add(f"bias{l}_2", 1, 3072)
        add(f"gate{l}", 4)
        add(f"bra{l}", 1, 2048)
        add(f"brb{l}", 2)
        add(f"wo{l}", 2)
        for e in range(16):
            add(f"eg{l}_{e}", 2, KS, True)
            add(f"eu{l}_{e}", 2, KS, True)
            add(f"ed{l}_{e}", 2, KS, True)
    return s


PV = {}
_at = 0
for _n, _w in [("g1", 8), ("cw", 32), ("cb", 8), ("br", 8), ("bi", 8), ("ra", 8), ("sub", 1), ("gb", 24),
               ("g2", 8), ("fw", 132), ("fb", 44), ("gm0", 8), ("gm1", 8), ("bg0", 16), ("bg1", 16),
               ("gf0", 8), ("gf1", 8)]:
    PV[_n] = (_at, _w)
    _at += _w
NPV = _at


class Queue:

    def __init__(self, eng, sem):
        self.eng, self.sem, self.n, self.items, self.seen = eng, sem, 0, [], {}

    def wait(self, *toks):
        for sem, v in toks:
            if self.seen.get(sem.name, 0) < v:
                self.seen[sem.name] = v
                self.items.append((self.eng.wait_ge, (sem, v), {}, None, 0))

    def __call__(self, after, fn, *a, **k):
        self.wait(*after)
        self.n += 1
        self.items.append((fn, a, k, self.sem, 1))
        return (self.sem, self.n)

    def quiet(self, after, fn, *a, **k):
        self.wait(*after)
        self.items.append((fn, a, k, None, 0))

    def dma(self, after, sem, out, in_):
        self.wait(*after)
        self.items.append((self.eng.dma_start, (out, in_), {}, sem, 16))

    def play(self):
        for fn, a, k, sem, by in self.items:
            i = fn(*a, **k)
            if sem is not None:
                i.then_inc(sem, by)


class Slot:
    def __init__(self, ap, sem, extra):
        self.ap, self.sem, self.extra, self.count, self.free = ap, sem, extra, 0, ()


class Stream:

    def __init__(self, sp, slabs, dram):
        self.sp, self.slabs, self.dram, self.next = sp, slabs, dram, 0
        self.ready, self.idle = {}, []

    def open(self, slot, free=()):
        slot.free = free
        self.idle.append(slot)
        self.fill()

    def fill(self):
        while self.next < len(self.slabs):
            name, i, cols, extra = self.slabs[self.next]
            pick = [s for s in self.idle if extra or not s.extra]
            if not pick:
                return
            s = pick[0]
            self.idle.remove(s)
            s.count += 16
            self.sp.dma(s.free, s.sem, s.ap[:, 0:cols], self.dram[self.next, :, 0:cols])
            self.ready[(name, i)] = (s, (s.sem, s.count))
            self.next += 1

    def get(self, name, i=0):
        return self.ready[(name, i)]

    def done(self, slot, *toks):
        self.open(slot, toks)

    def take_extras(self):
        out = [s for s in self.idle if s.extra]
        self.idle = [s for s in self.idle if not s.extra]
        return [t for s in out for t in s.free], out


def build(nc, I, out):
    slabs = slab_list()
    from contextlib import ExitStack
    ctx = ExitStack()
    with ctx:
        def sb(name, shape):
            return ctx.enter_context(nc.sbuf_tensor(name, shape, F32))

        def sem(name):
            return ctx.enter_context(nc.semaphore(name))

        P = Queue(nc.tensor, sem("s_pe"))
        V = Queue(nc.vector, sem("s_dve"))
        A = Queue(nc.scalar, sem("s_act"))
        G = Queue(nc.gpsimd, sem("s_pool"))
        S = Queue(nc.sync, sem("s_sp"))
        v, a, g, pe = nc.vector, nc.scalar, nc.gpsimd, nc.tensor

        NPAGE = 126
        arena = sb("arena", [128, NPAGE * 256])
        base = [sb(f"slot{i}", [128, KS]) for i in range(4)]
        ident = sb("ident", [128, 128])
        pv = sb("pv", [128, NPV])
        sm = sb("sm", [128, 640])
        cmask = sb("cmask", [128, 384])
        bk = [ctx.enter_context(nc.psum_tensor(f"bank{i}", [128, 512], F32)) for i in range(8)]
        bfree = [()] * 8
        scr = nc.dram_tensor("scratch", [4, 128 * 512], F32, kind="Internal").ap()

        def pg(at, n, cols=256):
            return arena[:, at * 256:at * 256 + n * cols].rearrange("p (n c) -> p n c", n=n)

        def par(name, i=0, n=1):
            return pv[:, PV[name][0] + i:PV[name][0] + i + n]

        s_x, s_c, s_id, s_m = sem("s_x"), sem("s_c"), sem("s_id"), sem("s_m")
        stream = Stream(S, slabs, I["slabs"])

        X = pg(0, 2, 1024)
        HT = pg(8, 8)
        S.dma((), s_x, X, I["x"].rearrange("(b p) d -> p b d", p=128))
        t_x = (s_x, 16)
        S.dma((), s_id, ident[:, :], I["ident"])
        S.dma((), s_id, pv[:, :], I["pv"])
        t_c = (s_id, 32)
        for i in range(4):
            stream.open(Slot(base[i][:, :], sem(f"s_w{i}"), False))
        A.dma((), s_m, cmask[:, :], I["cmask"])

        c_ss, c_rs = sm[:, 0:8], sm[:, 8:16]
        c_sp4, c_t1, c_t2, c_t3 = sm[:, 16:24], sm[:, 24:32], sm[:, 32:40], sm[:, 40:48]
        c_lam, c_sub = sm[:, 48:52], sm[:, 52:53]
        c_hb = sm[:, 56:96]
        c_hg = sm[:, 96:128]
        c_mx, c_nm, c_dn, c_rc = sm[:, 128:140], sm[:, 140:152], sm[:, 152:164], sm[:, 164:176]
        c_lq = sm[:, 192:448]
        c_sink = sm[:, 448:480]
        c_fb = sm[:, 480:481]
        c_rel = sm[:, 484:488]
        c_es = sm[:, 488:500]
        c_tmp = sm[:, 512:640]

        A.dma((), s_c, c_lq, I["lq"].rearrange("(a n) -> a n", a=1).to_broadcast([128, 256]))
        A.dma((), s_c, c_sink, I["sink"].rearrange("(a n) -> a n", a=1).to_broadcast([128, 32]))
        A.dma((), s_c, c_fb[0:8, :], I["fb"].rearrange("(n a) -> n a", a=1))
        A.dma((), s_c, c_rel[0:32, :], I["rel"])
        t_s = (s_c, 64)

        def evac_T(bank, pair, dst, gname, tok, eng):
            r = []
            for h in range(2):
                src = bk[bank][:, h * 256:(h + 1) * 256]
                if eng is A:
                    r.append(A((tok, t_c), a.activation, dst[:, 2 * pair + h, :], src, ACT.Copy,
                               scale=par(gname, 2 * pair + h)))
                else:
                    r.append(V((tok, t_c), v.tensor_scalar, dst[:, 2 * pair + h, :], src,
                               par(gname, 2 * pair + h), None, ALU.mult))
            return r[-1]

        def rstd(t_in, src, junk, free=()):
            for b in range(2):
                t = A((t_in, *free), a.activation, junk[:, b, :], src[:, b, :], ACT.Square,
                      accum_out=c_ss[:, b:b + 1])
            t = V((t,), v.tensor_scalar, c_rs[:, 0:2], c_ss[:, 0:2], 1.0 / 1024, 1e-6, ALU.mult, ALU.add)
            t = A((t,), a.activation, c_rs[:, 2:4], c_rs[:, 0:2], ACT.Sqrt)
            return V((t,), v.reciprocal, c_rs[:, 4:6], c_rs[:, 2:4])

        def norm_T(t_in, gname, XN, HT, free=()):
            t = rstd(t_in, X, XN, free)
            for b in range(2):
                tn = V((t,), v.tensor_scalar, XN[:, b, :], X[:, b, :], c_rs[:, 4 + b:5 + b], None, ALU.mult)
            th = []
            for pr in range(4):
                b = pr
                for h in range(2):
                    for tb in range(2):
                        c = 2 * pr + h
                        tt = P((tn, t_c, *bfree[b]), pe.transpose,
                               bk[b][:, h * 256 + tb * 128:h * 256 + tb * 128 + 128],
                               XN[:, tb, c * 128:(c + 1) * 128], ident[:, :])
                te = evac_T(b, pr, HT, gname, tt, A if pr % 2 else V)
                bfree[b] = (te,)
                th.append(te)
            return tn, th

        def dense(b, off, w, k0, nk, col, rhs, first=None, last=None, after=()):
            for k in range(nk):
                f = P.quiet if k < nk - 1 else P
                t = f(after, pe.matmul, bk[b][:, off:off + 256], w[:, k, col:col + 128], rhs[:, k0 + k, :],
                      start=(k == 0 if first is None else first and k == 0),
                      stop=(k == nk - 1 if last is None else last and k == nk - 1))
            return t

        rot = [0]

        def nextbank(lo, hi):
            rot[0] += 1
            return lo + rot[0] % (hi - lo)

        def pair_T(name, i, prs, rhs, tin, sink, banks, nk=8, release=True):
            s, td = stream.get(name, i)
            w = s.ap.rearrange("p (k n) -> p k n", k=nk)
            for pr in prs:
                b = nextbank(*banks)
                dense(b, 0, w, 0, nk, pr * 256, rhs, after=(td, *tin, *bfree[b]))
                t = dense(b, 256, w, 0, nk, pr * 256 + 128, rhs)
                bfree[b] = sink(pr, b, t)
            if release:
                stream.done(s, t)

        def two(ap):
            return ap.rearrange("p (n c) -> p n c", n=2)

        XN1 = pg(100, 2, 1024)
        _, tHT = norm_T(t_x, "g1", XN1, HT)

        tsl = V((t_s, t_c), v.tensor_scalar, c_hb[:, 0:16], par("br", 0, 16), 0.5, None, ALU.mult)
        V((), v.tensor_scalar, c_hb[:, 16:40], par("gb", 0, 24), 0.5, None, ALU.mult)
        V((), v.tensor_scalar, c_hg, par("bg0", 0, 32), 0.5, None, ALU.mult)
        t_hb = V((), v.tensor_scalar, c_sub, par("sub"), 0.8, None, ALU.mult)
        t = V((t_c,), v.scalar_tensor_tensor, c_t1, par("ra", 0, 8), -1.0, par("ra", 0, 8), ALU.mult, ALU.min)
        t = A((t,), a.activation, c_t1, c_t1, ACT.Exp)
        t = V((t,), v.tensor_scalar, c_t2, c_t1, 2.0, None, ALU.add)
        t = V((t,), v.reciprocal, c_t2, c_t2)
        t = V((t,), v.tensor_tensor, c_t1, c_t1, c_t2, ALU.mult)
        t = V((t,), v.tensor_tensor, c_t2, c_t1, c_t1, ALU.mult)
        t = V((t,), v.tensor_scalar, c_t3, c_t2, 1.0 / 17, 1.0 / 15, ALU.mult, ALU.add)
        for d in (13, 11, 9, 7, 5, 3, 1):
            t = V((t,), v.tensor_tensor, c_t3, c_t3, c_t2, ALU.mult)
            t = V((t,), v.tensor_scalar, c_t3, c_t3, 1.0 / d, None, ALU.add)
        t = V((t,), v.tensor_tensor, c_t3, c_t3, c_t1, ALU.mult)
        t = V((t,), v.tensor_scalar, c_t3, c_t3, 8.0, None, ALU.mult)
        t2 = V((t,), v.tensor_scalar, c_t1, par("ra", 0, 8), -4.0, 0.0, ALU.mult, ALU.max)
        t_sp = V((t2,), v.tensor_tensor, c_sp4, c_t3, c_t1, ALU.add)
        for i in range(2):
            t = V((t_s,), v.tensor_tensor, c_tmp[:, i * 64:(i + 1) * 64], c_lq[:, i * 128:i * 128 + 64],
                  c_lq[:, i * 128 + 64:i * 128 + 128], ALU.mult)
        t = V((t,), v.reduce_sum, c_lam[:, 0:2], two(c_tmp), axis=AX)
        t = A((t,), a.activation, c_lam[:, 0:2], c_lam[:, 0:2], ACT.Exp)
        t = V((t,), v.tensor_tensor, c_lam[:, 2:3], c_lam[:, 1:2], c_lam[:, 0:1], ALU.subtract)
        t_lam = V((t,), v.tensor_scalar, c_lam[:, 3:4], c_lam[:, 2:3], -0.2, None, ALU.add)

        XC, GR, TR, TI, AA = pg(16, 8), pg(24, 8), pg(32, 8), pg(40, 8), pg(48, 8)
        QD = pg(56, 8).rearrange("p (h c) n -> p h c n", c=2)
        KD, VD = pg(64, 4), pg(68, 2, 512)
        QF = pg(72, 8).rearrange("p (h c) n -> p h c n", c=2)
        KF, VF = pg(80, 4), pg(84, 2, 512)
        GT = pg(88, 24)
        BT = pg(112, 4, 384)
        O = pg(16, 2, 512)
        YD, YF = pg(20, 4), pg(32, 4)
        SD = [pg(118, 1, 768)[:, 0, :], pg(121, 1, 768)[:, 0, :]]
        PTB = [pg(124, 1, 384)[:, 0, :], pg(36, 1, 384)[:, 0, :]]
        LH, RH = pg(40, 8), pg(48, 8)
        OH = pg(118, 2)
        REL = pg(120, 2, 512)
        WF = pg(124, 1)[:, 0, 0:64].rearrange("p (k n) -> p k n", k=8)
        LF = pg(125, 1)

        tz = G((), g.memset, QD, 0.0)
        tz = G((), g.memset, QF, 0.0)

        s_oh, s_wf, s_b = sem("s_oh"), sem("s_wf"), sem("s_b")
        s_r = [sem(f"s_r{h}") for h in range(4)]
        t_r = tuple((q, 16) for q in s_r)
        A.dma((), s_oh, OH.rearrange("p n c -> p (n c)")[0:32, :], I["onehot"])
        A.dma((), s_wf, WF, I["wf"].rearrange("(k p) n -> p k n", p=128))
        for h in range(4):
            b = 4 + h % 2
            t = P((t_s, (s_oh, 16), *bfree[b]), pe.matmul, bk[b][:, :], c_rel[0:32, h:h + 1].to_broadcast([32, 128]),
                  OH.rearrange("p n c -> p (n c)")[0:32, :], start=True, stop=True)
            t = A((t, *(t_r[h - 2:h - 1] if h >= 2 else ())), a.activation, REL[:, h % 2, :], bk[b][:, :], ACT.Copy)
            bfree[b] = (t,)
            A.dma((t,), s_r[h], scr[h].rearrange("(p n) -> p n", p=128), REL[:, h % 2, :])
        skew = bass.AP(scr.tensor, 127, [[511, 128], [65536, 4], [1, 384]])
        A.dma(t_r, s_b, BT, skew)
        for h in range(4):
            t_bt = V(((s_b, 16), (s_m, 16)), v.scalar_tensor_tensor, BT[:, h, :], BT[:, h, :], 8.0, cmask[:, :],
                     ALU.mult, ALU.add)

        tC = [None] * 8

        def conv_rnn(i):
            def f(pr, b, t):
                for h in range(2):
                    n = 4 * i + 2 * pr + h
                    ps = bk[b][:, h * 256:(h + 1) * 256]
                    o = XC[:, n, :]
                    r = V((t, t_c), v.tensor_scalar, o, ps, par("cw", 24 + n), par("cb", n), ALU.mult, ALU.add)
                    for d in range(1, 4):
                        r = V((r,), v.scalar_tensor_tensor, o[:, d:256], ps[:, 0:256 - d],
                              par("cw", (3 - d) * 8 + n), o[:, d:256], ALU.mult, ALU.add)
                    tC[n] = r
                return (r,)
            return f
        for i in range(2):
            pair_T("xrnn", i, range(2), HT, tHT, conv_rnn(i), (0, 4))

        def gelu_g(i):
            def f(pr, b, t):
                n = 4 * i + 2 * pr
                r = A((t,), a.activation, GR[:, n:n + 2, :], two(bk[b][:, :]), ACT.Gelu_apprx_tanh)
                return (r,)
            return f
        for i in range(2):
            pair_T("grnn", i, range(2), HT, (), gelu_g(i), (0, 4))
        t_gr = (A.sem, A.n)

        def halves(dst, at=0, free=()):
            def f(pr, b, t):
                src = two(bk[b][:, :])
                for h in range(2):
                    p0 = 64 * h
                    r = A((t, tz, *free), a.activation, dst[p0:p0 + 64, at + 2 * pr:at + 2 * pr + 2, h, :],
                          src[p0:p0 + 64, :, :], ACT.Copy)
                return (r,)
            return f

        def plain(dst, at=0, eng=None, free=()):
            def f(pr, b, t):
                d, s_ = dst[:, at + 2 * pr:at + 2 * pr + 2, :], two(bk[b][:, :])
                if eng is V:
                    return (V((t, *free), v.tensor_copy, d, s_),)
                return (A((t, *free), a.activation, d, s_, ACT.Copy),)
            return f

        def tokmajor(name, i, dst, c0, nc_, wcols, kcols, banks, tin=(), release=True, off=0, free=()):
            s, td = stream.get(name, i)
            w = s.ap[:, 0:8 * kcols].rearrange("p (k n) -> p k n", k=8)
            for tb in range(2):
                b = nextbank(*banks)
                for k in range(8):
                    f = P.quiet if k < 7 else P
                    t = f((td, *tin, *bfree[b]), pe.matmul, bk[b][:, 0:nc_], HT[:, k, tb * 128:(tb + 1) * 128],
                          w[:, k, off:off + nc_], start=(k == 0), stop=(k == 7))
                r = A((t, *free), a.activation, dst[:, tb, c0:c0 + nc_], bk[b][:, 0:nc_], ACT.Copy)
                bfree[b] = (r,)
            if release:
                stream.done(s, t)
            return r

        pair_T("dq", 0, range(2), HT, (), halves(QD), (0, 4))
        pair_T("dk", 0, range(2), HT, (), plain(KD), (0, 4))
        s_, td = stream.get("rg")
        w = s_.ap[:, 0:2048].rearrange("p (k n) -> p k n", k=16)
        for n in range(8):
            b = nextbank(0, 4)
            for q in range(2):
                t = P((td, tC[n], *bfree[b]), pe.matmul, bk[b][:, q * 256:(q + 1) * 256], w[:, q * 8 + n, :],
                      XC[:, n, :], start=True, stop=True)
            A((t, t_hb), a.activation, TR[:, n, :], bk[b][:, 0:256], ACT.Tanh, bias=c_hb[:, n:n + 1], scale=0.5)
            r = A((), a.activation, TI[:, n, :], bk[b][:, 256:512], ACT.Tanh, bias=c_hb[:, 8 + n:9 + n], scale=0.5)
            bfree[b] = (r,)
            ty = V((r, t_sp), v.tensor_scalar, TR[:, n, :], TR[:, n, :], 1.0, c_sp4[:, n:n + 1], ALU.add, ALU.mult)
        stream.done(s_, t)
        ta = A((ty,), a.activation, AA, TR, ACT.Exp, scale=-1.0)
        tt = A((ta,), a.activation, TR, TR, ACT.Tanh)
        ti = V((r,), v.scalar_tensor_tensor, TI.rearrange("p n c -> p (n c)"), TI.rearrange("p n c -> p (n c)"), 1.0,
               XC.rearrange("p n c -> p (n c)"), ALU.add, ALU.mult)
        t = V((tt, ti), v.tensor_scalar, XC, TR, 1.0, None, ALU.add)
        t = V((t,), v.reciprocal, XC, XC)
        t = V((t,), v.tensor_tensor, TR, TR, XC, ALU.mult)
        t = A((t,), a.activation, TR, TR, ACT.Sqrt, scale=0.5)
        t = V((t,), v.tensor_tensor, TI, TI, TR, ALU.mult)
        for n in range(8):
            ts = V((t,), v.tensor_tensor_scan, XC[:, n, :], AA[:, n, :], TI[:, n, :], 0.0, ALU.mult, ALU.add)
        t_yr = V((ts, t_gr), v.tensor_tensor, GR, GR, XC, ALU.mult)

        t_vd = tokmajor("dv", 0, VD, 0, 512, 512, 512, (0, 4))
        pair_T("fq", 0, range(2), HT, (), halves(QF), (0, 4))
        pair_T("fk", 0, range(2), HT, (), plain(KF), (0, 4))
        t_vf = tokmajor("fv", 0, VF, 0, 512, 512, 512, (0, 4))

        b = nextbank(0, 4)
        for k in range(8):
            f = P.quiet if k < 7 else P
            t = f(((s_wf, 16), *bfree[b]), pe.matmul, bk[b][0:8, 0:256], WF[:, k, :], HT[:, k, :],
                  start=(k == 0), stop=(k == 7))
        Z, Z2 = XC[0:8, 4, :], XC[0:8, 5, :]
        lf = XC[0:8, 6, :]
        on = XC[0:8, 7, :]
        t = V((t, t_yr), v.tensor_scalar, Z, bk[b][0:8, 0:256], c_fb[0:8, :], None, ALU.add)
        bfree[b] = (t,)
        t = V((t,), v.scalar_tensor_tensor, Z2, Z, -1.0, Z, ALU.mult, ALU.min)
        t = A((t,), a.activation, Z2, Z2, ACT.Exp)
        t = A((t,), a.activation, Z2, Z2, ACT.Ln, bias=1.0)
        t = V((t,), v.tensor_scalar, Z, Z, 0.0, None, ALU.min)
        t = V((t,), v.tensor_tensor, Z, Z, Z2, ALU.subtract)
        V((), v.memset, on, 1.0)
        t = (V.sem, V.n)
        t = V((t,), v.tensor_tensor_scan, lf, on, Z, 0.0, ALU.mult, ALU.add)
        s_l = sem("s_l")
        tl = G((t_yr,), g.memset, LH, 0.0)
        tl = G((t_yr,), g.memset, RH, 0.0)
        A.dma((tl,), s_l, LH[0:8, :, :], I["sel"])
        A.dma((tl,), s_l, RH[32:40, :, :], I["sel"])
        V((t, tl), v.tensor_scalar, RH[0:8, :, :], lf.rearrange("p (a c) -> p a c", a=1).to_broadcast([8, 8, 256]),
          -8.0, None, ALU.mult)
        t_l = V((t, tl), v.tensor_scalar, LH[32:40, :, :],
                lf.rearrange("p (a c) -> p a c", a=1).to_broadcast([8, 8, 256]), 8.0, None, ALU.mult)

        def gate_fill(name, nsl, dst, hb, bank, free=()):
            for i in range(nsl):
                s, td = stream.get(name, i)
                w = s.ap.rearrange("p (k n) -> p k n", k=8)
                for pr in range(2):
                    dense(bank, 0, w, 0, 8, pr * 256, HT, after=(td, *bfree[bank]))
                    t = dense(bank, 256, w, 0, 8, pr * 256 + 128, HT)
                    for h in range(2):
                        n = 4 * i + 2 * pr + h
                        r = A((t, *free), a.activation, dst[:, n, :], bk[bank][:, h * 256:(h + 1) * 256], ACT.Tanh,
                              bias=hb[:, n:n + 1], scale=0.5)
                    bfree[bank] = (r,)
                    if pr == 1:
                        stream.done(s, t)
                    yield

        def run_pipeline(units, filler, per=1):
            lag = (0, 1, 1, 2)
            for step in range(len(units) + 2):
                for j in (0, 1, 2, 3):
                    i = step - lag[j]
                    if 0 <= i < len(units) and units[i][j] is not None:
                        units[i][j]()
                    if j == 0:
                        for _ in range(per):
                            next(filler, None)
            for _ in filler:
                pass

        sfree = [(), (), ()]
        ptfree = [(), ()]
        avst = {}

        def scores_row(ps, bias, S_, st, tok, free):
            return V((tok, *free), v.tensor_tensor_reduce, out=S_, in0=ps, in1=bias, scale=0.125, scalar=-3.0e38,
                     op0=ALU.add, op1=ALU.max, accum_out=c_mx[:, st:st + 1])

        units = []
        for h in range(4):
            i = h

            def s0(h=h, i=i):
                b0 = 0 if i % 2 == 0 else 2
                pa, pb_ = bk[b0], bk[b0 + 1]
                for c in range(2):
                    t0 = P((tz, t_hb, (A.sem, A.n), *bfree[b0], *bfree[b0 + 1]), pe.matmul, pa[:, c * 128:(c + 1) * 128],
                           QD[:, h, c, 0:128], KD[:, h, 0:128], start=True, stop=True)
                for c in range(2):
                    t0 = P((), pe.matmul, pb_[:, c * 256:(c + 1) * 256],
                           QD[:, h, c, 128:256], KD[:, h, :], start=True, stop=True)
                Sx = SD[i % 2]
                st = 4 * (i % 3)
                fr = sfree[i % 2]
                r = []
                r.append(scores_row(pa[:, 0:128], BT[:, h, 128:256], Sx[:, 0:128], st, t0, (*fr, t_bt)))
                r.append(scores_row(pa[:, 128:256], BT[:, h, 128:256], Sx[:, 128:256], st + 1, t0, ()))
                r.append(scores_row(pb_[:, 0:256], BT[:, h, 0:256], Sx[:, 256:512], st + 2, t0, ()))
                r.append(scores_row(pb_[:, 256:512], BT[:, h, 0:256], Sx[:, 512:768], st + 3, t0, ()))
                bfree[b0] = bfree[b0 + 1] = (r[-1],)
                tn = V((r[-1],), v.tensor_scalar, c_nm[:, st:st + 4], c_mx[:, st:st + 4], -1.0, None, ALU.mult)
                for q, (lo, hi) in enumerate(((0, 128), (128, 256), (256, 512), (512, 768))):
                    te = A((tn,), a.activation, Sx[:, lo:hi], Sx[:, lo:hi], ACT.Exp, bias=c_nm[:, st + q:st + q + 1],
                           accum_out=c_dn[:, st + q:st + q + 1])
                avst[("e", i)] = te

            def s1(h=h, i=i):
                Sx = SD[i % 2]
                st = 4 * (i % 3)
                t = V((avst[("e", i)],), v.reciprocal, c_rc[:, st:st + 4], c_dn[:, st:st + 4])
                for c in (1, 3):
                    tm = V((t, t_lam), v.tensor_scalar, c_rc[:, st + c:st + c + 1], c_rc[:, st + c:st + c + 1],
                           c_lam[:, 3:4], None, ALU.mult)
                for q, (lo, mid, hi) in enumerate(((0, 128, 256), (256, 512, 768))):
                    t = V((tm,), v.tensor_scalar, Sx[:, lo:mid], Sx[:, lo:mid], c_rc[:, st + 2 * q:st + 2 * q + 1], None,
                          ALU.mult)
                    t = V((t,), v.scalar_tensor_tensor, Sx[:, lo:mid], Sx[:, mid:hi],
                          c_rc[:, st + 2 * q + 1:st + 2 * q + 2], Sx[:, lo:mid], ALU.mult, ALU.add)
                avst[("p", i)] = t

            def s2(h=h, i=i):
                Sx, b, pt = SD[i % 2], 4 + i % 2, PTB[i % 2]
                for n, lo in enumerate((0, 256, 384)):
                    t = P((avst[("p", i)], *bfree[b]), pe.transpose, bk[b][:, n * 128:(n + 1) * 128], Sx[:, lo:lo + 128],
                          ident[:, :])
                sfree[i % 2] = (t,)
                t = V((t, t_yr, (s_wf, 16), *ptfree[i % 2]), v.tensor_copy, pt[:, 0:384], bk[b][:, 0:384])
                bfree[b] = (t,)
                avst[("t", i)] = t

            def s3(h=h, i=i):
                pt = PTB[i % 2]
                t = P((avst[("t", i)], t_vd, *bfree[6]), pe.matmul, bk[6][:, 0:128], pt[:, 0:128],
                      VD[:, 0, h * 128:(h + 1) * 128], start=True, stop=True)
                P((), pe.matmul, bk[6][:, 128:256], pt[:, 128:256], VD[:, 0, h * 128:(h + 1) * 128], start=True, stop=False)
                t = P((), pe.matmul, bk[6][:, 128:256], pt[:, 256:384], VD[:, 1, h * 128:(h + 1) * 128], start=False,
                      stop=True)
                ptfree[i % 2] = (t,)
                t = A((t, t_yr), a.activation, O[:, :, h * 128:(h + 1) * 128], two(bk[6][:, 0:256]), ACT.Copy)
                bfree[6] = (t,)
                avst[("o", h)] = t
            units.append([s0, s1, s2, s3])
        for h in range(8):
            i = 4 + h

            def s0(h=h, i=i):
                b0 = i % 4
                c, hf = h // 2, h % 2
                w_ = (t_l, (s_l, 32), *bfree[b0])
                for lo, n, q0 in ((0, 128, 0), (128, 256, 128)):
                    P.quiet(w_, pe.matmul, bk[b0][:, lo:lo + n], QF[:, c, hf, q0:q0 + 128], KF[:, c, 0:n], start=True,
                            stop=False)
                    t0 = P((), pe.matmul, bk[b0][:, lo:lo + n], LH[:, h, q0:q0 + 128], RH[:, h, 0:n], start=False, stop=True)
                Sx, st = SD[i % 2], 4 * (i % 3)
                scores_row(bk[b0][:, 0:128], cmask[:, 128:256], Sx[:, 0:128], st, t0, sfree[i % 2])
                r = scores_row(bk[b0][:, 128:384], cmask[:, 0:256], Sx[:, 128:384], st + 1, t0, ())
                bfree[b0] = (r,)
                tn = V((r,), v.tensor_scalar, c_nm[:, st:st + 2], c_mx[:, st:st + 2], -1.0, None, ALU.mult)
                for q, (lo, hi) in enumerate(((0, 128), (128, 384))):
                    te = A((tn,), a.activation, Sx[:, lo:hi], Sx[:, lo:hi], ACT.Exp, bias=c_nm[:, st + q:st + q + 1],
                           accum_out=c_dn[:, st + q:st + q + 1])
                avst[("e", i)] = te

            def s1(h=h, i=i):
                Sx, st = SD[i % 2], 4 * (i % 3)
                t = V((avst[("e", i)],), v.reciprocal, c_rc[:, st:st + 2], c_dn[:, st:st + 2])
                for q, (lo, hi) in enumerate(((0, 128), (128, 384))):
                    tp = V((t,), v.tensor_scalar, Sx[:, lo:hi], Sx[:, lo:hi], c_rc[:, st + q:st + q + 1], None, ALU.mult)
                avst[("p", i)] = tp

            def s2(h=h, i=i):
                Sx, b, pt = SD[i % 2], 4 + i % 2, PTB[i % 2]
                for n in range(3):
                    t = P((avst[("p", i)], *bfree[b]), pe.transpose, bk[b][:, n * 128:(n + 1) * 128],
                          Sx[:, n * 128:(n + 1) * 128], ident[:, :])
                sfree[i % 2] = (t,)
                t = V((t, *ptfree[i % 2]), v.tensor_copy, pt[:, 0:384], bk[b][:, 0:384])
                bfree[b] = (t,)
                avst[("t", i)] = t

            def s3(h=h, i=i):
                pt, p0 = PTB[i % 2], 64 * (h % 2)
                w_ = bfree[6] if h % 2 == 0 else ()
                o = bk[6][p0:p0 + 64, :]
                P.quiet((avst[("t", i)], t_vf, *w_), pe.matmul, o[:, 0:256], VF[:, 0, h * 64:(h + 1) * 64], pt[:, 0:256],
                        start=True, stop=False)
                t = P((), pe.matmul, o[:, 128:256], VF[:, 1, h * 64:(h + 1) * 64], pt[:, 256:384], start=False, stop=True)
                ptfree[i % 2] = (t,)
                if h % 2:
                    t = A((t, t_yr), a.activation, YF[:, h // 2, :], bk[6][:, 0:256], ACT.Copy)
                    bfree[6] = (t,)
                    avst["yf"] = t
            units.append([s0, s1, s2, s3])
        run_pipeline(units, gate_fill("gates", 6, GT, c_hb[:, 16:40], 7, free=(t_hb,)))
        t_gt = (A.sem, A.n)

        O8 = O.rearrange("p b (h d) -> p (b h) d", d=128)
        SQ = pg(40, 8, 128)
        t = V((avst[("o", 3)], (P.sem, P.n)), v.tensor_tensor, SQ, O8, O8, ALU.mult)
        t = V((t,), v.reduce_sum, c_ss, SQ, axis=AX)
        t = V((t,), v.tensor_scalar, c_ss, c_ss, 1.0 / 128, 1e-6, ALU.mult, ALU.add)
        t = A((t,), a.activation, c_ss, c_ss, ACT.Sqrt)
        t = V((t,), v.reciprocal, c_rs, c_ss)
        t = V((t,), v.tensor_tensor, O8, O8, c_rs.rearrange("p (n a) -> p n a", a=1).to_broadcast([128, 8, 128]), ALU.mult)
        for pr in range(2):
            for h in range(2):
                for tb in range(2):
                    tt = P((t, *bfree[pr]), pe.transpose, bk[pr][:, h * 256 + tb * 128:h * 256 + tb * 128 + 128],
                           O[:, tb, (2 * pr + h) * 128:(2 * pr + h + 1) * 128], ident[:, :])
            t_yd = V((tt,), v.tensor_scalar, YD[:, 2 * pr:2 * pr + 2, :], two(bk[pr][:, :]), c_sub, None, ALU.mult)
            bfree[pr] = (t_yd,)

        def merge(M, TMP, GTs, branches, mfree):
            tm = {}
            cnt = [0]
            for bi, (pieces, rhs, toks) in enumerate(branches):
                for (name, i, nk, n0, k0) in pieces:
                    def sink(pr, b, t, bi=bi, n0=n0):
                        n = n0 + 2 * pr
                        gate, ps = GTs[:, bi * 8 + n:bi * 8 + n + 2, :], two(bk[b][:, :])
                        if bi == 0:
                            r = V((t, t_gt, *mfree), v.scalar_tensor_tensor, M[:, n:n + 2, :], gate, 1.0, ps, ALU.add,
                                  ALU.mult)
                            tm[n] = r
                            return (r,)
                        q = cnt[0] % 2
                        cnt[0] += 1
                        r = V((t, *mfree), v.scalar_tensor_tensor, TMP[:, 2 * q:2 * q + 2, :], gate, 1.0, ps, ALU.add,
                              ALU.mult)
                        tm[n] = V((r,), v.tensor_tensor, M[:, n:n + 2, :], M[:, n:n + 2, :], TMP[:, 2 * q:2 * q + 2, :],
                                  ALU.add)
                        return (r,)
                    ncols = 1024 if k0 else 512
                    s, td = stream.get(name, i)
                    w = s.ap[:, 0:nk * ncols].rearrange("p (k n) -> p k n", k=nk)
                    for pr in range(ncols // 256):
                        b = nextbank(0, 4)
                        dense(b, 0, w, 0, nk, pr * 256, rhs, after=(td, *toks, *bfree[b]))
                        t = dense(b, 256, w, 0, nk, pr * 256 + 128, rhs)
                        bfree[b] = sink(pr, b, t)
                    stream.done(s, t)
            return tm

        M1, TMP = pg(112, 8), pg(120, 4)
        tm = merge(M1, TMP, GT, [
            ([("brr", 0, 8, 0, 0), ("brr", 1, 8, 4, 0)], GR, (t_yr,)),
            ([("brd", 0, 4, 0, 1)], YD, (t_yd,)),
            ([("brf", 0, 4, 0, 1)], YF, (avst["yf"],))], ((P.sem, P.n),))

        def project_out(name, M, tm, X):
            for i in range(2):
                s, td = stream.get(name, i)
                w = s.ap.rearrange("p (k n) -> p k n", k=8)
                for tb in range(2):
                    b = 4 + 2 * i + tb
                    for k in range(8):
                        f = P.quiet if k < 7 else P
                        t = f((td, tm[k - k % 2], *bfree[b]), pe.matmul, bk[b][:, :], M[:, k, tb * 128:(tb + 1) * 128],
                              w[:, k, :], start=(k == 0), stop=(k == 7))
                    r = V((t,), v.scalar_tensor_tensor, X[:, tb, i * 512:(i + 1) * 512], bk[b][:, :], 0.5,
                          X[:, tb, i * 512:(i + 1) * 512], ALU.mult, ALU.add)
                    bfree[b] = (r,)
                stream.done(s, t)
            return r

        t_x1 = project_out("wout", M1, tm, X)

        s_fg = sem("s_fg")
        FG = pg(116, 1, 1024)[:, 0, :]
        _, tHT = norm_T(t_x1, "g2", pg(100, 2, 1024), HT, ((P.sem, P.n),))
        AT = pg(16, 22)
        UU = [pg(40 + 4 * i, 4) for i in range(4)]
        ufree = [()] * 4
        tA = {}
        for i in range(11):
            s, td = stream.get("up", i)
            w = s.ap.rearrange("p (k n) -> p k n", k=8)
            q = i % 4
            U = UU[q]
            tc_ = []
            for kind in range(2):
                b = (2 * i + kind) % 4
                dense(b, 0, w, 0, 8, kind * 256, HT, after=(td, *tHT, *bfree[b]))
                t = dense(b, 256, w, 0, 8, kind * 256 + 128, HT)
                for h in range(2):
                    n = kind * 22 + 2 * i + h
                    ps, o = bk[b][:, h * 256:(h + 1) * 256], U[:, 2 * kind + h, :]
                    r = V((t, *ufree[q]), v.tensor_scalar, o, ps, par("fw", 88 + n), par("fb", n), ALU.mult, ALU.add)
                    for d in (1, 2):
                        r = V((r,), v.scalar_tensor_tensor, o[:, d:256], ps[:, 0:256 - d], par("fw", (2 - d) * 44 + n),
                              o[:, d:256], ALU.mult, ALU.add)
                bfree[b] = (r,)
                tc_.append(r)
                if kind == 0:
                    tg = A((r,), a.activation, U[:, 0:2, :], U[:, 0:2, :], ACT.Gelu_apprx_tanh)
            stream.done(s, t)
            r = V((tg, r), v.tensor_tensor, AT[:, 2 * i:2 * i + 2, :], U[:, 0:2, :], U[:, 2:4, :], ALU.mult)
            ufree[q] = (r,)
            tA[2 * i] = tA[2 * i + 1] = r
        A.dma(((P.sem, P.n), (V.sem, V.n)), s_fg, FG, I["final_g"].rearrange("(a n) -> a n", a=1).to_broadcast([128, 1024]))
        for i in range(6):
            s, td = stream.get("down" if i < 5 else "down5", i if i < 5 else 0)
            nk = 4 if i < 5 else 2
            w = s.ap[:, 0:nk * 1024].rearrange("p (k n) -> p k n", k=nk)
            for k in range(nk):
                kk = 4 * i + k
                for tb in range(2):
                    for hf in range(2):
                        b = 4 + 2 * tb + hf
                        t = P((td, tA[kk], *(bfree[b] if kk == 0 else ())), pe.matmul, bk[b][:, :],
                              AT[:, kk, tb * 128:(tb + 1) * 128], w[:, k, hf * 512:(hf + 1) * 512],
                              start=(kk == 0), stop=(kk == 21))
            stream.done(s, t)
        for tb in range(2):
            for hf in range(2):
                b = 4 + 2 * tb + hf
                xs = X[:, tb, hf * 512:(hf + 1) * 512]
                r = V((t,), v.tensor_tensor, xs, xs, bk[b][:, :], ALU.add)
                bfree[b] = (r,)

        def final_norm(t_in, FGt, t_fg, junk, free):
            t = rstd(t_in, X, junk, free)
            for b in range(2):
                r = V((t, t_fg), v.scalar_tensor_tensor, X[:, b, :], X[:, b, :], c_rs[:, 4 + b:5 + b], FGt, ALU.mult,
                      ALU.mult)
            return r
        t_x = final_norm(r, FG, (s_fg, 16), pg(100, 2, 1024), ((P.sem, P.n),))

        extras = []
        n_ex = 4
        exsem = [sem(f"s_e{i}") for i in range(n_ex)]
        extra_slots = [Slot(pg(62 + 16 * i, 1, KS)[:, 0, :], exsem[i], True) for i in range(n_ex)]
        s_rt, s_io, s_nf = sem("s_rt"), sem("s_io"), sem("s_nf")
        ex_toks = ()

        for l in range(2):
            XN = pg(100, 2, 1024)
            all_now = ((P.sem, P.n), (V.sem, V.n), (A.sem, A.n), (G.sem, G.n), *ex_toks)
            tzz = G(all_now, g.memset, pg(16, 28), 0.0)
            QA = pg(16, 12).rearrange("p (h c) n -> p h c n", c=2)
            QW = pg(28, 16).rearrange("p (h c) n -> p h c n", c=2)
            KA, KW = pg(44, 6), pg(50, 4)
            VA, VW = pg(54, 2, 768), pg(60, 2, 256)
            GL = pg(62, 16)
            OA, OB = pg(78, 2), pg(80, 8)
            SX = [pg(88 + 3 * i, 1, 768)[:, 0, :] for i in range(3)]
            PTL = [pg(97, 1, 768)[:, 0, :], pg(108, 1, 768)[:, 0, :]]
            ML, TMPL = pg(111, 8), pg(119, 4)
            sfree = [(), (), ()]
            ptfree = [(), ()]
            _, tHT = norm_T(t_x, f"gm{l}", XN, HT, all_now)
            tz = tzz

            def qk_sink(i):
                def f(pr, b, t):
                    n = 4 * i + 2 * pr
                    if n < 6:
                        return halves(QA, n - 2 * pr)(pr, b, t)
                    return plain(KA, n - 6 - 2 * pr)(pr, b, t)
                return f
            for i in range(3):
                pair_T(f"qka{l}", i, range(2), HT, tHT, qk_sink(i), (0, 4))
            tokmajor(f"va{l}", 0, VA, 0, 512, 512, 512, (0, 4), free=all_now)
            tokmajor(f"vb{l}", 0, VA, 512, 256, 256, 256, (0, 4))
            for i in range(2):
                pair_T(f"qw{l}", i, range(2), HT, (), halves(QW, 4 * i), (0, 4))

            def kw_sink(pr, b, t):
                for c in range(2):
                    for h in range(2):
                        for d in range(2):
                            r = A((t,), a.activation, KW[64 * d:64 * d + 64, 2 * c + h, :],
                                  bk[b][64 * h:64 * h + 64, c * 256:(c + 1) * 256], ACT.Copy)
                return (r,)
            pair_T(f"kvw{l}", 0, range(1), HT, (), kw_sink, (0, 4), release=False)
            t_v = tokmajor(f"kvw{l}", 0, VW, 0, 256, 512, 512, (0, 4), off=256)

            bslab = [stream.get(f"bias{l}_", 0), stream.get(f"bias{l}_", 1), stream.get(f"bias{l}_2", 0)]

            def bias_of(n, q0, cnt):
                s, td = bslab[n // 10]
                o = 0 if q0 else 128
                return s.ap[:, (n % 10) * 384:(n % 10 + cnt) * 384].rearrange("p (n c) -> p n c", n=cnt)[:, :, o:o + 256], td

            units = []
            for h in range(4):
                for qb in range(2):
                    i = 2 * h + qb

                    def s0(h=h, qb=qb, i=i, t_v=t_v):
                        b0 = 0 if i % 2 == 0 else 2
                        Sx, st = SX[i % 3], 4 * (i % 3)
                        r = None
                        for gi in range(3):
                            s = gi * 4 + h
                            bb, off = (b0, gi * 256) if gi < 2 else (b0 + 1, 0)
                            t0 = P((t_v, *bfree[b0], *bfree[b0 + 1]), pe.matmul, bk[bb][:, off:off + 256],
                                   QA[:, s // 2, s % 2, qb * 128:(qb + 1) * 128], KA[:, s // 2, :], start=True, stop=True)
                        for gi in range(3):
                            bb, off = (b0, gi * 256) if gi < 2 else (b0 + 1, 0)
                            bi, td = bias_of(3 * h + gi, qb, 1)
                            r = V((t0, td, *sfree[i % 3]), v.tensor_tensor_reduce, out=Sx[:, gi * 256:(gi + 1) * 256],
                                  in0=bk[bb][:, off:off + 256], in1=bi[:, 0, :], scale=0.125, scalar=-3.0e38,
                                  op0=ALU.add, op1=ALU.max, accum_out=c_mx[:, st + gi:st + gi + 1])
                        bfree[b0] = bfree[b0 + 1] = (r,)
                        r = V((r,), v.reduce_max, c_nm[:, st:st + 1], c_mx[:, st:st + 3], axis=AX, negate=True)
                        te = A((r,), a.activation, Sx[:, 0:768], Sx[:, 0:768], ACT.Exp, bias=c_nm[:, st:st + 1],
                               accum_out=c_dn[:, st:st + 1])
                        avst[("e", i)] = te

                    def s1(i=i):
                        Sx, st = SX[i % 3], 4 * (i % 3)
                        t = V((avst[("e", i)],), v.reciprocal, c_rc[:, st:st + 1], c_dn[:, st:st + 1])
                        avst[("p", i)] = V((t,), v.tensor_scalar, Sx[:, 0:768], Sx[:, 0:768], c_rc[:, st:st + 1], None,
                                           ALU.mult)

                    def s2(i=i):
                        Sx, pt = SX[i % 3], PTL[i % 2]
                        for n in range(6):
                            b = 4 + n // 4
                            t = P((avst[("p", i)], *bfree[4], *bfree[5]), pe.transpose,
                                  bk[b][:, (n % 4) * 128:(n % 4 + 1) * 128], Sx[:, n * 128:(n + 1) * 128], ident[:, :])
                        sfree[i % 3] = (t,)
                        V((t, *ptfree[i % 2]), v.tensor_copy, pt[:, 0:512], bk[4][:, :])
                        t = V((), v.tensor_copy, pt[:, 512:768], bk[5][:, 0:256])
                        bfree[4] = bfree[5] = (t,)
                        avst[("t", i)] = t

                    def s3(h=h, qb=qb, i=i):
                        pt, p0 = PTL[i % 2], 64 * (h % 2)
                        w_ = bfree[6] if i % 4 == 0 else ()
                        o = bk[6][p0:p0 + 64, qb * 128:(qb + 1) * 128]
                        for n in range(6):
                            s = (n // 2) * 4 + h
                            f = P.quiet if n < 5 else P
                            t = f((avst[("t", i)], *w_), pe.matmul, o, VA[:, n % 2, s * 64:(s + 1) * 64],
                                  pt[:, n * 128:(n + 1) * 128], start=(n == 0), stop=(n == 5))
                        ptfree[i % 2] = (t,)
                        if i % 4 == 3:
                            t = A((t,), a.activation, OA[:, h // 2, :], bk[6][:, 0:256], ACT.Copy)
                            bfree[6] = (t,)
                            avst["oa"] = t
                    units.append([s0, s1, s2, s3])
            for h in range(16):
                i = 8 + h

                def s0(h=h, i=i, l=l):
                    b0 = i % 4
                    Sx, st = SX[i % 3], 4 * (i % 3)
                    for qb in range(2):
                        t0 = P(bfree[b0], pe.matmul, bk[b0][:, qb * 256:(qb + 1) * 256],
                               QW[:, h // 2, h % 2, qb * 128:(qb + 1) * 128], KW[:, h // 4, :], start=True, stop=True)
                    for qb in range(2):
                        bi, td = bias_of(12 + h, qb, 1)
                        r = V((t0, td, *sfree[i % 3]), v.tensor_tensor_reduce, out=Sx[:, qb * 256:(qb + 1) * 256],
                              in0=bk[b0][:, qb * 256:(qb + 1) * 256], in1=bi[:, 0, :], scale=0.125, scalar=-3.0e38,
                              op0=ALU.add, op1=ALU.max, accum_out=c_mx[:, st + qb:st + qb + 1])
                    bfree[b0] = (r,)
                    sk = c_sink[:, 16 * l + h:16 * l + h + 1]
                    r = V((r,), v.tensor_scalar, c_nm[:, st:st + 2], c_mx[:, st:st + 2], sk, -1.0, ALU.max, ALU.mult)
                    for qb in range(2):
                        A((r,), a.activation, Sx[:, qb * 256:(qb + 1) * 256], Sx[:, qb * 256:(qb + 1) * 256], ACT.Exp,
                          bias=c_nm[:, st + qb:st + qb + 1], accum_out=c_dn[:, st + qb:st + qb + 1])
                    te = A((), a.activation, c_es[:, st:st + 2], c_nm[:, st:st + 2], ACT.Exp, bias=sk)
                    avst[("e", i)] = te

                def s1(i=i):
                    Sx, st = SX[i % 3], 4 * (i % 3)
                    t = V((avst[("e", i)],), v.tensor_tensor, c_dn[:, st:st + 2], c_dn[:, st:st + 2], c_es[:, st:st + 2],
                          ALU.add)
                    t = V((t,), v.reciprocal, c_rc[:, st:st + 2], c_dn[:, st:st + 2])
                    for qb in range(2):
                        tp = V((t,), v.tensor_scalar, Sx[:, qb * 256:(qb + 1) * 256], Sx[:, qb * 256:(qb + 1) * 256],
                               c_rc[:, st + qb:st + qb + 1], None, ALU.mult)
                    avst[("p", i)] = tp

                def s2(i=i):
                    Sx, b, pt = SX[i % 3], 4 + i % 2, PTL[i % 2]
                    for kb in range(2):
                        for qb in range(2):
                            t = P((avst[("p", i)], *bfree[b]), pe.transpose,
                                  bk[b][:, kb * 256 + qb * 128:kb * 256 + qb * 128 + 128],
                                  Sx[:, qb * 256 + kb * 128:qb * 256 + kb * 128 + 128], ident[:, :])
                    sfree[i % 3] = (t,)
                    t = A((t, *ptfree[i % 2]), a.activation, pt[:, 0:512], bk[b][:, :], ACT.Copy)
                    bfree[b] = (t,)
                    avst[("t", i)] = t

                def s3(h=h, i=i):
                    pt, p0 = PTL[i % 2], 64 * (h % 2)
                    w_ = bfree[6] if h % 2 == 0 else ()
                    hk = h // 4
                    for kb in range(2):
                        f = P.quiet if kb < 1 else P
                        t = f((avst[("t", i)], *w_), pe.matmul, bk[6][p0:p0 + 64, 0:256], VW[:, kb, hk * 64:(hk + 1) * 64],
                              pt[:, kb * 256:(kb + 1) * 256], start=(kb == 0), stop=(kb == 1))
                    ptfree[i % 2] = (t,)
                    if h % 2:
                        t = A((t,), a.activation, OB[:, h // 2, :], bk[6][:, 0:256], ACT.Copy)
                        bfree[6] = (t,)
                        avst["ob"] = t
                units.append([s0, s1, s2, s3])

            def slow(gen, every):
                for _ in gen:
                    for _ in range(every):
                        yield

            run_pipeline(units, slow(gate_fill(f"gate{l}", 4, GL, c_hg[:, 16 * l:16 * l + 16], 7), 3))
            for s, _ in bslab:
                stream.done(s, (V.sem, V.n))
            t_gt = (A.sem, A.n)
            t_att = ((P.sem, P.n), (V.sem, V.n), (A.sem, A.n))
            tm = merge(ML, TMPL, GL, [
                ([(f"bra{l}", 0, 2, 0, 1)], OA, (avst["oa"],)),
                ([(f"brb{l}", 0, 8, 0, 0), (f"brb{l}", 1, 8, 4, 0)], OB, (avst["ob"],))], ())
            t_x1 = project_out(f"wo{l}", ML, tm, X)
            done = ((P.sem, P.n), (V.sem, V.n), (A.sem, A.n), (G.sem, G.n))

            XN = pg(16, 2, 1024)
            XE = pg(24, 8, 512)
            PO = pg(40, 2, 512)
            PG = pg(44, 2, 512)
            GZ = [pg(48, 4), pg(52, 4)]
            RW = pg(56, 1)[:, 0, 0:128].rearrange("p (k n) -> p k n", k=8)
            IO = pg(56, 1)[:, 0, 128:160]
            LG = pg(56, 1)[:, 0, 160:192]
            AF = pg(57, 1)[:, 0, :]
            WK = pg(58, 1)[:, 0, :]
            MK = pg(59, 1)[:, 0, :]
            TA = pg(57, 1)[:, 0, :]
            YE = [pg(58, 1)[:, 0, :], pg(59, 1)[:, 0, :]]
            AF2 = pg(60, 1)[:, 0, :]
            HA = [pg(60, 1)[:, 0, :], pg(61, 1)[:, 0, :]]
            A.dma(done, s_rt, RW, I["router"][l].rearrange("(k p) n -> p k n", p=128))
            A.dma(done, s_io, IO, I["iota"])
            for s in extra_slots:
                stream.open(s, done)
            tzg = G(done, g.memset, pg(48, 8), 0.0)
            tXN, tHT = norm_T(t_x1, f"gf{l}", XN, HT, done)
            for tb in range(2):
                for k in range(8):
                    f = P.quiet if k < 7 else P
                    t = f((*tHT, (s_rt, 16 * (l + 1)), *bfree[4]), pe.matmul, bk[4][:, tb * 16:(tb + 1) * 16],
                          HT[:, k, tb * 128:(tb + 1) * 128], RW[:, k, :], start=(k == 0), stop=(k == 7))
            L2 = LG.rearrange("p (b n) -> p b n", b=2)
            t = V((t,), v.tensor_copy, LG, bk[4][:, 0:32])
            bfree[4] = (t,)
            t = V((t,), v.reduce_max, c_nm[:, 0:2], L2, axis=AX, negate=True)
            for tb in range(2):
                te = A((t,), a.activation, L2[:, tb, :], L2[:, tb, :], ACT.Exp, bias=c_nm[:, tb:tb + 1],
                       accum_out=c_dn[:, tb:tb + 1])
            t = V((te,), v.reciprocal, c_rc[:, 0:2], c_dn[:, 0:2])
            for tb in range(2):
                t_lg = V((t,), v.tensor_scalar, L2[:, tb, :], L2[:, tb, :], c_rc[:, tb:tb + 1], None, ALU.mult)
            for tb in range(2):
                t = P((t_lg, *bfree[5]), pe.transpose, bk[5][0:16, tb * 128:(tb + 1) * 128], L2[:, tb, :], ident[:, :])
            af, wk, mk = AF[0:16, :], WK[0:16, :], MK[0:16, :]
            t = V((t,), v.tensor_copy, af, bk[5][0:16, 0:256])
            bfree[5] = (t,)
            src = af
            for r_ in range(4):
                t = V((t,), v.max, c_tmp[0:16, 8 * r_:8 * r_ + 8], src)
                t = V((t,), v.match_replace, wk, c_tmp[0:16, 8 * r_:8 * r_ + 8], src, -1.0)
                src = wk
            t = V((t,), v.tensor_scalar, mk, wk, 0.0, None, ALU.is_lt)
            t = V((t,), v.tensor_scalar, wk, wk, 0.0, 1.0, ALU.mult, ALU.add)
            t = V((t,), v.tensor_tensor_scan, AF2[0:16, :], wk, mk, 0.0, ALU.mult, ALU.add)
            t = V((t,), v.tensor_tensor, mk, mk, AF2[0:16, :], ALU.mult)
            for tb in range(2):
                tt = P((t, *bfree[6]), pe.transpose, bk[6][:, tb * 16:(tb + 1) * 16], mk[:, tb * 128:(tb + 1) * 128],
                       ident[0:16, 0:16])
            t = V((tt,), v.tensor_copy, c_tmp[:, 32:64], bk[6][:, 0:32])
            bfree[6] = (t,)
            iob = IO.rearrange("p (a t) -> p a t", a=1).to_broadcast([128, 16, 32])
            for tb in range(2):
                rk = c_tmp[:, 32 + 16 * tb:48 + 16 * tb].rearrange("p (e a) -> p e a", a=1).to_broadcast([128, 16, 32])
                po = PO[:, tb, :].rearrange("p (e t) -> p e t", t=32)
                t_po = V((t, (s_io, 16 * (l + 1))), v.tensor_tensor, po, rk, iob, ALU.is_equal)
            for tb in range(2):
                po = PO[:, tb, :].rearrange("p (e t) -> p e t", t=32)
                gg = L2[:, tb, :].rearrange("p (e a) -> p e a", a=1).to_broadcast([128, 16, 32])
                t_pg = V((t_po,), v.tensor_tensor, PG[:, tb, :].rearrange("p (e t) -> p e t", t=32), po, gg, ALU.mult)
            for c in range(8):
                b = nextbank(0, 4)
                for tb in range(2):
                    f = P.quiet if tb < 1 else P
                    t = f((t_po, tXN, *bfree[b]), pe.matmul, bk[b][:, :], XN[:, tb, c * 128:(c + 1) * 128], PO[:, tb, :],
                          start=(tb == 0), stop=(tb == 1))
                r = A((t,), a.activation, XE[:, c, :], bk[b][:, :], ACT.Copy, scale=par(f"gf{l}", c)) if c % 2 else \
                    V((t,), v.tensor_scalar, XE[:, c, :], bk[b][:, :], par(f"gf{l}", c), None, ALU.mult)
                bfree[b] = (r,)
            t_xe = ((V.sem, V.n), (A.sem, A.n))
            ZR = c_tmp[0:1, 64:128]
            zk = [None]
            yfree = [(), ()]
            gzf = [(), ()]
            haf = [(), ()]

            def expert_up(e, kind, bank):
                for i in range(2):
                    s, td = stream.get(f"{kind}{l}_{e}", i)
                    w = s.ap.rearrange("p (k n) -> p k n", k=4)
                    for k in range(4):
                        for j in range(4):
                            f = P if (k == 3 and j == 3) else P.quiet
                            t = f((td, *t_xe, *bfree[bank]), pe.matmul, bk[bank][32 * j:32 * j + 32, 0:256],
                                  XE[:, 4 * i + k, 32 * e:32 * e + 32], w[:, k, 256 * j:256 * j + 256],
                                  start=(i == 0 and k == 0), stop=(i == 1 and k == 3))
                    stream.done(s, t)
                return t

            def expert_in(e):
                tg = expert_up(e, "eg", 0)
                q = e % 2
                t1 = A((tg, (V.sem, V.n), *haf[q]), a.activation, TA, bk[0][:, 0:256], ACT.Tanh, scale=0.5)
                t2 = V((t1,), v.scalar_tensor_tensor, TA, TA, 1.0, bk[0][:, 0:256], ALU.add, ALU.mult)
                bfree[0] = (t2,)
                tu = expert_up(e, "eu", 1)
                t3 = V((tu, t2), v.scalar_tensor_tensor, TA, bk[1][:, 0:256], 0.5, TA, ALU.mult, ALU.mult)
                bfree[1] = (t3,)
                for c in range(2):
                    t = P((t3, *bfree[2]), pe.transpose, bk[2][:, c * 128:(c + 1) * 128], TA[:, c * 128:(c + 1) * 128],
                          ident[:, :])
                for tb in range(2):
                    tg = P((t_pg,), pe.transpose, bk[2][0:32, 256 + tb * 128:384 + tb * 128],
                           PG[:, tb, 32 * e:32 * e + 32], ident[:, :])
                r = A((tg, *haf[q]), a.activation, HA[q], bk[2][:, 0:256], ACT.Copy)
                for j in range(4):
                    r = A((tzg, *gzf[q]), a.activation, GZ[q][32 * j:32 * j + 32, j, :],
                          bk[2][0:32, 256:512], ACT.Copy)
                bfree[2] = (r,)
                return r

            def expert_out(e, th):
                q = e % 2
                for i in range(2):
                    s, td = stream.get(f"ed{l}_{e}", i)
                    w = s.ap.rearrange("p (k n) -> p k n", k=4)
                    for k in range(4):
                        kk = 4 * i + k
                        hh = HA[q][:, (kk % 2) * 128 + (kk // 2) * 32:(kk % 2) * 128 + (kk // 2) * 32 + 32]
                        for j in range(4):
                            f = P if (k == 3 and j == 3) else P.quiet
                            t = f((td, th, *bfree[3]), pe.matmul, bk[3][32 * j:32 * j + 32, 0:256], hh,
                                  w[:, k, 256 * j:256 * j + 256], start=(i == 0 and k == 0), stop=(i == 1 and k == 3))
                    stream.done(s, t)
                haf[q] = (t,)
                r = V((t, *yfree[q]), v.tensor_copy, YE[q], bk[3][:, 0:256])
                bfree[3] = (r,)
                for tb in range(2):
                    for j in range(4):
                        b = 4 + 2 * tb + j // 2
                        t = P((r, *(bfree[b] if e == 0 else ())), pe.matmul, bk[b][:, (j % 2) * 256:(j % 2) * 256 + 256],
                              GZ[q][:, j, tb * 128:(tb + 1) * 128], YE[q], start=(e == 0 and j % 2 == 0),
                              stop=(e == 15), skip_group_check=True)
                yfree[q] = gzf[q] = (t,)
                return t

            for e in range(16):
                th = expert_in(e)
                t = expert_out(e, th)
            for tb in range(2):
                for hf in range(2):
                    b = 4 + 2 * tb + hf
                    xs = X[:, tb, hf * 512:(hf + 1) * 512]
                    r = V((t,), v.tensor_tensor, xs, xs, bk[b][:, :], ALU.add)
                    bfree[b] = (r,)
            t_x = r
            toks, _ = stream.take_extras()
            ex_toks = tuple(toks)

        done = ((P.sem, P.n), (V.sem, V.n), (A.sem, A.n), *ex_toks)
        FG = pg(40, 1, 1024)[:, 0, :]
        A.dma(done, s_nf, FG, I["norm_final"].rearrange("(a n) -> a n", a=1).to_broadcast([128, 1024]))
        t = final_norm(t_x, FG, (s_nf, 16), pg(16, 2, 1024), done)
        s_o = sem("s_o")
        S.dma((t,), s_o, out.rearrange("(b p) d -> p b d", p=128), X)
        S.wait((s_o, 16), *t_r)

        block = ctx.enter_context(nc.Block())

        @block.sync
        def _(e):
            S.play()

        @block.scalar
        def _(e):
            A.play()

        @block.vector
        def _(e):
            V.play()

        @block.gpsimd
        def _(e):
            G.play()

        @block.tensor
        def _(e):
            P.play()


def bucket(n):
    if n < 16:
        return max(n, 0)
    return min(31, 16 + int(math.log(n / 16) / math.log(8.0) * 16))


def constants():
    p = np.arange(128)[:, None]
    j = np.arange(384)[None, :]
    d = p + 128 - j
    cmask = np.where(d >= 0, 0.0, 8 * BIG).astype(np.float32)
    bias = []
    for h in range(4):
        for gi in range(3):
            ok = (np.abs(d) <= 64) if gi == 0 else (d % (4 if gi == 1 else 16) == 0)
            bias.append(np.where(ok, -8.0 * np.float32(SLOPES_A[gi * 4 + h]) * np.abs(d), 8 * BIG))
    for h in range(16):
        bias.append(np.where(np.abs(d) <= 128, -8.0 * np.float32(SLOPES_W[h]) * np.abs(d), 8 * BIG))
    bias = np.stack(bias, 1).astype(np.float32).reshape(128, 28 * 384)
    onehot = np.zeros((32, 512), np.float32)
    for u in range(512):
        onehot[bucket(255 - u), u] = 1.0
    sel = np.zeros((8, 8, 256), np.float32)
    for h in range(8):
        sel[h, h, :] = 1.0
    iota = np.tile(np.arange(1, 33, dtype=np.float32), (128, 1))
    return dict(ident=np.eye(128, dtype=np.float32), cmask=cmask, onehot=onehot, sel=sel, iota=iota), bias


def cols(w, c0, n):
    k = w.shape[0] // 128
    return w[:, c0:c0 + n].reshape(k, 128, n).transpose(1, 0, 2).reshape(128, k * n)


def rows(w, k0, nk):
    n = w.shape[1]
    return w[k0 * 128:(k0 + nk) * 128, :].reshape(nk, 128, n).transpose(1, 0, 2).reshape(128, nk * n)


def pack(I, bias):
    w = I["w_in"][0]
    d = {}
    for i in range(2):
        d["xrnn", i] = cols(w, 512 * i, 512)
        d["grnn", i] = cols(w, 1024 + 512 * i, 512)
        d["brr", i] = cols(I["w_br_rnn"][0], 512 * i, 512)
        d["wout", i] = cols(I["w_out"][0], 512 * i, 512)
    for i, n in enumerate(("dq", "dk", "dv", "fq", "fk", "fv")):
        d[n, 0] = cols(w, 2048 + 512 * i, 512)
    for i in range(6):
        d["gates", i] = cols(w, 5128 + 512 * i, 512)
    rg = np.concatenate([I["rg_w_r"][0], I["rg_w_i"][0]], 0)
    d["rg", 0] = rg.transpose(1, 0, 2).reshape(128, 2048)
    d["brd", 0] = rows(I["w_br_diff"][0], 0, 4)
    d["brf", 0] = rows(I["w_br_fox"][0], 0, 4)
    up = I["ffn_up"][0]
    for i in range(11):
        d["up", i] = cols(np.concatenate([up[:, 256 * i:256 * i + 256], up[:, 2816 + 256 * i:3072 + 256 * i]], 1), 0, 512)
    for i in range(5):
        d["down", i] = rows(I["ffn_down"][0], 4 * i, 4)
    d["down5", 0] = rows(I["ffn_down"][0], 20, 2)
    for l in range(2):
        w = I["w_in_2"][l]
        for i in range(3):
            d[f"qka{l}", i] = cols(w, 512 * i, 512)
        d[f"va{l}", 0] = cols(w, 1536, 512)
        d[f"vb{l}", 0] = cols(w, 2048, 256)
        for i in range(2):
            d[f"qw{l}", i] = cols(w, 2304 + 512 * i, 512)
            d[f"brb{l}", i] = cols(I["w_branch_b_2"][l], 512 * i, 512)
            d[f"wo{l}", i] = cols(I["w_out_2"][l], 512 * i, 512)
            d[f"bias{l}_", i] = bias[:, 3840 * i:3840 * (i + 1)]
        d[f"kvw{l}", 0] = cols(w, 3328, 512)
        d[f"bias{l}_2", 0] = bias[:, 7680:]
        for i in range(4):
            d[f"gate{l}", i] = cols(w, 3840 + 512 * i, 512)
        d[f"bra{l}", 0] = rows(I["w_branch_a_2"][l], 0, 2)
        for e in range(16):
            for i in range(2):
                d[f"eg{l}_{e}", i] = rows(I["w_expert_gate_2"][l, e], 4 * i, 4)
                d[f"eu{l}_{e}", i] = rows(I["w_expert_up_2"][l, e], 4 * i, 4)
                d[f"ed{l}_{e}", i] = rows(I["w_expert_down_2"][l, e], 4 * i, 4)
    sl = slab_list()
    out = np.zeros((len(sl), 128, KS), np.float32)
    for n, (name, i, c, _) in enumerate(sl):
        out[n, :, 0:c] = d[name, i]
    return out


def pack_params(I):
    def c(a):
        return np.asarray(a).reshape(-1, 128).T
    out = np.zeros((128, NPV), np.float32)
    for name, arr in (("g1", I["norm1_g"]), ("cw", I["rnn_conv_w"]), ("cb", I["rnn_conv_b"]), ("br", I["rg_b_r"]),
                      ("bi", I["rg_b_i"]), ("ra", I["rg_a"]), ("sub", I["diff_subln_g"]), ("gb", I["gate_b"]),
                      ("g2", I["norm2_g"]), ("fw", I["ffn_conv_w"]), ("fb", I["ffn_conv_b"]),
                      ("gm0", I["norm_mix_2"][0]), ("gm1", I["norm_mix_2"][1]), ("bg0", I["b_gate_2"][0]),
                      ("bg1", I["b_gate_2"][1]), ("gf0", I["norm_ffn_2"][0]), ("gf1", I["norm_ffn_2"][1])):
        at, n = PV[name]
        out[:, at:at + n] = c(arr)
    return out


def kernel(**inputs):
    import concourse.bacc as bacc
    from concourse.bass_utils import run_bass_kernel_spmd

    I = {k: np.asarray(x) for k, x in inputs.items()}
    consts, bias = constants()
    arrays = dict(consts)
    arrays["x"] = np.ascontiguousarray(I["x"][0])
    arrays["pv"] = pack_params(I)
    arrays["slabs"] = pack(I, bias)
    arrays["wf"] = np.ascontiguousarray(I["w_in"][0][:, 5120:5128])
    arrays["router"] = I["w_router_2"]
    arrays["rel"] = I["rel_bias"]
    arrays["fb"] = I["fox_b_f"][0]
    arrays["sink"] = I["sink_logit_2"].reshape(32)
    arrays["lq"] = np.concatenate([I[n][0] for n in ("diff_lq1", "diff_lk1", "diff_lq2", "diff_lk2")])
    arrays["final_g"] = I["final_g"]
    arrays["norm_final"] = I["norm_final_2"]
    arrays = {f"in_{k}": np.ascontiguousarray(x) for k, x in arrays.items()}
    nc = bacc.Bacc("TRN2", target_bir_lowering=False, num_devices=1)
    aps = {k[3:]: nc.dram_tensor(k, x.shape, F32, kind="ExternalInput").ap() for k, x in arrays.items()}
    out = nc.dram_tensor("out", [256, 1024], F32, kind="ExternalOutput").ap()
    build(nc, aps, out)
    r = run_bass_kernel_spmd(nc, [arrays], core_ids=[0])
    return r.results[0]["out"].reshape(1, 256, 1024)
```

```python
import math
import numpy as np
import concourse.bass as bass
from concourse import mybir

F32 = mybir.dt.float32
F32R = mybir.dt.float32r
ACT = mybir.ActivationFunctionType
ALU = mybir.AluOpType
AX = mybir.AxisListType.X

KS, CS = 4096, 256
BIG = -1.0e30
SLOPES_A = [float(np.float32(2.0) ** np.float32(-8.0 * i / 12)) for i in range(1, 13)]
SLOPES_W = [float(np.float32(2.0) ** np.float32(-8.0 * i / 16)) for i in range(1, 17)]



def slab_list():
    s = []

    def add(name, n, cols=KS, extra=False):
        for i in range(n):
            s.append((name, i, cols, extra))
    add("xrnn", 2)
    add("grnn", 2)
    add("dq", 1)
    add("dk", 1)
    add("dv", 1)
    add("fq", 1)
    add("fk", 1)
    add("fv", 1)
    add("gates", 6)
    add("brr", 2)
    add("brd", 1)
    add("brf", 1)
    add("wout", 2)
    add("up", 11)
    add("down", 5)
    add("down5", 1, 2048)
    for l in range(2):
        add(f"qka{l}", 3)
        add(f"va{l}", 1)
        add(f"vb{l}", 1, 2048)
        add(f"qw{l}", 2)
        add(f"kvw{l}", 1)
        add(f"gate{l}", 4)
        add(f"bra{l}", 1, 2048)
        add(f"brb{l}", 2)
        add(f"wo{l}", 2)
        for e in range(16):
            add(f"eg{l}_{e}", 2, KS, True)
            add(f"eu{l}_{e}", 2, KS, True)
            add(f"ed{l}_{e}", 2, KS, True)
    return s


PV = {}
_at = 0
for _n, _w in [("g1", 8), ("cw", 32), ("cb", 8), ("br", 8), ("bi", 8), ("ra", 8), ("sub", 1), ("gb", 24),
               ("g2", 8), ("fw", 132), ("fb", 44), ("gm0", 8), ("gm1", 8), ("bg0", 16), ("bg1", 16),
               ("gf0", 8), ("gf1", 8)]:
    PV[_n] = (_at, _w)
    _at += _w
NPV = _at


class Queue:

    def __init__(self, eng, sem):
        self.eng, self.sem, self.n, self.items, self.seen = eng, sem, 0, [], {}

    def wait(self, *toks):
        for sem, v in toks:
            if self.seen.get(sem.name, 0) < v:
                self.seen[sem.name] = v
                self.items.append((self.eng.wait_ge, (sem, v), {}, None, 0))

    def __call__(self, after, fn, *a, **k):
        self.wait(*after)
        self.n += 1
        self.items.append((fn, a, k, self.sem, 1))
        return (self.sem, self.n)

    def quiet(self, after, fn, *a, **k):
        self.wait(*after)
        self.items.append((fn, a, k, None, 0))

    def dma(self, after, sem, out, in_):
        self.wait(*after)
        self.items.append((self.eng.dma_start, (out, in_), {}, sem, 16))

    def play(self):
        for fn, a, k, sem, by in self.items:
            i = fn(*a, **k)
            if sem is not None:
                i.then_inc(sem, by)


class Slot:
    def __init__(self, ap, sem, extra):
        self.ap, self.sem, self.extra, self.count, self.free = ap, sem, extra, 0, ()


class Stream:

    def __init__(self, sp, slabs, dram):
        self.sp, self.slabs, self.dram, self.next = sp, slabs, dram, 0
        self.ready, self.idle = {}, []

    def open(self, slot, free=()):
        slot.free = free
        self.idle.append(slot)
        self.fill()

    def fill(self):
        while self.next < len(self.slabs):
            name, i, cols, extra = self.slabs[self.next]
            pick = [s for s in self.idle if extra or not s.extra]
            if not pick:
                return
            s = pick[0]
            self.idle.remove(s)
            s.count += 16
            self.sp.dma(s.free, s.sem, s.ap[:, 0:cols], self.dram[self.next, :, 0:cols])
            self.ready[(name, i)] = (s, (s.sem, s.count))
            self.next += 1

    def get(self, name, i=0):
        return self.ready[(name, i)]

    def done(self, slot, *toks):
        self.open(slot, toks)

    def retire(self, slot):
        self.idle.remove(slot)
        return slot.free

    def take_extras(self):
        out = [s for s in self.idle if s.extra]
        self.idle = [s for s in self.idle if not s.extra]
        return [t for s in out for t in s.free], out


class Splitter:

    def __init__(self, hi_eng, lo_eng, stream, bufs):
        self.A, self.V, self.stream = hi_eng, lo_eng, stream
        self.plan, self.made, self.used, self.ready = [], 0, 0, {}
        self.idle = [(b, ()) for b in bufs]
        self.out = []
        self.back = iter(())

    def add(self, name, i, views):
        for n, view in enumerate(views):
            self.plan.append((name, i, view, n == len(views) - 1))

    def make(self):
        name, i, view, last = self.plan[self.made]
        slot, td = self.stream.get(name, i)
        buf, free = self.idle.pop(0)
        src = view(slot.ap)
        a, b = src.shape[1], src.shape[2]
        hi, lo = (x[:, 0:a * b].rearrange("p (a b) -> p a b", a=a) for x in buf)
        th = self.A((td, *free), self.A.eng.activation, hi, src, ACT.Copy)
        tl = self.V((th,), self.V.eng.tensor_tensor, lo, src, hi.bitcast(F32), ALU.subtract)
        if last:
            self.stream.done(slot, tl)
        self.ready[self.made] = (hi, lo, (th, tl), buf)
        self.made += 1

    def take(self):
        next(self.back, None)
        while self.idle and self.made < len(self.plan):
            self.make()
        self.used += 1
        hi, lo, toks, self.out = self.ready.pop(self.used - 1)
        return hi, lo, toks

    def done(self, tok):
        self.idle.append((self.out, (tok,)))


def v_cols(pr, kh):
    return lambda ap: ap.rearrange("p (k n) -> p k n", k=8)[:, 4 * kh:4 * kh + 4, 256 * pr:256 * pr + 256]


def v_flat(j, a, b):
    return lambda ap: ap[:, j * a * b:(j + 1) * a * b].rearrange("p (a b) -> p a b", a=a)


def v_rows(pr, nk):
    return lambda ap: ap[:, 0:nk * 1024].rearrange("p (k n) -> p k n", k=nk)[:, :, 256 * pr:256 * pr + 256]


PAIRS = [v_cols(pr, kh) for pr in range(2) for kh in range(2)]
TOKS = [v_flat(j, 2, 512) for j in range(4)]


def build(nc, I, out):
    slabs = slab_list()
    from contextlib import ExitStack
    ctx = ExitStack()
    with ctx:
        def sb(name, shape):
            return ctx.enter_context(nc.sbuf_tensor(name, shape, F32))

        def sem(name):
            return ctx.enter_context(nc.semaphore(name))

        P = Queue(nc.tensor, sem("s_pe"))
        V = Queue(nc.vector, sem("s_dve"))
        A = Queue(nc.scalar, sem("s_act"))
        G = Queue(nc.gpsimd, sem("s_pool"))
        S = Queue(nc.sync, sem("s_sp"))
        v, a, g, pe = nc.vector, nc.scalar, nc.gpsimd, nc.tensor

        A0, CUTS = 22528, (0, 24, 48, 96, 148, 201)

        def at(name, cols, offset, dt=F32):
            return nc.alloc_sbuf_tensor_at(name, [128, cols], dt, offset=offset)
        ident, pv = at("ident", 128, 16512), at("pv", NPV, 17024)
        sm, cmask = at("sm", 640, 18432), at("cmask", 384, 20992)
        arena = {dt: [at(f"{n_}{lo}", (hi - lo) * 256, A0 + lo * 1024, dt) for lo, hi in zip(CUTS, CUTS[1:])]
                 for n_, dt in (("pages", F32), ("pages_r", F32R))}

        def pages(dt, first, n, cols):
            i = max(j for j, lo in enumerate(CUTS) if lo <= first)
            c = (first - CUTS[i]) * 256
            return arena[dt][i][:, c:c + n * cols].rearrange("p (n c) -> p n c", n=n)
        bk = [ctx.enter_context(nc.psum_tensor(f"bank{i}", [128, 512], F32)) for i in range(8)]
        bfree = [()] * 8
        scr = nc.dram_tensor("scratch", [4, 128 * 512], F32, kind="Internal").ap()

        def pg(at, n, cols=256):
            return pages(F32, at, n, cols)

        def pr_(at, n, cols=256):
            return pages(F32R, at, n, cols)

        class Two:

            def __init__(self, hi, lo, n, cols=256):
                self.h, self.l, self.raw = pr_(hi, n, cols), pr_(lo, n, cols), pg(lo, n, cols)
                self.hf, self.lf = self.h.bitcast(F32), self.l.bitcast(F32)

        def par(name, i=0, n=1):
            return pv[:, PV[name][0] + i:PV[name][0] + i + n]

        s_x, s_c, s_id, s_m = sem("s_x"), sem("s_c"), sem("s_id"), sem("s_m")
        stream = Stream(S, slabs, I["slabs"])

        X = pg(0, 2, 1024)
        HT = Two(8, 16, 8)
        wb = [[pr_(24 + 8 * i + o, 4).rearrange("p n c -> p (n c)") for o in (0, 4)] for i in range(3)]
        ringp = [48, 64, 80]
        S.dma((), s_x, X, I["x"].rearrange("(b p) d -> p b d", p=128))
        t_x = (s_x, 16)
        S.dma((), s_id, ident[:, :], I["ident"])
        S.dma((), s_id, pv[:, :], I["pv"])
        t_c = (s_id, 32)
        slots = [Slot(pg(ringp[i], 1, KS)[:, 0, :], sem(f"s_w{i}"), False) for i in range(3)]
        for s_ in slots[0:2]:
            stream.open(s_)
        sp = Splitter(A, V, stream, wb)
        A.dma((), s_m, cmask[:, :], I["cmask"])

        c_ss, c_rs = sm[:, 0:8], sm[:, 8:16]
        c_sp4, c_t1, c_t2, c_t3 = sm[:, 16:24], sm[:, 24:32], sm[:, 32:40], sm[:, 40:48]
        c_lam, c_sub = sm[:, 48:52], sm[:, 52:53]
        c_hb = sm[:, 56:96]
        c_hg = sm[:, 96:128]
        c_mx, c_nm, c_dn, c_rc = sm[:, 128:140], sm[:, 140:152], sm[:, 152:164], sm[:, 164:176]
        c_lq = sm[:, 192:448]
        c_sink = sm[:, 448:480]
        c_fb = sm[:, 480:481]
        c_rel = sm[:, 484:488]
        c_es = sm[:, 488:500]
        c_tmp = sm[:, 512:640]

        A.dma((), s_c, c_lq, I["lq"].rearrange("(a n) -> a n", a=1).to_broadcast([128, 256]))
        A.dma((), s_c, c_sink, I["sink"].rearrange("(a n) -> a n", a=1).to_broadcast([128, 32]))
        A.dma((), s_c, c_fb[0:8, :], I["fb"].rearrange("(n a) -> n a", a=1))
        A.dma((), s_c, c_rel[0:32, :], I["rel"])
        t_s = (s_c, 64)

        def split_out(t, dst, src, scale=None, free=()):
            d_h, d_l, d_hf = dst
            if scale is None:
                th = A((t, *free), a.activation, d_h, src, ACT.Copy)
                return V((th,), v.tensor_tensor, d_l, src, d_hf, ALU.subtract)
            th = A((t, t_c, *free), a.activation, d_h, src, ACT.Copy, scale=scale)
            return V((th,), v.scalar_tensor_tensor, d_l, src, scale, d_hf, ALU.mult, ALU.subtract)

        def rstd(t_in, src, junk, free=()):
            t = A((t_in, *free), a.activation, junk[:, 0, :], src[:, 0, :], ACT.Square, accum_out=c_ss[:, 0:1])
            t1 = V((t_in, *free), v.tensor_tensor_reduce, out=junk[:, 1, :], in0=src[:, 1, :], in1=src[:, 1, :],
                   scale=1.0, scalar=0.0, op0=ALU.mult, op1=ALU.add, accum_out=c_ss[:, 1:2])
            t = V((t, t1), v.tensor_scalar, c_rs[:, 0:2], c_ss[:, 0:2], 1.0 / 1024, 1e-6, ALU.mult, ALU.add)
            t = A((t,), a.activation, c_rs[:, 2:4], c_rs[:, 0:2], ACT.Sqrt)
            return V((t,), v.reciprocal, c_rs[:, 4:6], c_rs[:, 2:4])

        def norm_T(t_in, gname, XN, HT, free=()):
            t = rstd(t_in, X, XN, free)
            for b in range(2):
                tn = V((t,), v.tensor_scalar, XN[:, b, :], X[:, b, :], c_rs[:, 4 + b:5 + b], None, ALU.mult)
            th = []
            for pr in range(4):
                b = pr
                for h in range(2):
                    for tb in range(2):
                        c = 2 * pr + h
                        tt = P((tn, t_c, *bfree[b]), pe.transpose,
                               bk[b][:, h * 256 + tb * 128:h * 256 + tb * 128 + 128],
                               XN[:, tb, c * 128:(c + 1) * 128], ident[:, :])
                cs = [(2 * pr + h, bk[b][:, h * 256:(h + 1) * 256]) for h in range(2)]
                if isinstance(HT, Two):
                    for c, ps in cs:
                        te = A((tt, t_c), a.activation, HT.h[:, c, :], ps, ACT.Copy, scale=par(gname, c))
                    for c, ps in cs:
                        te = V((te,), v.scalar_tensor_tensor, HT.l[:, c, :], ps, par(gname, c), HT.hf[:, c, :],
                               ALU.mult, ALU.subtract)
                else:
                    for c, ps in cs:
                        if pr % 2:
                            te = A((tt, t_c), a.activation, HT[:, c, :], ps, ACT.Copy, scale=par(gname, c))
                        else:
                            te = V((tt, t_c), v.tensor_scalar, HT[:, c, :], ps, par(gname, c), None, ALU.mult)
                bfree[b] = (te,)
                th.append(te)
            return tn, th

        def mm3(q, out_, wh, wl, xh, xl, start, stop, after=()):
            P.quiet(after, pe.matmul, out_, wh, xh, start=start, stop=False, skip_group_check=True)
            P.quiet((), pe.matmul, out_, wh, xl, start=False, stop=False, skip_group_check=True)
            return q((), pe.matmul, out_, wl, xh, start=False, stop=stop, skip_group_check=True)

        rot = [0]

        def nextbank(lo, hi):
            rot[0] += 1
            return lo + rot[0] % (hi - lo)

        def pair(b, npieces, k_per, X2, tin=()):
            for j in range(npieces):
                wh, wl, tw = sp.take()
                for c in range(2):
                    for k in range(k_per):
                        end = c == 1 and k == k_per - 1
                        t = mm3(P if end else P.quiet, bk[b][:, c * 256:(c + 1) * 256], wh[:, k, c * 128:(c + 1) * 128],
                                wl[:, k, c * 128:(c + 1) * 128], X2.h[:, j * k_per + k, :], X2.l[:, j * k_per + k, :],
                                start=(j == 0 and k == 0 and c == 0), stop=(j == npieces - 1 and end),
                                after=(*tw, *tin, *bfree[b]))
                sp.done(t)
            return t

        def pair_T(prs, rhs, tin, sink, banks):
            for pr in prs:
                b = nextbank(*banks)
                t = pair(b, 2, 4, rhs, tin)
                bfree[b] = sink(pr, b, t)

        def two(ap):
            return ap.rearrange("p (n c) -> p n c", n=2)

        for n_, i_ in (("xrnn", 0), ("xrnn", 1), ("grnn", 0), ("grnn", 1), ("dq", 0), ("dk", 0)):
            sp.add(n_, i_, PAIRS)
        sp.add("dv", 0, TOKS)
        sp.add("fq", 0, PAIRS)
        sp.add("fk", 0, PAIRS)
        sp.add("fv", 0, TOKS)
        for i_ in range(6):
            sp.add("gates", i_, PAIRS)
        for i_ in range(2):
            sp.add("brr", i_, PAIRS)
        sp.add("brd", 0, [v_rows(pr, 4) for pr in range(4)])
        sp.add("brf", 0, [v_rows(pr, 4) for pr in range(4)])
        for i_ in range(2):
            sp.add("wout", i_, TOKS)
        for i_ in range(11):
            sp.add("up", i_, PAIRS)
        for i_ in range(6):
            sp.add("down" if i_ < 5 else "down5", i_ if i_ < 5 else 0, [v_flat(j, 1, 1024) for j in range(4 if i_ < 5 else 2)])

        XN1 = pg(158, 2, 1024)
        _, tHT = norm_T(t_x, "g1", XN1, HT)

        GT = pg(96, 24)
        QD = pg(120, 8).rearrange("p (h c) n -> p h c n", c=2)
        KD, VD = pg(128, 4), pg(132, 2, 512)
        QF = pg(136, 8).rearrange("p (h c) n -> p h c n", c=2)
        KF, VF = pg(144, 4), pg(148, 2, 512)
        BT = pg(152, 4, 384)
        XC, GR, TR, TI, AA = pg(158, 8), pg(166, 8), pg(174, 8), pg(182, 8), pg(190, 8)
        YR = Two(166, 174, 8)
        YD, YF = Two(80, 84, 4), Two(88, 92, 4)
        O = pg(158, 2, 512)
        SD = [pg(198, 1, 768)[:, 0, :], pg(162, 1, 768)[:, 0, :]]
        PTB = [pg(194, 1, 384)[:, 0, :], pg(196, 1, 384)[:, 0, :]]
        LH, RH = pg(182, 8), pg(190, 2)
        QC = pg(192, 2)
        OH = pg(198, 2)
        REL = pg(190, 4, 512)
        WF = pg(200, 1)[:, 0, 0:64].rearrange("p (k n) -> p k n", k=8)

        tz = G((), g.memset, QD, 0.0)
        tz = G((), g.memset, QF, 0.0)

        s_oh, s_wf, s_b, s_rg = sem("s_oh"), sem("s_wf"), sem("s_b"), sem("s_rg")
        RG = pg(80, 8).rearrange("p n c -> p (n c)").rearrange("p (k n) -> p k n", k=16)
        G.dma((), s_rg, pg(80, 8).rearrange("p n c -> p (n c)"), I["rg"])
        s_r = [sem(f"s_r{h}") for h in range(4)]
        t_r = tuple((q, 16) for q in s_r)
        A.dma((), s_oh, OH.rearrange("p n c -> p (n c)")[0:32, :], I["onehot"])
        A.dma((), s_wf, WF, I["wf"].rearrange("(k p) n -> p k n", p=128))
        for h in range(4):
            b = 4 + h
            t = P((t_s, (s_oh, 16), *bfree[b]), pe.matmul, bk[b][:, :], c_rel[0:32, h:h + 1].to_broadcast([32, 128]),
                  OH.rearrange("p n c -> p (n c)")[0:32, :], start=True, stop=True)
            t = A((t,), a.activation, REL[:, h, :], bk[b][:, :], ACT.Copy)
            bfree[b] = (t,)
            G.dma((t,), s_r[h], scr[h].rearrange("(p n) -> p n", p=128), REL[:, h, :])
        skew = bass.AP(scr.tensor, 127, [[511, 128], [65536, 4], [1, 384]])
        G.dma(t_r, s_b, BT, skew)

        tC = [None] * 8

        def conv_rnn(i):
            def f(pr, b, t):
                for h in range(2):
                    n = 4 * i + 2 * pr + h
                    r0 = A((t, t_c), a.activation, XC[:, n, :], bk[b][:, h * 256:(h + 1) * 256], ACT.Identity,
                           scale=par("cw", 24 + n), bias=par("cb", n))
                for h in range(2):
                    n = 4 * i + 2 * pr + h
                    ps = bk[b][:, h * 256:(h + 1) * 256]
                    o = XC[:, n, :]
                    r = r0
                    for d in range(1, 4):
                        r = V((r,), v.scalar_tensor_tensor, o[:, d:256], ps[:, 0:256 - d],
                              par("cw", (3 - d) * 8 + n), o[:, d:256], ALU.mult, ALU.add)
                    tC[n] = r
                return (r,)
            return f
        for i in range(2):
            pair_T(range(2), HT, tHT, conv_rnn(i), (0, 4))

        def gelu_g(i):
            def f(pr, b, t):
                n = 4 * i + 2 * pr
                r = A((t,), a.activation, GR[:, n:n + 2, :], two(bk[b][:, :]), ACT.Gelu_apprx_tanh)
                return (r,)
            return f
        for i in range(2):
            pair_T(range(2), HT, (), gelu_g(i), (0, 4))
        t_gr = (A.sem, A.n)

        tsl = V((t_s, t_c), v.tensor_scalar, c_hb[:, 0:16], par("br", 0, 16), 0.5, None, ALU.mult)
        V((), v.tensor_scalar, c_hb[:, 16:40], par("gb", 0, 24), 0.5, None, ALU.mult)
        V((), v.tensor_scalar, c_hg, par("bg0", 0, 32), 0.5, None, ALU.mult)
        t_hb = V((), v.tensor_scalar, c_sub, par("sub"), 0.8, None, ALU.mult)
        t = V((t_c,), v.scalar_tensor_tensor, c_t1, par("ra", 0, 8), -1.0, par("ra", 0, 8), ALU.mult, ALU.min)
        t = A((t,), a.activation, c_t1, c_t1, ACT.Exp)
        t = V((t,), v.tensor_scalar, c_t2, c_t1, 2.0, None, ALU.add)
        t = V((t,), v.reciprocal, c_t2, c_t2)
        t = V((t,), v.tensor_tensor, c_t1, c_t1, c_t2, ALU.mult)
        t = V((t,), v.tensor_tensor, c_t2, c_t1, c_t1, ALU.mult)
        t = V((t,), v.tensor_scalar, c_t3, c_t2, 1.0 / 17, 1.0 / 15, ALU.mult, ALU.add)
        for d in (13, 11, 9, 7, 5, 3, 1):
            t = V((t,), v.tensor_tensor, c_t3, c_t3, c_t2, ALU.mult)
            t = V((t,), v.tensor_scalar, c_t3, c_t3, 1.0 / d, None, ALU.add)
        t = V((t,), v.tensor_tensor, c_t3, c_t3, c_t1, ALU.mult)
        t = V((t,), v.tensor_scalar, c_t3, c_t3, 8.0, None, ALU.mult)
        t2 = V((t,), v.tensor_scalar, c_t1, par("ra", 0, 8), -4.0, 0.0, ALU.mult, ALU.max)
        t_sp = V((t2,), v.tensor_tensor, c_sp4, c_t3, c_t1, ALU.add)
        for i in range(2):
            t = V((t_s,), v.tensor_tensor, c_tmp[:, i * 64:(i + 1) * 64], c_lq[:, i * 128:i * 128 + 64],
                  c_lq[:, i * 128 + 64:i * 128 + 128], ALU.mult)
        t = V((t,), v.reduce_sum, c_lam[:, 0:2], two(c_tmp), axis=AX)
        t = A((t,), a.activation, c_lam[:, 0:2], c_lam[:, 0:2], ACT.Exp)
        t = V((t,), v.tensor_tensor, c_lam[:, 2:3], c_lam[:, 1:2], c_lam[:, 0:1], ALU.subtract)
        t_lam = V((t,), v.tensor_scalar, c_lam[:, 3:4], c_lam[:, 2:3], -0.2, None, ALU.add)


        def halves(dst, at=0, free=()):
            def f(pr, b, t):
                src = two(bk[b][:, :])
                for h in range(2):
                    p0 = 64 * h
                    r = A((t, tz, *free), a.activation, dst[p0:p0 + 64, at + 2 * pr:at + 2 * pr + 2, h, :],
                          src[p0:p0 + 64, :, :], ACT.Copy)
                return (r,)
            return f

        def plain(dst, at=0, eng=None, free=()):
            def f(pr, b, t):
                d, s_ = dst[:, at + 2 * pr:at + 2 * pr + 2, :], two(bk[b][:, :])
                if eng is V:
                    return (V((t, *free), v.tensor_copy, d, s_),)
                return (A((t, *free), a.activation, d, s_, ACT.Copy),)
            return f

        def tokmajor(dst, c0, nc_, banks, npieces, k_per, free=()):
            bs = (nextbank(*banks), nextbank(*banks))
            for j in range(npieces):
                wh, wl, tw = sp.take()
                for tb in range(2):
                    for k in range(k_per):
                        kk = j * k_per + k
                        end = tb == 1 and k == k_per - 1
                        q = slice(tb * 128, (tb + 1) * 128)
                        t = mm3(P if end else P.quiet, bk[bs[tb]][:, 0:nc_], HT.h[:, kk, q], HT.l[:, kk, q],
                                wh[:, k, :], wl[:, k, :], start=(kk == 0), stop=(kk == 7), after=(*tw, *bfree[bs[tb]]))
                sp.done(t)
            for tb in range(2):
                r = A((t, *free), a.activation, dst[:, tb, c0:c0 + nc_], bk[bs[tb]][:, 0:nc_], ACT.Copy)
                bfree[bs[tb]] = (r,)
            return r

        last = {}

        def rnn():
            for n in range(8):
                for q in range(2):
                    t = P(((s_rg, 16), tC[n], *bfree[7]), pe.matmul, bk[7][:, q * 256:(q + 1) * 256], RG[:, q * 8 + n, :],
                          XC[:, n, :], start=True, stop=True)
                A((t, t_hb), a.activation, TR[:, n, :], bk[7][:, 0:256], ACT.Tanh, bias=c_hb[:, n:n + 1], scale=0.5)
                r = A((), a.activation, TI[:, n, :], bk[7][:, 256:512], ACT.Tanh, bias=c_hb[:, 8 + n:9 + n], scale=0.5)
                bfree[7] = (r,)
                ty = V((r, t_sp), v.tensor_scalar, TR[:, n, :], TR[:, n, :], 1.0, c_sp4[:, n:n + 1], ALU.add, ALU.mult)
                if n % 2:
                    yield
            tr, tt = (V.sem, V.n), {}
            qs = [slice(2 * q, 2 * q + 2) for q in range(4)]
            for q in qs:
                te = A((tr, *t_r), a.activation, AA[:, q, :], TR[:, q, :], ACT.Exp, scale=-1.0)
                tt[q.start] = A((te,), a.activation, TR[:, q, :], TR[:, q, :], ACT.Tanh)
                yield
            for q in qs:
                t = V((tt[q.start],), v.scalar_tensor_tensor, TI[:, q, :], TI[:, q, :], 1.0, XC[:, q, :], ALU.add, ALU.mult)
                t = V((t,), v.tensor_scalar, XC[:, q, :], TR[:, q, :], 1.0, None, ALU.add)
                t = V((t,), v.reciprocal, XC[:, q, :], XC[:, q, :])
                t = V((t,), v.tensor_tensor, TR[:, q, :], TR[:, q, :], XC[:, q, :], ALU.mult)
                yield
            for q in qs:
                tt[q.start] = A((t,), a.activation, TR[:, q, :], TR[:, q, :], ACT.Sqrt, scale=0.5)
            yield
            for q in qs:
                t = V((tt[q.start],), v.tensor_tensor, TI[:, q, :], TI[:, q, :], TR[:, q, :], ALU.mult)
                for n in (q.start, q.start + 1):
                    ts = V((t,), v.tensor_tensor_scan, XC[:, n, :], AA[:, n, :], TI[:, n, :], 0.0, ALU.mult, ALU.add)
                yield
                t = V((ts, t_gr), v.tensor_tensor, XC[:, q, :], GR[:, q, :], XC[:, q, :], ALU.mult)
                last["yr"] = split_out(t, (YR.h[:, q, :], YR.l[:, q, :], YR.hf[:, q, :]), XC[:, q, :])
                yield
        sp.back = rnn()

        pair_T(range(2), HT, (), halves(QD), (0, 4))
        pair_T(range(2), HT, (), plain(KD), (0, 4))
        t_vd = tokmajor(VD, 0, 512, (0, 4), 4, 2)
        pair_T(range(2), HT, (), halves(QF), (0, 4))
        pair_T(range(2), HT, (), plain(KF), (0, 4))
        t_vf = tokmajor(VF, 0, 512, (0, 4), 4, 2)

        for _ in sp.back:
            pass
        t_yr = last["yr"]

        b = nextbank(0, 4)
        for k in range(8):
            P.quiet(((s_wf, 16), *bfree[b]), pe.matmul, bk[b][0:8, 0:256], WF[:, k, :], HT.hf[:, k, :],
                    start=(k == 0), stop=False)
            f = P.quiet if k < 7 else P
            t = f((), pe.matmul, bk[b][0:8, 0:256], WF[:, k, :], HT.lf[:, k, :], start=False, stop=(k == 7))
        Z, Z2 = XC[0:8, 4, :], XC[0:8, 5, :]
        lf = XC[0:8, 6, :]
        on = XC[0:8, 7, :]
        t = V((t, t_yr), v.tensor_scalar, Z, bk[b][0:8, 0:256], c_fb[0:8, :], None, ALU.add)
        bfree[b] = (t,)
        t = V((t,), v.scalar_tensor_tensor, Z2, Z, -1.0, Z, ALU.mult, ALU.min)
        t = A((t,), a.activation, Z2, Z2, ACT.Exp)
        t = A((t,), a.activation, Z2, Z2, ACT.Ln, bias=1.0)
        t = V((t,), v.tensor_scalar, Z, Z, 0.0, None, ALU.min)
        t = V((t,), v.tensor_tensor, Z, Z, Z2, ALU.subtract)
        V((), v.memset, on, 1.0)
        t = (V.sem, V.n)
        t = V((t,), v.tensor_tensor_scan, lf, on, Z, 0.0, ALU.mult, ALU.add)
        s_l = sem("s_l")
        G((t_yr,), g.memset, LH, 0.0)
        tl = G((t_yr,), g.memset, pg(190, 4), 0.0)
        A.dma((tl,), s_l, LH[0:8, :, :], I["sel"])
        V((t, tl), v.tensor_scalar, RH[0:8, 0, :], lf, -8.0, None, ALU.mult)
        t_l = V((t, tl), v.tensor_scalar, QC[0:8, 0, :], lf, 8.0, None, ALU.mult)

        def gate_fill(npairs, dst, hb, bank, free=()):
            for n in range(0, 2 * npairs, 2):
                t = pair(bank, 2, 4, HT)
                for h in range(2):
                    r = A((t, *free), a.activation, dst[:, n + h, :], bk[bank][:, h * 256:(h + 1) * 256], ACT.Tanh,
                          bias=hb[:, n + h:n + h + 1], scale=0.5)
                bfree[bank] = (r,)
                yield

        def run_pipeline(units, filler, per=1):
            for step in range(len(units) + 3):
                for j in (2, 0, 1, 3):
                    if j == 0:
                        for _ in range(per):
                            next(filler, None)
                    i = step - j
                    if 0 <= i < len(units):
                        units[i][j]()
            for _ in filler:
                pass

        for h in range(4):
            t_bt = V(((s_b, 16), (s_m, 16)), v.scalar_tensor_tensor, BT[:, h, :], BT[:, h, :], 8.0, cmask[:, :],
                     ALU.mult, ALU.add)
        sfree = [(), (), ()]
        ptfree = [(), ()]
        avst = {}

        def scores_row(ps, bias, S_, st, tok, free):
            return V((tok, *free), v.tensor_tensor_reduce, out=S_, in0=ps, in1=bias, scale=0.125, scalar=-3.0e38,
                     op0=ALU.add, op1=ALU.max, accum_out=c_mx[:, st:st + 1])

        units = []
        for h in range(4):
            i = h

            def s0(h=h, i=i):
                b0 = 0 if i % 2 == 0 else 2
                pa, pb_ = bk[b0], bk[b0 + 1]
                for c in range(2):
                    t0 = P((tz, t_hb, (A.sem, A.n), *bfree[b0], *bfree[b0 + 1]), pe.matmul, pa[:, c * 128:(c + 1) * 128],
                           QD[:, h, c, 0:128], KD[:, h, 0:128], start=True, stop=True)
                for c in range(2):
                    t0 = P((), pe.matmul, pb_[:, c * 256:(c + 1) * 256],
                           QD[:, h, c, 128:256], KD[:, h, :], start=True, stop=True)
                Sx = SD[i % 2]
                st = 4 * (i % 3)
                fr = sfree[i % 2]
                r = []
                r.append(scores_row(pa[:, 0:128], BT[:, h, 128:256], Sx[:, 0:128], st, t0, (*fr, t_bt)))
                r.append(scores_row(pa[:, 128:256], BT[:, h, 128:256], Sx[:, 128:256], st + 1, t0, ()))
                r.append(scores_row(pb_[:, 0:256], BT[:, h, 0:256], Sx[:, 256:512], st + 2, t0, ()))
                r.append(scores_row(pb_[:, 256:512], BT[:, h, 0:256], Sx[:, 512:768], st + 3, t0, ()))
                bfree[b0] = bfree[b0 + 1] = (r[-1],)
                tn = V((r[-1],), v.tensor_scalar, c_nm[:, st:st + 4], c_mx[:, st:st + 4], -1.0, None, ALU.mult)
                for q, (lo, hi) in enumerate(((0, 128), (128, 256), (256, 512), (512, 768))):
                    te = A((tn,), a.activation, Sx[:, lo:hi], Sx[:, lo:hi], ACT.Exp, bias=c_nm[:, st + q:st + q + 1],
                           accum_out=c_dn[:, st + q:st + q + 1])
                avst[("e", i)] = te

            def s1(h=h, i=i):
                Sx = SD[i % 2]
                st = 4 * (i % 3)
                t = V((avst[("e", i)],), v.reciprocal, c_rc[:, st:st + 4], c_dn[:, st:st + 4])
                for c in (1, 3):
                    tm = V((t, t_lam), v.tensor_scalar, c_rc[:, st + c:st + c + 1], c_rc[:, st + c:st + c + 1],
                           c_lam[:, 3:4], None, ALU.mult)
                for q, (lo, mid, hi) in enumerate(((0, 128, 256), (256, 512, 768))):
                    t = V((tm,), v.tensor_scalar, Sx[:, lo:mid], Sx[:, lo:mid], c_rc[:, st + 2 * q:st + 2 * q + 1], None,
                          ALU.mult)
                    t = V((t,), v.scalar_tensor_tensor, Sx[:, lo:mid], Sx[:, mid:hi],
                          c_rc[:, st + 2 * q + 1:st + 2 * q + 2], Sx[:, lo:mid], ALU.mult, ALU.add)
                avst[("p", i)] = t

            def s2(h=h, i=i):
                Sx, b, pt = SD[i % 2], 4 + i % 2, PTB[i % 2]
                for n, lo in enumerate((0, 256, 384)):
                    t = P((avst[("p", i)], *bfree[b]), pe.transpose, bk[b][:, n * 128:(n + 1) * 128], Sx[:, lo:lo + 128],
                          ident[:, :])
                sfree[i % 2] = (t,)
                t = V((t, t_yr, (s_wf, 16), *ptfree[i % 2]), v.tensor_copy, pt[:, 0:384], bk[b][:, 0:384])
                bfree[b] = (t,)
                avst[("t", i)] = t

            def s3(h=h, i=i):
                pt = PTB[i % 2]
                t = P((avst[("t", i)], t_vd, *bfree[6]), pe.matmul, bk[6][:, 0:128], pt[:, 0:128],
                      VD[:, 0, h * 128:(h + 1) * 128], start=True, stop=True)
                P((), pe.matmul, bk[6][:, 128:256], pt[:, 128:256], VD[:, 0, h * 128:(h + 1) * 128], start=True, stop=False)
                t = P((), pe.matmul, bk[6][:, 128:256], pt[:, 256:384], VD[:, 1, h * 128:(h + 1) * 128], start=False,
                      stop=True)
                ptfree[i % 2] = (t,)
                t = A((t, t_yr), a.activation, O[:, :, h * 128:(h + 1) * 128], two(bk[6][:, 0:256]), ACT.Copy)
                bfree[6] = (t,)
                avst[("o", h)] = t
            units.append([s0, s1, s2, s3])
        for h in range(8):
            i = 4 + h

            def s0(h=h, i=i):
                b0 = i % 4
                c, hf = h // 2, h % 2
                w_ = (t_l, (s_l, 16), *bfree[b0])
                for lo, n, q0 in ((0, 128, 0), (128, 256, 128)):
                    P.quiet(w_, pe.matmul, bk[b0][:, lo:lo + n], QF[:, c, hf, q0:q0 + 128], KF[:, c, 0:n], start=True,
                            stop=False)
                    P.quiet((), pe.matmul, bk[b0][:, lo:lo + n], LH[:, h, 0:128], RH[:, 0, 0:n], start=False, stop=False)
                    t0 = P((), pe.matmul, bk[b0][:, lo:lo + n], QC[:, 0, q0:q0 + 128], LH[:, h, 0:n], start=False, stop=True)
                Sx, st = SD[i % 2], 4 * (i % 3)
                scores_row(bk[b0][:, 0:128], cmask[:, 128:256], Sx[:, 0:128], st, t0, sfree[i % 2])
                r = scores_row(bk[b0][:, 128:384], cmask[:, 0:256], Sx[:, 128:384], st + 1, t0, ())
                bfree[b0] = (r,)
                tn = V((r,), v.tensor_scalar, c_nm[:, st:st + 2], c_mx[:, st:st + 2], -1.0, None, ALU.mult)
                for q, (lo, hi) in enumerate(((0, 128), (128, 384))):
                    te = A((tn,), a.activation, Sx[:, lo:hi], Sx[:, lo:hi], ACT.Exp, bias=c_nm[:, st + q:st + q + 1],
                           accum_out=c_dn[:, st + q:st + q + 1])
                avst[("e", i)] = te

            def s1(h=h, i=i):
                Sx, st = SD[i % 2], 4 * (i % 3)
                t = V((avst[("e", i)],), v.reciprocal, c_rc[:, st:st + 2], c_dn[:, st:st + 2])
                for q, (lo, hi) in enumerate(((0, 128), (128, 384))):
                    tp = V((t,), v.tensor_scalar, Sx[:, lo:hi], Sx[:, lo:hi], c_rc[:, st + q:st + q + 1], None, ALU.mult)
                avst[("p", i)] = tp

            def s2(h=h, i=i):
                Sx, b, pt = SD[i % 2], 4 + i % 2, PTB[i % 2]
                for n in range(3):
                    t = P((avst[("p", i)], *bfree[b]), pe.transpose, bk[b][:, n * 128:(n + 1) * 128],
                          Sx[:, n * 128:(n + 1) * 128], ident[:, :])
                sfree[i % 2] = (t,)
                t = V((t, *ptfree[i % 2]), v.tensor_copy, pt[:, 0:384], bk[b][:, 0:384])
                bfree[b] = (t,)
                avst[("t", i)] = t

            def s3(h=h, i=i):
                pt, p0 = PTB[i % 2], 64 * (h % 2)
                w_ = bfree[6] if h % 2 == 0 else ()
                o = bk[6][p0:p0 + 64, :]
                P.quiet((avst[("t", i)], t_vf, *w_), pe.matmul, o[:, 0:256], VF[:, 0, h * 64:(h + 1) * 64], pt[:, 0:256],
                        start=True, stop=False)
                t = P((), pe.matmul, o[:, 128:256], VF[:, 1, h * 64:(h + 1) * 64], pt[:, 256:384], start=False, stop=True)
                ptfree[i % 2] = (t,)
                if h % 2:
                    t = split_out(t, (YF.h[:, h // 2, :], YF.l[:, h // 2, :], YF.hf[:, h // 2, :]), bk[6][:, 0:256])
                    bfree[6] = (t,)
                    avst["yf"] = t
            units.append([s0, s1, s2, s3])
        run_pipeline(units, gate_fill(12, GT, c_hb[:, 16:40], 7, free=(t_hb,)))
        t_gt = (A.sem, A.n)

        O8 = O.rearrange("p b (h d) -> p (b h) d", d=128)
        SQ = pg(140, 8, 128)
        t = V((avst[("o", 3)], (P.sem, P.n)), v.tensor_tensor, SQ, O8, O8, ALU.mult)
        t = V((t,), v.reduce_sum, c_ss, SQ, axis=AX)
        t = V((t,), v.tensor_scalar, c_ss, c_ss, 1.0 / 128, 1e-6, ALU.mult, ALU.add)
        t = A((t,), a.activation, c_ss, c_ss, ACT.Sqrt)
        t = V((t,), v.reciprocal, c_rs, c_ss)
        t = V((t,), v.tensor_tensor, O8, O8, c_rs.rearrange("p (n a) -> p n a", a=1).to_broadcast([128, 8, 128]), ALU.mult)
        for pr in range(2):
            for h in range(2):
                for tb in range(2):
                    tt = P((t, *bfree[pr]), pe.transpose, bk[pr][:, h * 256 + tb * 128:h * 256 + tb * 128 + 128],
                           O[:, tb, (2 * pr + h) * 128:(2 * pr + h + 1) * 128], ident[:, :])
            q = slice(2 * pr, 2 * pr + 2)
            t_yd = split_out(tt, (YD.h[:, q, :], YD.l[:, q, :], YD.hf[:, q, :]), two(bk[pr][:, :]), c_sub)
            bfree[pr] = (t_yd,)

        def merge(M, TMP, GTs, branches, mfree):
            tm, tl = {}, {}
            cnt = 0
            for bi, (npieces, k_per, rhs, toks) in enumerate(branches):
                for n in range(0, 8, 2):
                    b = nextbank(0, 4)
                    t = pair(b, npieces, k_per, rhs, toks)
                    gate, ps, m = GTs[:, bi * 8 + n:bi * 8 + n + 2, :], two(bk[b][:, :]), M.raw[:, n:n + 2, :]
                    if bi == 0:
                        r = tm[n] = V((t, t_gt, *mfree), v.scalar_tensor_tensor, m, gate, 1.0, ps, ALU.add, ALU.mult)
                    else:
                        x = TMP[:, 2 * (cnt % 2):2 * (cnt % 2) + 2, :]
                        cnt += 1
                        r = V((t, *mfree), v.scalar_tensor_tensor, x, gate, 1.0, ps, ALU.add, ALU.mult)
                        tm[n] = V((r, tm[n]), v.tensor_tensor, m, m, x, ALU.add)
                    bfree[b] = (r,)
                    if bi == len(branches) - 1:
                        tl[n] = split_out(tm[n], (M.h[:, n:n + 2, :], M.l[:, n:n + 2, :], M.hf[:, n:n + 2, :]), m)
            return tl

        M1, TMP = Two(120, 128, 8), pg(136, 4)
        tm = merge(M1, TMP, GT, [(2, 4, YR, (t_yr,)), (1, 4, YD, (t_yd,)), (1, 4, YF, (avst["yf"],))],
                   ((P.sem, P.n),))

        def project_out(M, tm, X):
            for i in range(2):
                for j in range(4):
                    wh, wl, tw = sp.take()
                    for tb in range(2):
                        b = 4 + 2 * i + tb
                        q = slice(tb * 128, (tb + 1) * 128)
                        for k in range(2):
                            kk = 2 * j + k
                            t = mm3(P if k == 1 else P.quiet, bk[b][:, :], M.h[:, kk, q], M.l[:, kk, q], wh[:, k, :],
                                    wl[:, k, :], start=(kk == 0), stop=(kk == 7), after=(*tw, tm[2 * j], *bfree[b]))
                    sp.done(t)
                for tb in range(2):
                    b = 4 + 2 * i + tb
                    xs = X[:, tb, i * 512:(i + 1) * 512]
                    r = V((t,), v.scalar_tensor_tensor, xs, bk[b][:, :], 0.5, xs, ALU.mult, ALU.add)
                    bfree[b] = (r,)
            return r

        t_x1 = project_out(M1, tm, X)

        s_fg = sem("s_fg")
        slots[2].free = ((P.sem, P.n),)
        stream.open(slots[2], slots[2].free)
        FG = pg(168, 1, 1024)[:, 0, :]
        A.dma(((P.sem, P.n), (V.sem, V.n)), s_fg, FG, I["final_g"].rearrange("(a n) -> a n", a=1).to_broadcast([128, 1024]))
        _, tHT = norm_T(t_x1, "g2", pg(160, 2, 1024), HT, ((P.sem, P.n),))
        AT = Two(96, 118, 22)
        t_ = ((P.sem, P.n), (V.sem, V.n), (A.sem, A.n))
        for p_ in (172, 180, 188):
            sp.idle.append(([pr_(p_ + o, 4).rearrange("p n c -> p (n c)") for o in (0, 4)], t_))
        UU = [pg(140 + 4 * i, 4) for i in range(4)]
        ufree = [()] * 4
        tA = {}
        for i in range(11):
            q = i % 4
            U = UU[q]
            for kind in range(2):
                b = nextbank(0, 4)
                t = pair(b, 2, 4, HT, tHT)
                for h in range(2):
                    n = kind * 22 + 2 * i + h
                    r0 = A((t, *ufree[q]), a.activation, U[:, 2 * kind + h, :], bk[b][:, h * 256:(h + 1) * 256],
                           ACT.Identity, scale=par("fw", 88 + n), bias=par("fb", n))
                for h in range(2):
                    n = kind * 22 + 2 * i + h
                    ps, o = bk[b][:, h * 256:(h + 1) * 256], U[:, 2 * kind + h, :]
                    r = r0
                    for d in (1, 2):
                        r = V((r,), v.scalar_tensor_tensor, o[:, d:256], ps[:, 0:256 - d], par("fw", (2 - d) * 44 + n),
                              o[:, d:256], ALU.mult, ALU.add)
                bfree[b] = (r,)
                if kind == 0:
                    tg = A((r,), a.activation, U[:, 0:2, :], U[:, 0:2, :], ACT.Gelu_apprx_tanh)
            r = V((tg, r), v.tensor_tensor, U[:, 2:4, :], U[:, 0:2, :], U[:, 2:4, :], ALU.mult)
            x = slice(2 * i, 2 * i + 2)
            r = split_out(r, (AT.h[:, x, :], AT.l[:, x, :], AT.hf[:, x, :]), U[:, 2:4, :])
            ufree[q] = (r,)
            tA[2 * i] = tA[2 * i + 1] = r
        for kk in range(22):
            wh, wl, tw = sp.take()
            for tb in range(2):
                q = slice(tb * 128, (tb + 1) * 128)
                for hf in range(2):
                    b = 4 + 2 * tb + hf
                    c = slice(hf * 512, (hf + 1) * 512)
                    t = mm3(P, bk[b][:, :], AT.h[:, kk, q], AT.l[:, kk, q], wh[:, 0, c], wl[:, 0, c],
                            start=(kk == 0), stop=(kk == 21), after=(*tw, tA[kk], *(bfree[b] if kk == 0 else ())))
            sp.done(t)
        for tb in range(2):
            for hf in range(2):
                b = 4 + 2 * tb + hf
                xs = X[:, tb, hf * 512:(hf + 1) * 512]
                r = V((t,), v.tensor_tensor, xs, xs, bk[b][:, :], ALU.add)
                bfree[b] = (r,)

        def final_norm(t_in, FGt, t_fg, junk, free):
            t = rstd(t_in, X, junk, free)
            for b in range(2):
                r = V((t, t_fg), v.scalar_tensor_tensor, X[:, b, :], X[:, b, :], c_rs[:, 4 + b:5 + b], FGt, ALU.mult,
                      ALU.mult)
            return r
        t_x = final_norm(r, FG, (s_fg, 16), pg(160, 2, 1024), ((P.sem, P.n),))

        sp.idle = [(b_, ((P.sem, P.n),)) for b_ in wb]
        ex_at = [116, 132, 148, 165, 181, 96]
        extra_slots = [Slot(pg(p_, 1, KS)[:, 0, :], sem(f"s_e{i}"), True) for i, p_ in enumerate(ex_at)]
        s_rt, s_io, s_nf = sem("s_rt"), sem("s_io"), sem("s_nf")
        ex_toks = ()
        btiles = [pg(157, 5, 384)[:, i, :] for i in range(5)]
        s_bt = [sem(f"s_bt{i}") for i in range(5)]
        bcount = [0] * 5

        for l in range(2):
            for i_ in range(3):
                sp.add(f"qka{l}", i_, PAIRS)
            sp.add(f"va{l}", 0, TOKS)
            sp.add(f"vb{l}", 0, [v_flat(j, 4, 256) for j in range(2)])
            for i_ in range(2):
                sp.add(f"qw{l}", i_, PAIRS)
            sp.add(f"kvw{l}", 0, PAIRS)
            for i_ in range(4):
                sp.add(f"gate{l}", i_, PAIRS)
            sp.add(f"bra{l}", 0, [v_rows(pr, 2) for pr in range(4)])
            for i_ in range(2):
                sp.add(f"brb{l}", i_, PAIRS)
            for i_ in range(2):
                sp.add(f"wo{l}", i_, TOKS)
            XN = pg(165, 2, 1024)
            all_now = ((P.sem, P.n), (V.sem, V.n), (A.sem, A.n), (G.sem, G.n), *ex_toks)
            tzz = G(all_now, g.memset, pg(96, 28), 0.0)
            QA = pg(96, 12).rearrange("p (h c) n -> p h c n", c=2)
            QW = pg(108, 16).rearrange("p (h c) n -> p h c n", c=2)
            KA, KW = pg(124, 6), pg(130, 4)
            VA, VW = pg(134, 2, 768), pg(140, 2, 256)
            GL = pg(165, 16)
            OA, OB = Two(181, 183, 2), Two(185, 193, 8)
            SX = [pg(142 + 3 * i, 1, 768)[:, 0, :] for i in range(3)]
            PTL = [pg(151, 1, 768)[:, 0, :], pg(154, 1, 768)[:, 0, :]]
            ML, TMPL = Two(96, 104, 8), pg(112, 4)
            sfree = [(), (), ()]
            ptfree = [(), ()]
            bready, bnext = {}, [0]

            def load_bias(q, toks):
                if bnext[0] < 28:
                    bcount[q] += 16
                    G.dma(toks, s_bt[q], btiles[q], I["bias"][bnext[0]])
                    bready[bnext[0]] = (q, (s_bt[q], bcount[q]))
                    bnext[0] += 1
            for q in range(5):
                load_bias(q, all_now)

            def bias_win(n, qb):
                q, td = bready[n]
                return btiles[q][:, 0:256] if qb else btiles[q][:, 128:384], td

            _, tHT = norm_T(t_x, f"gm{l}", XN, HT, all_now)
            tz = tzz

            def qk_sink(i):
                def f(pr, b, t):
                    n = 4 * i + 2 * pr
                    if n < 6:
                        return halves(QA, n - 2 * pr)(pr, b, t)
                    return plain(KA, n - 6 - 2 * pr)(pr, b, t)
                return f
            for i in range(3):
                pair_T(range(2), HT, tHT, qk_sink(i), (0, 4))
            tokmajor(VA, 0, 512, (0, 4), 4, 2, free=all_now)
            tokmajor(VA, 512, 256, (0, 4), 2, 4)
            for i in range(2):
                pair_T(range(2), HT, (), halves(QW, 4 * i), (0, 4))

            def kw_sink(pr, b, t):
                for c in range(2):
                    for h in range(2):
                        for d in range(2):
                            r = A((t,), a.activation, KW[64 * d:64 * d + 64, 2 * c + h, :],
                                  bk[b][64 * h:64 * h + 64, c * 256:(c + 1) * 256], ACT.Copy)
                return (r,)
            pair_T(range(1), HT, (), kw_sink, (0, 4))
            t_v = tokmajor(VW, 0, 256, (0, 4), 2, 4)

            units = []
            for h in range(4):
                for qb in range(2):
                    i = 2 * h + qb

                    def s0(h=h, qb=qb, i=i, t_v=t_v):
                        b0 = 0 if i % 2 == 0 else 2
                        Sx, st = SX[i % 3], 4 * (i % 3)
                        r = None
                        for gi in range(3):
                            s = gi * 4 + h
                            bb, off = (b0, gi * 256) if gi < 2 else (b0 + 1, 0)
                            t0 = P((t_v, *bfree[b0], *bfree[b0 + 1]), pe.matmul, bk[bb][:, off:off + 256],
                                   QA[:, s // 2, s % 2, qb * 128:(qb + 1) * 128], KA[:, s // 2, :], start=True, stop=True)
                        for gi in range(3):
                            bb, off = (b0, gi * 256) if gi < 2 else (b0 + 1, 0)
                            bi, td = bias_win(3 * h + gi, qb)
                            r = V((t0, td, *sfree[i % 3]), v.tensor_tensor_reduce, out=Sx[:, gi * 256:(gi + 1) * 256],
                                  in0=bk[bb][:, off:off + 256], in1=bi, scale=0.125, scalar=-3.0e38,
                                  op0=ALU.add, op1=ALU.max, accum_out=c_mx[:, st + gi:st + gi + 1])
                        bfree[b0] = bfree[b0 + 1] = (r,)
                        if qb == 1:
                            for gi in range(3):
                                load_bias(bready[3 * h + gi][0], (r,))
                        r = V((r,), v.reduce_max, c_nm[:, st:st + 1], c_mx[:, st:st + 3], axis=AX, negate=True)
                        te = A((r,), a.activation, Sx[:, 0:768], Sx[:, 0:768], ACT.Exp, bias=c_nm[:, st:st + 1],
                               accum_out=c_dn[:, st:st + 1])
                        avst[("e", i)] = te

                    def s1(i=i):
                        Sx, st = SX[i % 3], 4 * (i % 3)
                        t = V((avst[("e", i)],), v.reciprocal, c_rc[:, st:st + 1], c_dn[:, st:st + 1])
                        avst[("p", i)] = V((t,), v.tensor_scalar, Sx[:, 0:768], Sx[:, 0:768], c_rc[:, st:st + 1], None,
                                           ALU.mult)

                    def s2(i=i):
                        Sx, pt = SX[i % 3], PTL[i % 2]
                        for n in range(6):
                            b = 4 + n // 4
                            t = P((avst[("p", i)], *bfree[4], *bfree[5]), pe.transpose,
                                  bk[b][:, (n % 4) * 128:(n % 4 + 1) * 128], Sx[:, n * 128:(n + 1) * 128], ident[:, :])
                        sfree[i % 3] = (t,)
                        t4 = A((t, *ptfree[i % 2]), a.activation, pt[:, 0:512], bk[4][:, :], ACT.Copy)
                        t5 = V((t, *ptfree[i % 2]), v.tensor_copy, pt[:, 512:768], bk[5][:, 0:256])
                        bfree[4], bfree[5] = (t4,), (t5,)
                        avst[("t", i)] = (t4, t5)

                    def s3(h=h, qb=qb, i=i):
                        pt, p0 = PTL[i % 2], 64 * (h % 2)
                        w_ = bfree[6] if i % 4 == 0 else ()
                        o = bk[6][p0:p0 + 64, qb * 128:(qb + 1) * 128]
                        for n in range(6):
                            s = (n // 2) * 4 + h
                            f = P.quiet if n < 5 else P
                            t = f((*avst[("t", i)], *w_), pe.matmul, o, VA[:, n % 2, s * 64:(s + 1) * 64],
                                  pt[:, n * 128:(n + 1) * 128], start=(n == 0), stop=(n == 5))
                        ptfree[i % 2] = (t,)
                        if i % 4 == 3:
                            t = split_out(t, (OA.h[:, h // 2, :], OA.l[:, h // 2, :], OA.hf[:, h // 2, :]), bk[6][:, 0:256])
                            bfree[6] = (t,)
                            avst["oa"] = t
                    units.append([s0, s1, s2, s3])
            for h in range(16):
                i = 8 + h

                def s0(h=h, i=i, l=l):
                    b0 = i % 4
                    Sx, st = SX[i % 3], 4 * (i % 3)
                    for qb in range(2):
                        t0 = P(bfree[b0], pe.matmul, bk[b0][:, qb * 256:(qb + 1) * 256],
                               QW[:, h // 2, h % 2, qb * 128:(qb + 1) * 128], KW[:, h // 4, :], start=True, stop=True)
                    for qb in range(2):
                        bi, td = bias_win(12 + h, qb)
                        r = V((t0, td, *sfree[i % 3]), v.tensor_tensor_reduce, out=Sx[:, qb * 256:(qb + 1) * 256],
                              in0=bk[b0][:, qb * 256:(qb + 1) * 256], in1=bi, scale=0.125, scalar=-3.0e38,
                              op0=ALU.add, op1=ALU.max, accum_out=c_mx[:, st + qb:st + qb + 1])
                    bfree[b0] = (r,)
                    load_bias(bready[12 + h][0], (r,))
                    sk = c_sink[:, 16 * l + h:16 * l + h + 1]
                    r = V((r,), v.tensor_scalar, c_nm[:, st:st + 2], c_mx[:, st:st + 2], sk, -1.0, ALU.max, ALU.mult)
                    for qb in range(2):
                        A((r,), a.activation, Sx[:, qb * 256:(qb + 1) * 256], Sx[:, qb * 256:(qb + 1) * 256], ACT.Exp,
                          bias=c_nm[:, st + qb:st + qb + 1], accum_out=c_dn[:, st + qb:st + qb + 1])
                    te = A((), a.activation, c_es[:, st:st + 2], c_nm[:, st:st + 2], ACT.Exp, bias=sk)
                    avst[("e", i)] = te

                def s1(i=i):
                    Sx, st = SX[i % 3], 4 * (i % 3)
                    t = V((avst[("e", i)],), v.tensor_tensor, c_dn[:, st:st + 2], c_dn[:, st:st + 2], c_es[:, st:st + 2],
                          ALU.add)
                    t = V((t,), v.reciprocal, c_rc[:, st:st + 2], c_dn[:, st:st + 2])
                    for qb in range(2):
                        tp = V((t,), v.tensor_scalar, Sx[:, qb * 256:(qb + 1) * 256], Sx[:, qb * 256:(qb + 1) * 256],
                               c_rc[:, st + qb:st + qb + 1], None, ALU.mult)
                    avst[("p", i)] = tp

                def s2(i=i):
                    Sx, b, pt = SX[i % 3], 4 + i % 2, PTL[i % 2]
                    for kb in range(2):
                        for qb in range(2):
                            t = P((avst[("p", i)], *bfree[b]), pe.transpose,
                                  bk[b][:, kb * 256 + qb * 128:kb * 256 + qb * 128 + 128],
                                  Sx[:, qb * 256 + kb * 128:qb * 256 + kb * 128 + 128], ident[:, :])
                    sfree[i % 3] = (t,)
                    t = A((t, *ptfree[i % 2]), a.activation, pt[:, 0:512], bk[b][:, :], ACT.Copy)
                    bfree[b] = (t,)
                    avst[("t", i)] = t

                def s3(h=h, i=i):
                    pt, p0 = PTL[i % 2], 64 * (h % 2)
                    w_ = bfree[6] if h % 2 == 0 else ()
                    hk = h // 4
                    for kb in range(2):
                        f = P.quiet if kb < 1 else P
                        t = f((avst[("t", i)], *w_), pe.matmul, bk[6][p0:p0 + 64, 0:256], VW[:, kb, hk * 64:(hk + 1) * 64],
                              pt[:, kb * 256:(kb + 1) * 256], start=(kb == 0), stop=(kb == 1))
                    ptfree[i % 2] = (t,)
                    if h % 2:
                        t = split_out(t, (OB.h[:, h // 2, :], OB.l[:, h // 2, :], OB.hf[:, h // 2, :]), bk[6][:, 0:256])
                        bfree[6] = (t,)
                        avst["ob"] = t
                units.append([s0, s1, s2, s3])

            def slow(gen, every):
                for _ in gen:
                    for _ in range(every):
                        yield

            run_pipeline(units, slow(gate_fill(8, GL, c_hg[:, 16 * l:16 * l + 16], 7), 3))
            t_gt = (A.sem, A.n)
            t_att = ((P.sem, P.n), (V.sem, V.n), (A.sem, A.n))
            for s_ in extra_slots[0:3]:
                stream.open(s_, t_att)
            tm = merge(ML, TMPL, GL, [(1, 2, OA, (avst["oa"],)), (2, 4, OB, (avst["ob"],))], t_att)
            t_mg = ((P.sem, P.n), (V.sem, V.n))
            for s_ in extra_slots[3:5]:
                stream.open(s_, t_mg)
            t_x1 = project_out(ML, tm, X)
            done = ((P.sem, P.n), (V.sem, V.n), (A.sem, A.n), (G.sem, G.n))

            XN, XH, XL = pg(96, 2, 1024), pr_(104, 2, 1024), pr_(96, 2, 1024)
            HTf = pg(8, 8)
            POr = pr_(40, 2, 512)
            XE = pg(24, 8, 512)
            PG = pg(44, 2, 512)
            GZ = [pg(16, 4), pg(20, 4)]
            RW = pg(112, 1)[:, 0, 0:128].rearrange("p (k n) -> p k n", k=8)
            IO = pg(112, 1)[:, 0, 128:160]
            LG = pg(112, 1)[:, 0, 160:192]
            AF, WK, MK, AF2 = (pg(p_, 1)[:, 0, :] for p_ in (113, 114, 115, 197))
            TA = pg(198, 1)[:, 0, :]
            YE = [pg(199, 1)[:, 0, :], pg(200, 1)[:, 0, :]]
            HA = [pg(113, 1)[:, 0, :], pg(114, 1)[:, 0, :]]
            A.dma(done, s_rt, RW, I["router"][l].rearrange("(k p) n -> p k n", p=128))
            A.dma(done, s_io, IO, I["iota"])
            tzg = G(done, g.memset, pg(16, 8), 0.0)
            tXN, tHT = norm_T(t_x1, f"gf{l}", XN, HTf, done)
            t_tr = (P.sem, P.n)
            for k in range(8):
                f = P.quiet if k < 7 else P
                t = f((tHT[k // 2], (s_rt, 16 * (l + 1)), *bfree[4]), pe.matmul, bk[4][0:16, 0:256], RW[:, k, :],
                      HTf[:, k, :], start=(k == 0), stop=(k == 7))
            t_xh = A((tXN, *done), a.activation, XH, XN, ACT.Copy)
            L2 = LG.rearrange("p (b n) -> p b n", b=2)
            t = V((t,), v.tensor_copy, AF[0:16, :], bk[4][0:16, 0:256])
            bfree[4] = (t,)
            for tb in range(2):
                t2 = P((t, *bfree[7]), pe.transpose, bk[7][:, tb * 16:(tb + 1) * 16], AF[0:16, tb * 128:(tb + 1) * 128],
                       ident[0:16, 0:16])
            t = V((t2,), v.tensor_copy, LG, bk[7][:, 0:32])
            bfree[7] = (t,)
            t = V((t,), v.reduce_max, c_nm[:, 0:2], L2, axis=AX, negate=True)
            for tb in range(2):
                te = A((t,), a.activation, L2[:, tb, :], L2[:, tb, :], ACT.Exp, bias=c_nm[:, tb:tb + 1],
                       accum_out=c_dn[:, tb:tb + 1])
            t = V((te,), v.reciprocal, c_rc[:, 0:2], c_dn[:, 0:2])
            for tb in range(2):
                t_lg = V((t,), v.tensor_scalar, L2[:, tb, :], L2[:, tb, :], c_rc[:, tb:tb + 1], None, ALU.mult)
            for tb in range(2):
                t = P((t_lg, *bfree[5]), pe.transpose, bk[5][0:16, tb * 128:(tb + 1) * 128], L2[:, tb, :], ident[:, :])
            af, wk, mk = AF[0:16, :], WK[0:16, :], MK[0:16, :]
            t_xl = V((t_xh, t_tr), v.tensor_tensor, XL, XN, XH.bitcast(F32), ALU.subtract)
            t = V((t,), v.tensor_copy, af, bk[5][0:16, 0:256])
            bfree[5] = (t,)
            src = af
            for r_ in range(4):
                t = V((t,), v.max, c_tmp[0:16, 8 * r_:8 * r_ + 8], src)
                t = V((t,), v.match_replace, wk, c_tmp[0:16, 8 * r_:8 * r_ + 8], src, -1.0)
                src = wk
            t = V((t,), v.tensor_scalar, mk, wk, 0.0, None, ALU.is_lt)
            t = V((t,), v.tensor_scalar, wk, wk, 0.0, 1.0, ALU.mult, ALU.add)
            t = V((t,), v.tensor_tensor_scan, AF2[0:16, :], wk, mk, 0.0, ALU.mult, ALU.add)
            t = V((t,), v.tensor_tensor, mk, mk, AF2[0:16, :], ALU.mult)
            for tb in range(2):
                tt = P((t, *bfree[6]), pe.transpose, bk[6][:, tb * 16:(tb + 1) * 16], mk[:, tb * 128:(tb + 1) * 128],
                       ident[0:16, 0:16])
            t = V((tt,), v.tensor_copy, c_tmp[:, 32:64], bk[6][:, 0:32])
            bfree[6] = (t,)
            iob = IO.rearrange("p (a t) -> p a t", a=1).to_broadcast([128, 16, 32])
            for tb in range(2):
                rk = c_tmp[:, 32 + 16 * tb:48 + 16 * tb].rearrange("p (e a) -> p e a", a=1).to_broadcast([128, 16, 32])
                por = POr[:, tb, :].rearrange("p (e t) -> p e t", t=32)
                t_po = V((t, (s_io, 16 * (l + 1))), v.tensor_tensor, por, rk, iob, ALU.is_equal)
            t_xe = []
            for c in range(8):
                b = nextbank(0, 4)
                cs = slice(c * 128, (c + 1) * 128)
                for tb in range(2):
                    P.quiet((t_po, t_xh, t_xl, *bfree[b]), pe.matmul, bk[b][:, :], XH[:, tb, cs], POr[:, tb, :],
                            start=(tb == 0), stop=False)
                    f = P.quiet if tb < 1 else P
                    t = f((), pe.matmul, bk[b][:, :], XL[:, tb, cs], POr[:, tb, :], start=False, stop=(tb == 1))
                r = A((t,), a.activation, XE[:, c, :], bk[b][:, :], ACT.Copy, scale=par(f"gf{l}", c)) if c % 2 else \
                    V((t,), v.tensor_scalar, XE[:, c, :], bk[b][:, :], par(f"gf{l}", c), None, ALU.mult)
                bfree[b] = (r,)
                t_xe.append(r)
            stream.open(extra_slots[5], ((P.sem, P.n),))
            for tb in range(2):
                po = POr[:, tb, :].bitcast(F32).rearrange("p (e t) -> p e t", t=32)
                gg = L2[:, tb, :].rearrange("p (e a) -> p e a", a=1).to_broadcast([128, 16, 32])
                t_pg = V((t_po,), v.tensor_tensor, PG[:, tb, :].rearrange("p (e t) -> p e t", t=32), po, gg, ALU.mult)
            yfree = [(), ()]
            gzf = [(), ()]
            haf = [(), ()]

            def expert_up(e, kind, bank):
                for i in range(2):
                    s, td = stream.get(f"{kind}{l}_{e}", i)
                    w = s.ap.rearrange("p (k n) -> p k n", k=4)
                    for k in range(4):
                        for j in range(4):
                            f = P if (k == 3 and j == 3) else P.quiet
                            t = f((td, t_xe[4 * i + k], *bfree[bank]), pe.matmul, bk[bank][32 * j:32 * j + 32, 0:256],
                                  XE[:, 4 * i + k, 32 * e:32 * e + 32], w[:, k, 256 * j:256 * j + 256],
                                  start=(i == 0 and k == 0), stop=(i == 1 and k == 3))
                    stream.done(s, t)
                return t

            def expert_in(e):
                tg = expert_up(e, "eg", 0)
                q = e % 2
                t1 = A((tg, (V.sem, V.n), *haf[q]), a.activation, TA, bk[0][:, 0:256], ACT.Tanh, scale=0.5)
                t2 = V((t1,), v.scalar_tensor_tensor, TA, TA, 1.0, bk[0][:, 0:256], ALU.add, ALU.mult)
                bfree[0] = (t2,)
                tu = expert_up(e, "eu", 1)
                t3 = V((tu, t2), v.scalar_tensor_tensor, TA, bk[1][:, 0:256], 0.5, TA, ALU.mult, ALU.mult)
                bfree[1] = (t3,)
                for c in range(2):
                    t = P((t3, *bfree[2]), pe.transpose, bk[2][:, c * 128:(c + 1) * 128], TA[:, c * 128:(c + 1) * 128],
                          ident[:, :])
                for tb in range(2):
                    tg = P((t_pg,), pe.transpose, bk[2][0:32, 256 + tb * 128:384 + tb * 128],
                           PG[:, tb, 32 * e:32 * e + 32], ident[:, :])
                r = A((tg, *haf[q]), a.activation, HA[q], bk[2][:, 0:256], ACT.Copy)
                for j in range(4):
                    r = A((tzg, *gzf[q]), a.activation, GZ[q][32 * j:32 * j + 32, j, :],
                          bk[2][0:32, 256:512], ACT.Copy)
                bfree[2] = (r,)
                return r

            def expert_out(e, th):
                q = e % 2
                for i in range(2):
                    s, td = stream.get(f"ed{l}_{e}", i)
                    w = s.ap.rearrange("p (k n) -> p k n", k=4)
                    for k in range(4):
                        kk = 4 * i + k
                        hh = HA[q][:, (kk % 2) * 128 + (kk // 2) * 32:(kk % 2) * 128 + (kk // 2) * 32 + 32]
                        for j in range(4):
                            f = P if (k == 3 and j == 3) else P.quiet
                            t = f((td, th, *bfree[3]), pe.matmul, bk[3][32 * j:32 * j + 32, 0:256], hh,
                                  w[:, k, 256 * j:256 * j + 256], start=(i == 0 and k == 0), stop=(i == 1 and k == 3))
                    stream.done(s, t)
                haf[q] = (t,)
                r = V((t, *yfree[q]), v.tensor_copy, YE[q], bk[3][:, 0:256])
                bfree[3] = (r,)
                for tb in range(2):
                    for j in range(4):
                        b = 4 + 2 * tb + j // 2
                        t = P((r, *(bfree[b] if e == 0 else ())), pe.matmul, bk[b][:, (j % 2) * 256:(j % 2) * 256 + 256],
                              GZ[q][:, j, tb * 128:(tb + 1) * 128], YE[q], start=(e == 0 and j % 2 == 0),
                              stop=(e == 15), skip_group_check=True)
                yfree[q] = gzf[q] = (t,)
                return t

            for e in range(16):
                th = expert_in(e)
                t = expert_out(e, th)
            for tb in range(2):
                for hf in range(2):
                    b = 4 + 2 * tb + hf
                    xs = X[:, tb, hf * 512:(hf + 1) * 512]
                    r = V((t,), v.tensor_tensor, xs, xs, bk[b][:, :], ALU.add)
                    bfree[b] = (r,)
            t_x = r
            toks, _ = stream.take_extras()
            ex_toks = tuple(toks)

        done = ((P.sem, P.n), (V.sem, V.n), (A.sem, A.n), *ex_toks)
        FG = pg(96, 1, 1024)[:, 0, :]
        A.dma(done, s_nf, FG, I["norm_final"].rearrange("(a n) -> a n", a=1).to_broadcast([128, 1024]))
        t = final_norm(t_x, FG, (s_nf, 16), pg(104, 2, 1024), done)
        s_o = sem("s_o")
        S.dma((t,), s_o, out.rearrange("(b p) d -> p b d", p=128), X)
        S.wait((s_o, 16), *t_r)

        block = ctx.enter_context(nc.Block())

        @block.sync
        def _(e):
            S.play()

        @block.scalar
        def _(e):
            A.play()

        @block.vector
        def _(e):
            V.play()

        @block.gpsimd
        def _(e):
            G.play()

        @block.tensor
        def _(e):
            P.play()


def bucket(n):
    if n < 16:
        return max(n, 0)
    return min(31, 16 + int(math.log(n / 16) / math.log(8.0) * 16))


def constants():
    p = np.arange(128)[:, None]
    j = np.arange(384)[None, :]
    d = p + 128 - j
    cmask = np.where(d >= 0, 0.0, 8 * BIG).astype(np.float32)
    bias = []
    for h in range(4):
        for gi in range(3):
            ok = (np.abs(d) <= 64) if gi == 0 else (d % (4 if gi == 1 else 16) == 0)
            bias.append(np.where(ok, -8.0 * np.float32(SLOPES_A[gi * 4 + h]) * np.abs(d), 8 * BIG))
    for h in range(16):
        bias.append(np.where(np.abs(d) <= 128, -8.0 * np.float32(SLOPES_W[h]) * np.abs(d), 8 * BIG))
    bias = np.stack(bias, 0).astype(np.float32)
    onehot = np.zeros((32, 512), np.float32)
    for u in range(512):
        onehot[bucket(255 - u), u] = 1.0
    sel = np.zeros((8, 8, 256), np.float32)
    for h in range(8):
        sel[h, h, :] = 1.0
    iota = np.tile(np.arange(1, 33, dtype=np.float32), (128, 1))
    return dict(ident=np.eye(128, dtype=np.float32), cmask=cmask, onehot=onehot, sel=sel, iota=iota), bias


def cols(w, c0, n):
    k = w.shape[0] // 128
    return w[:, c0:c0 + n].reshape(k, 128, n).transpose(1, 0, 2).reshape(128, k * n)


def rows(w, k0, nk):
    n = w.shape[1]
    return w[k0 * 128:(k0 + nk) * 128, :].reshape(nk, 128, n).transpose(1, 0, 2).reshape(128, nk * n)


def pack(I):
    w = I["w_in"][0]
    d = {}
    for i in range(2):
        d["xrnn", i] = cols(w, 512 * i, 512)
        d["grnn", i] = cols(w, 1024 + 512 * i, 512)
        d["brr", i] = cols(I["w_br_rnn"][0], 512 * i, 512)
        d["wout", i] = cols(I["w_out"][0], 512 * i, 512)
    for i, n in enumerate(("dq", "dk", "dv", "fq", "fk", "fv")):
        d[n, 0] = cols(w, 2048 + 512 * i, 512)
    for i in range(6):
        d["gates", i] = cols(w, 5128 + 512 * i, 512)
    d["brd", 0] = rows(I["w_br_diff"][0], 0, 4)
    d["brf", 0] = rows(I["w_br_fox"][0], 0, 4)
    up = I["ffn_up"][0]
    for i in range(11):
        d["up", i] = cols(np.concatenate([up[:, 256 * i:256 * i + 256], up[:, 2816 + 256 * i:3072 + 256 * i]], 1), 0, 512)
    for i in range(5):
        d["down", i] = rows(I["ffn_down"][0], 4 * i, 4)
    d["down5", 0] = rows(I["ffn_down"][0], 20, 2)
    for l in range(2):
        w = I["w_in_2"][l]
        for i in range(3):
            d[f"qka{l}", i] = cols(w, 512 * i, 512)
        d[f"va{l}", 0] = cols(w, 1536, 512)
        d[f"vb{l}", 0] = cols(w, 2048, 256)
        for i in range(2):
            d[f"qw{l}", i] = cols(w, 2304 + 512 * i, 512)
            d[f"brb{l}", i] = cols(I["w_branch_b_2"][l], 512 * i, 512)
            d[f"wo{l}", i] = cols(I["w_out_2"][l], 512 * i, 512)
        d[f"kvw{l}", 0] = cols(w, 3328, 512)
        for i in range(4):
            d[f"gate{l}", i] = cols(w, 3840 + 512 * i, 512)
        d[f"bra{l}", 0] = rows(I["w_branch_a_2"][l], 0, 2)
        for e in range(16):
            for i in range(2):
                d[f"eg{l}_{e}", i] = rows(I["w_expert_gate_2"][l, e], 4 * i, 4)
                d[f"eu{l}_{e}", i] = rows(I["w_expert_up_2"][l, e], 4 * i, 4)
                d[f"ed{l}_{e}", i] = rows(I["w_expert_down_2"][l, e], 4 * i, 4)
    sl = slab_list()
    out = np.zeros((len(sl), 128, KS), np.float32)
    for n, (name, i, c, _) in enumerate(sl):
        out[n, :, 0:c] = d[name, i]
    return out


def pack_params(I):
    def c(a):
        return np.asarray(a).reshape(-1, 128).T
    out = np.zeros((128, NPV), np.float32)
    for name, arr in (("g1", I["norm1_g"]), ("cw", I["rnn_conv_w"]), ("cb", I["rnn_conv_b"]), ("br", I["rg_b_r"]),
                      ("bi", I["rg_b_i"]), ("ra", I["rg_a"]), ("sub", I["diff_subln_g"]), ("gb", I["gate_b"]),
                      ("g2", I["norm2_g"]), ("fw", I["ffn_conv_w"]), ("fb", I["ffn_conv_b"]),
                      ("gm0", I["norm_mix_2"][0]), ("gm1", I["norm_mix_2"][1]), ("bg0", I["b_gate_2"][0]),
                      ("bg1", I["b_gate_2"][1]), ("gf0", I["norm_ffn_2"][0]), ("gf1", I["norm_ffn_2"][1])):
        at, n = PV[name]
        out[:, at:at + n] = c(arr)
    return out


def kernel(**inputs):
    import concourse.bacc as bacc
    from concourse.bass_utils import run_bass_kernel_spmd

    I = {k: np.asarray(x) for k, x in inputs.items()}
    consts, bias = constants()
    arrays = dict(consts)
    arrays["x"] = np.ascontiguousarray(I["x"][0])
    arrays["pv"] = pack_params(I)
    rg = np.concatenate([I["rg_w_r"][0], I["rg_w_i"][0]], 0)
    arrays["rg"] = rg.transpose(1, 0, 2).reshape(128, 2048)
    arrays["slabs"] = pack(I)
    arrays["bias"] = bias
    arrays["wf"] = np.ascontiguousarray(I["w_in"][0][:, 5120:5128])
    arrays["router"] = I["w_router_2"]
    arrays["rel"] = I["rel_bias"]
    arrays["fb"] = I["fox_b_f"][0]
    arrays["sink"] = I["sink_logit_2"].reshape(32)
    arrays["lq"] = np.concatenate([I[n][0] for n in ("diff_lq1", "diff_lk1", "diff_lq2", "diff_lk2")])
    arrays["final_g"] = I["final_g"]
    arrays["norm_final"] = I["norm_final_2"]
    arrays = {f"in_{k}": np.ascontiguousarray(x) for k, x in arrays.items()}
    nc = bacc.Bacc("TRN2", target_bir_lowering=False, num_devices=1)
    aps = {k[3:]: nc.dram_tensor(k, x.shape, F32, kind="ExternalInput").ap() for k, x in arrays.items()}
    out = nc.dram_tensor("out", [256, 1024], F32, kind="ExternalOutput").ap()
    build(nc, aps, out)
    r = run_bass_kernel_spmd(nc, [arrays], core_ids=[0])
    return r.results[0]["out"].reshape(1, 256, 1024)
```

```python
import math
import numpy as np
import concourse.bass as bass
from concourse import mybir

F32 = mybir.dt.float32
F32R = mybir.dt.float32r
ACT = mybir.ActivationFunctionType
ALU = mybir.AluOpType
AX = mybir.AxisListType.X

KS, CS = 4096, 256
BIG = -1.0e30
SLOPES_A = [float(np.float32(2.0) ** np.float32(-8.0 * i / 12)) for i in range(1, 13)]
SLOPES_W = [float(np.float32(2.0) ** np.float32(-8.0 * i / 16)) for i in range(1, 17)]



def slab_list():
    s = []

    def add(name, n, cols=KS, extra=False):
        for i in range(n):
            s.append((name, i, cols, extra))
    add("xrnn", 2)
    add("grnn", 2)
    add("dq", 1)
    add("dk", 1)
    add("dv", 1)
    add("fv", 1)
    add("fq", 1)
    add("fk", 1)
    add("gates", 6)
    add("brr", 2)
    add("brd", 1)
    add("brf", 1)
    add("wout", 2)
    add("up", 11)
    add("down", 5)
    add("down5", 1, 2048)
    for l in range(2):
        add(f"qka{l}", 3)
        add(f"va{l}", 1)
        add(f"vb{l}", 1, 2048)
        add(f"qw{l}", 2)
        add(f"kvw{l}", 1)
        add(f"gate{l}", 4)
        add(f"bra{l}", 1, 2048)
        add(f"brb{l}", 2)
        add(f"wo{l}", 2)
        for e in range(16):
            add(f"eg{l}_{e}", 2, KS, True)
            add(f"eu{l}_{e}", 2, KS, True)
            add(f"ed{l}_{e}", 2, KS, True)
    return s


PV = {}
_at = 0
for _n, _w in [("g1", 8), ("cw", 32), ("cb", 8), ("br", 8), ("bi", 8), ("ra", 8), ("sub", 1), ("gb", 24),
               ("g2", 8), ("fw", 132), ("fb", 44), ("gm0", 8), ("gm1", 8), ("bg0", 16), ("bg1", 16),
               ("gf0", 8), ("gf1", 8)]:
    PV[_n] = (_at, _w)
    _at += _w
NPV = _at


class Queue:

    def __init__(self, eng, sem):
        self.eng, self.sem, self.n, self.items, self.seen = eng, sem, 0, [], {}

    def wait(self, *toks):
        for sem, v in toks:
            if self.seen.get(sem.name, 0) < v:
                self.seen[sem.name] = v
                self.items.append((self.eng.wait_ge, (sem, v), {}, None, 0))

    def __call__(self, after, fn, *a, **k):
        self.wait(*after)
        self.n += 1
        self.items.append((fn, a, k, self.sem, 1))
        return (self.sem, self.n)

    def quiet(self, after, fn, *a, **k):
        self.wait(*after)
        self.items.append((fn, a, k, None, 0))

    def dma(self, after, sem, out, in_):
        self.wait(*after)
        self.items.append((self.eng.dma_start, (out, in_), {}, sem, 16))

    def play(self):
        for fn, a, k, sem, by in self.items:
            i = fn(*a, **k)
            if sem is not None:
                i.then_inc(sem, by)


class Slot:
    def __init__(self, ap, sem, extra):
        self.ap, self.sem, self.extra, self.count, self.free = ap, sem, extra, 0, ()


class Stream:

    def __init__(self, sp, slabs, dram):
        self.sp, self.slabs, self.dram, self.next = sp, slabs, dram, 0
        self.ready, self.idle = {}, []

    def open(self, slot, free=()):
        slot.free = free
        self.idle.append(slot)
        self.fill()

    def fill(self):
        while self.next < len(self.slabs):
            name, i, cols, extra = self.slabs[self.next]
            pick = [s for s in self.idle if extra or not s.extra]
            if not pick:
                return
            s = pick[0]
            self.idle.remove(s)
            s.count += 16
            self.sp.dma(s.free, s.sem, s.ap[:, 0:cols], self.dram[self.next, :, 0:cols])
            self.ready[(name, i)] = (s, (s.sem, s.count))
            self.next += 1

    def get(self, name, i=0):
        return self.ready[(name, i)]

    def done(self, slot, *toks):
        self.open(slot, toks)

    def take_extras(self):
        out = [s for s in self.idle if s.extra]
        self.idle = [s for s in self.idle if not s.extra]
        return [t for s in out for t in s.free], out


class Splitter:

    def __init__(self, hi_eng, lo_eng, stream, bufs):
        self.A, self.V, self.stream = hi_eng, lo_eng, stream
        self.plan, self.made, self.used, self.ready = [], 0, 0, {}
        self.idle = [(b, ()) for b in bufs]
        self.out, self.extra, self.gone = [], [], []
        self.back = iter(())

    def lend(self, bufs, free):
        self.extra = bufs
        self.idle += [(b, free) for b in bufs]

    def drop(self):
        self.idle = [i for i in self.idle if not any(i[0] is b for b in self.extra)]
        self.gone, self.extra = self.extra, []

    def add(self, name, i, views):
        for n, view in enumerate(views):
            self.plan.append((name, i, view, n == len(views) - 1))

    def make(self):
        name, i, view, last = self.plan[self.made]
        slot, td = self.stream.get(name, i)
        buf, free = self.idle.pop(0)
        src = view(slot.ap)
        a, b = src.shape[1], src.shape[2]
        hi, lo = (x[:, 0:a * b].rearrange("p (a b) -> p a b", a=a) for x in buf)
        th = self.A((td, *free), self.A.eng.activation, hi, src, ACT.Copy)
        tl = self.V((th,), self.V.eng.tensor_tensor, lo, src, hi.bitcast(F32), ALU.subtract)
        if last:
            self.stream.done(slot, tl)
        self.ready[self.made] = (hi, lo, (th, tl), buf)
        self.made += 1

    def fill(self):
        while self.idle and self.made < len(self.plan) and (self.plan[self.made][0:2] in self.stream.ready):
            self.make()

    def take(self):
        next(self.back, None)
        self.fill()
        self.used += 1
        hi, lo, toks, self.out = self.ready.pop(self.used - 1)
        return hi, lo, toks

    def done(self, tok):
        if not any(self.out is b for b in self.gone):
            self.idle.append((self.out, (tok,)))


def v_cols(pr, kh):
    return lambda ap: ap.rearrange("p (k n) -> p k n", k=8)[:, 4 * kh:4 * kh + 4, 256 * pr:256 * pr + 256]


def v_flat(j, a, b):
    return lambda ap: ap[:, j * a * b:(j + 1) * a * b].rearrange("p (a b) -> p a b", a=a)


def v_rows(pr, nk):
    return lambda ap: ap[:, 0:nk * 1024].rearrange("p (k n) -> p k n", k=nk)[:, :, 256 * pr:256 * pr + 256]


PAIRS = [v_cols(pr, kh) for pr in range(2) for kh in range(2)]
TOKS = [v_flat(j, 2, 512) for j in range(4)]


def build(nc, I, out):
    slabs = slab_list()
    from contextlib import ExitStack
    ctx = ExitStack()
    with ctx:
        def sem(name):
            return ctx.enter_context(nc.semaphore(name))

        P = Queue(nc.tensor, sem("s_pe"))
        V = Queue(nc.vector, sem("s_dve"))
        A = Queue(nc.scalar, sem("s_act"))
        G = Queue(nc.gpsimd, sem("s_pool"))
        S = Queue(nc.sync, sem("s_sp"))
        v, a, g, pe = nc.vector, nc.scalar, nc.gpsimd, nc.tensor

        A0, CUTS = 22528, (0, 24, 48, 96, 148, 201)

        def at(name, cols, offset, dt=F32):
            return nc.alloc_sbuf_tensor_at(name, [128, cols], dt, offset=offset)
        ident, pv = at("ident", 128, 16512), at("pv", NPV, 17024)
        sm, cmask = at("sm", 640, 18432), at("cmask", 384, 20992)
        arena = {dt: [at(f"{n_}{lo}", (hi - lo) * 256, A0 + lo * 1024, dt) for lo, hi in zip(CUTS, CUTS[1:])]
                 for n_, dt in (("pages", F32), ("pages_r", F32R))}

        def pages(dt, first, n, cols):
            i = max(j for j, lo in enumerate(CUTS) if lo <= first)
            c = (first - CUTS[i]) * 256
            return arena[dt][i][:, c:c + n * cols].rearrange("p (n c) -> p n c", n=n)
        bk = [ctx.enter_context(nc.psum_tensor(f"bank{i}", [128, 512], F32)) for i in range(8)]
        bfree = [()] * 8
        scr = nc.dram_tensor("scratch", [4, 128 * 512], F32, kind="Internal").ap()

        def pg(at, n, cols=256):
            return pages(F32, at, n, cols)

        def pr_(at, n, cols=256):
            return pages(F32R, at, n, cols)

        class Two:

            def __init__(self, hi, lo, n, cols=256):
                self.h, self.l, self.raw = pr_(hi, n, cols), pr_(lo, n, cols), pg(lo, n, cols)
                self.hf, self.lf = self.h.bitcast(F32), self.l.bitcast(F32)

        def par(name, i=0, n=1):
            return pv[:, PV[name][0] + i:PV[name][0] + i + n]

        s_x, s_c, s_id, s_m = sem("s_x"), sem("s_c"), sem("s_id"), sem("s_m")
        stream = Stream(S, slabs, I["slabs"])

        X = pg(0, 2, 1024)
        HT = Two(8, 16, 8)

        def wbuf(p_):
            return [pr_(p_ + o, 4).rearrange("p n c -> p (n c)") for o in (0, 4)]
        wb = [wbuf(24 + 8 * i) for i in range(3)]
        ringp = [48, 64, 80]
        S.dma((), s_x, X, I["x"].rearrange("(b p) d -> p b d", p=128))
        t_x = (s_x, 16)
        S.dma((), s_id, ident[:, :], I["ident"])
        S.dma((), s_id, pv[:, :], I["pv"])
        t_c = (s_id, 32)
        slots = [Slot(pg(ringp[i], 1, KS)[:, 0, :], sem(f"s_w{i}"), False) for i in range(3)]
        for s_ in slots[0:2]:
            stream.open(s_)
        sp = Splitter(A, V, stream, wb)
        sp.lend([wbuf(96), wbuf(104), wbuf(112)], ())
        A.dma((), s_m, cmask[:, :], I["cmask"])

        c_ss, c_rs = sm[:, 0:8], sm[:, 8:16]
        c_sp4, c_t1, c_t2, c_t3 = sm[:, 16:24], sm[:, 24:32], sm[:, 32:40], sm[:, 40:48]
        c_lam, c_sub = sm[:, 48:52], sm[:, 52:53]
        c_hb = sm[:, 56:96]
        c_hg = sm[:, 96:128]
        c_mx, c_nm, c_dn, c_rc = sm[:, 128:140], sm[:, 140:152], sm[:, 152:164], sm[:, 164:176]
        c_lq = sm[:, 192:448]
        c_sink = sm[:, 448:480]
        c_fb = sm[:, 480:481]
        c_rel = sm[:, 484:488]
        c_es = sm[:, 488:500]
        c_wm = sm[:, 500:501]
        c_tmp = sm[:, 512:640]

        A.dma((), s_c, c_lq, I["lq"].rearrange("(a n) -> a n", a=1).to_broadcast([128, 256]))
        A.dma((), s_c, c_sink, I["sink"].rearrange("(a n) -> a n", a=1).to_broadcast([128, 32]))
        A.dma((), s_c, c_fb[0:8, :], I["fb"].rearrange("(n a) -> n a", a=1))
        A.dma((), s_c, c_rel[0:32, :], I["rel"])
        t_s = (s_c, 64)

        def split_out(t, dst, src, scale=None, free=()):
            d_h, d_l, d_hf = dst
            if scale is None:
                th = A((t, *free), a.activation, d_h, src, ACT.Copy)
                return V((th,), v.tensor_tensor, d_l, src, d_hf, ALU.subtract)
            th = A((t, t_c, *free), a.activation, d_h, src, ACT.Copy, scale=scale)
            return V((th,), v.scalar_tensor_tensor, d_l, src, scale, d_hf, ALU.mult, ALU.subtract)

        def keep(toks, b, n):
            for t in toks:
                for _ in range(n):
                    P.quiet((t, t_c, *bfree[b]), pe.matmul, bk[b][:, 0:128], ident[:, :], ident[:, :], start=True, stop=True)

        t_warm = [()]

        def warm(fn):
            t_warm[0] = (A(t_warm[0], a.activation, c_wm[:, 0:1], ident[:, 0:1], fn),)

        def rstd(t_in, src, junk, free=()):
            t_warm[0] += (t_c,)
            warm(ACT.Sqrt)
            t = A((t_in[0], *free), a.activation, junk[:, 0, :], src[:, 0, :], ACT.Square, accum_out=c_ss[:, 0:1])
            t1 = V((t_in[1], *free), v.tensor_tensor_reduce, out=junk[:, 1, :], in0=src[:, 1, :], in1=src[:, 1, :],
                   scale=1.0, scalar=0.0, op0=ALU.mult, op1=ALU.add, accum_out=c_ss[:, 1:2])
            keep((*t_in, t), 7, 2)
            t = V((t, t1), v.tensor_scalar, c_rs[:, 0:2], c_ss[:, 0:2], 1.0 / 1024, 1e-6, ALU.mult, ALU.add)
            t = A((t,), a.activation, c_rs[:, 2:4], c_rs[:, 0:2], ACT.Sqrt)
            t = V((t,), v.reciprocal, c_rs[:, 4:6], c_rs[:, 2:4])
            keep((t,), 7, 2)
            return t

        def norm_T(t_in, gname, XN, HT, free=()):
            t = rstd(t_in, X, XN, free)
            tns = (A((t,), a.activation, XN[:, 0, :], X[:, 0, :], ACT.Copy, scale=c_rs[:, 4:5]),
                   V((t,), v.tensor_scalar, XN[:, 1, :], X[:, 1, :], c_rs[:, 5:6], None, ALU.mult))
            th = []
            for pr in range(4):
                b = pr
                for h in range(2):
                    for tb in range(2):
                        c = 2 * pr + h
                        tt = P((tns[tb], t_c, *bfree[b]), pe.transpose,
                               bk[b][:, h * 256 + tb * 128:h * 256 + tb * 128 + 128],
                               XN[:, tb, c * 128:(c + 1) * 128], ident[:, :])
                cs = [(2 * pr + h, bk[b][:, h * 256:(h + 1) * 256]) for h in range(2)]
                if isinstance(HT, Two):
                    for c, ps in cs:
                        te = A((tt, t_c), a.activation, HT.h[:, c, :], ps, ACT.Copy, scale=par(gname, c))
                    for c, ps in cs:
                        te = V((te,), v.scalar_tensor_tensor, HT.l[:, c, :], ps, par(gname, c), HT.hf[:, c, :],
                               ALU.mult, ALU.subtract)
                else:
                    for c, ps in cs:
                        if pr % 2:
                            te = A((tt, t_c), a.activation, HT[:, c, :], ps, ACT.Copy, scale=par(gname, c))
                        else:
                            te = V((tt, t_c), v.tensor_scalar, HT[:, c, :], ps, par(gname, c), None, ALU.mult)
                bfree[b] = (te,)
                th.append(te)
            return tns, th

        def mm3(q, out_, wh, wl, xh, xl, start, stop, after=()):
            P.quiet(after, pe.matmul, out_, wh, xh, start=start, stop=False, skip_group_check=True)
            P.quiet((), pe.matmul, out_, wh, xl, start=False, stop=False, skip_group_check=True)
            return q((), pe.matmul, out_, wl, xh, start=False, stop=stop, skip_group_check=True)

        rot = [0]

        def nextbank(lo, hi):
            rot[0] += 1
            return lo + rot[0] % (hi - lo)

        def piece(b, j, npieces, k_per, X2, tin=()):
            if isinstance(tin, list):
                tin = tin[0:(j + 1) * k_per // 2]
            wh, wl, tw = sp.take()
            for c in range(2):
                for k in range(k_per):
                    end = c == 1 and k == k_per - 1
                    t = mm3(P if end else P.quiet, bk[b][:, c * 256:(c + 1) * 256], wh[:, k, c * 128:(c + 1) * 128],
                            wl[:, k, c * 128:(c + 1) * 128], X2.h[:, j * k_per + k, :], X2.l[:, j * k_per + k, :],
                            start=(j == 0 and k == 0 and c == 0), stop=(j == npieces - 1 and end),
                            after=(*tw, *tin, *bfree[b]))
            sp.done(t)
            return t

        def pair(b, npieces, k_per, X2, tin=()):
            for j in range(npieces):
                t = piece(b, j, npieces, k_per, X2, tin)
            return t

        def pair_T(prs, rhs, tin, sink, banks):
            for pr in prs:
                b = nextbank(*banks)
                t = pair(b, 2, 4, rhs, tin)
                bfree[b] = sink(pr, b, t)

        def two(ap):
            return ap.rearrange("p (n c) -> p n c", n=2)

        for n_, i_ in (("xrnn", 0), ("xrnn", 1), ("grnn", 0), ("grnn", 1), ("dq", 0), ("dk", 0)):
            sp.add(n_, i_, PAIRS)
        sp.add("dv", 0, TOKS)
        sp.add("fv", 0, TOKS)
        sp.add("fq", 0, PAIRS)
        sp.add("fk", 0, PAIRS)
        for i_ in range(6):
            sp.add("gates", i_, PAIRS)
        for i_ in range(2):
            sp.add("brr", i_, PAIRS)
        sp.add("brd", 0, [v_rows(pr, 4) for pr in range(4)])
        sp.add("brf", 0, [v_rows(pr, 4) for pr in range(4)])
        for i_ in range(2):
            sp.add("wout", i_, TOKS)
        for i_ in range(11):
            sp.add("up", i_, PAIRS)
        for i_ in range(6):
            sp.add("down" if i_ < 5 else "down5", i_ if i_ < 5 else 0, [v_flat(j, 1, 1024) for j in range(4 if i_ < 5 else 2)])

        XN1 = pg(158, 2, 1024)
        _, tHT = norm_T((t_x, t_x), "g1", XN1, HT)

        GT = pg(96, 24)
        QD = pg(120, 8).rearrange("p (h c) n -> p h c n", c=2)
        KD, VD = pg(128, 4), pg(132, 2, 512)
        QF = pg(136, 8).rearrange("p (h c) n -> p h c n", c=2)
        KF, VF = pg(144, 4), pg(148, 2, 512)
        BT = pg(152, 4, 384)
        XC, GR, TR, TI, AA = pg(158, 8), pg(166, 8), pg(174, 8), pg(182, 8), pg(190, 8)
        YR = Two(166, 174, 8)
        YD, YF = Two(80, 84, 4), Two(88, 92, 4)
        O = pg(158, 2, 512)
        SD = [pg(198, 1, 768)[:, 0, :], pg(162, 1, 768)[:, 0, :], pg(80, 1, 768)[:, 0, :]]
        PTB = [pg(194, 1, 384)[:, 0, :], pg(196, 1, 384)[:, 0, :]]
        LH, RH = pg(182, 8), pg(190, 2)
        QC = pg(192, 2)
        OH = pg(198, 2)
        REL = pg(190, 4, 512)
        WF = pg(200, 1)[:, 0, 0:64].rearrange("p (k n) -> p k n", k=8)

        tz = G((), g.memset, QD, 0.0)
        tz = G((), g.memset, QF, 0.0)

        s_oh, s_wf, s_b, s_rg = sem("s_oh"), sem("s_wf"), sem("s_b"), sem("s_rg")
        RG = pg(80, 8).rearrange("p n c -> p (n c)").rearrange("p (k n) -> p k n", k=16)
        G.dma((), s_rg, pg(80, 8).rearrange("p n c -> p (n c)"), I["rg"])
        s_r = [sem(f"s_r{h}") for h in range(4)]
        t_r = tuple((q, 16) for q in s_r)
        A.dma((), s_oh, OH.rearrange("p n c -> p (n c)")[0:32, :], I["onehot"])
        A.dma((), s_wf, WF, I["wf"].rearrange("(k p) n -> p k n", p=128))
        small = {}

        def toeplitz():
            for h in range(4):
                b = 4 + h
                t = P((t_s, (s_oh, 16), *bfree[b]), pe.matmul, bk[b][:, :], c_rel[0:32, h:h + 1].to_broadcast([32, 128]),
                      OH.rearrange("p n c -> p (n c)")[0:32, :], start=True, stop=True)
                t = A((t,), a.activation, REL[:, h, :], bk[b][:, :], ACT.Copy)
                bfree[b] = (t,)
                G.dma((t,), s_r[h], scr[h].rearrange("(p n) -> p n", p=128), REL[:, h, :])
                yield
            skew = bass.AP(scr.tensor, 127, [[511, 128], [65536, 4], [1, 384]])
            G.dma(t_r, s_b, BT, skew)

        def params():
            tsl = V((t_s, t_c), v.tensor_scalar, c_hb[:, 0:16], par("br", 0, 16), 0.5, None, ALU.mult)
            V((), v.tensor_scalar, c_hb[:, 16:40], par("gb", 0, 24), 0.5, None, ALU.mult)
            V((), v.tensor_scalar, c_hg, par("bg0", 0, 32), 0.5, None, ALU.mult)
            small["hb"] = V((), v.tensor_scalar, c_sub, par("sub"), 0.8, None, ALU.mult)
            t = V((t_c,), v.scalar_tensor_tensor, c_t1, par("ra", 0, 8), -1.0, par("ra", 0, 8), ALU.mult, ALU.min)
            yield
            t = A((t,), a.activation, c_t1, c_t1, ACT.Exp)
            yield
            t = V((t,), v.tensor_scalar, c_t2, c_t1, 2.0, None, ALU.add)
            yield
            t = V((t,), v.reciprocal, c_t2, c_t2)
            yield
            t = V((t,), v.tensor_tensor, c_t1, c_t1, c_t2, ALU.mult)
            yield
            t = V((t,), v.tensor_tensor, c_t2, c_t1, c_t1, ALU.mult)
            yield
            t = V((t,), v.tensor_scalar, c_t3, c_t2, 1.0 / 17, 1.0 / 15, ALU.mult, ALU.add)
            yield
            for d in (13, 11, 9, 7, 5, 3, 1):
                t = V((t,), v.tensor_tensor, c_t3, c_t3, c_t2, ALU.mult)
                yield
                t = V((t,), v.tensor_scalar, c_t3, c_t3, 1.0 / d, None, ALU.add)
                yield
            t = V((t,), v.tensor_tensor, c_t3, c_t3, c_t1, ALU.mult)
            yield
            t = V((t,), v.tensor_scalar, c_t3, c_t3, 8.0, None, ALU.mult)
            yield
            t2 = V((t,), v.tensor_scalar, c_t1, par("ra", 0, 8), -4.0, 0.0, ALU.mult, ALU.max)
            small["sp"] = V((t2,), v.tensor_tensor, c_sp4, c_t3, c_t1, ALU.add)
            for i in range(2):
                t = V((t_s,), v.tensor_tensor, c_tmp[:, i * 64:(i + 1) * 64], c_lq[:, i * 128:i * 128 + 64],
                      c_lq[:, i * 128 + 64:i * 128 + 128], ALU.mult)
            t = V((t,), v.reduce_sum, c_lam[:, 0:2], two(c_tmp), axis=AX)
            yield
            t = A((t,), a.activation, c_lam[:, 0:2], c_lam[:, 0:2], ACT.Exp)
            yield
            t = V((t,), v.tensor_tensor, c_lam[:, 2:3], c_lam[:, 1:2], c_lam[:, 0:1], ALU.subtract)
            yield
            small["lam"] = V((t,), v.tensor_scalar, c_lam[:, 3:4], c_lam[:, 2:3], -0.2, None, ALU.add)

        last = {}

        def rnn():
            for n in range(8):
                for q in range(2):
                    b = 4 + n % 4
                    t = P(((s_rg, 16), tC[n], *bfree[b]), pe.matmul, bk[b][:, q * 256:(q + 1) * 256], RG[:, q * 8 + n, :],
                          XC[:, n, :], start=True, stop=True)
                A((t, small["hb"]), a.activation, TR[:, n, :], bk[b][:, 0:256], ACT.Tanh, bias=c_hb[:, n:n + 1], scale=0.5)
                r = A((), a.activation, TI[:, n, :], bk[b][:, 256:512], ACT.Tanh, bias=c_hb[:, 8 + n:9 + n], scale=0.5)
                bfree[b] = (r,)
                ty = V((r, small["sp"]), v.tensor_scalar, TR[:, n, :], TR[:, n, :], 1.0, c_sp4[:, n:n + 1], ALU.add, ALU.mult)
                if n % 2:
                    yield
            tr, tt = (V.sem, V.n), {}
            qs = [slice(2 * q, 2 * q + 2) for q in range(4)]
            for q in qs:
                te = A((tr, *t_r), a.activation, AA[:, q, :], TR[:, q, :], ACT.Exp, scale=-1.0)
                tt[q.start] = A((te,), a.activation, TR[:, q, :], TR[:, q, :], ACT.Tanh)
                yield
            for q in qs:
                t = V((tt[q.start],), v.scalar_tensor_tensor, TI[:, q, :], TI[:, q, :], 1.0, XC[:, q, :], ALU.add, ALU.mult)
                t = V((t,), v.tensor_scalar, XC[:, q, :], TR[:, q, :], 1.0, None, ALU.add)
                yield
                for n in (q.start, q.start + 1):
                    t = V((t,), v.reciprocal, XC[:, n, :], XC[:, n, :])
                    yield
                t = V((t,), v.tensor_tensor, TR[:, q, :], TR[:, q, :], XC[:, q, :], ALU.mult)
            for q in qs:
                tt[q.start] = A((t,), a.activation, TR[:, q, :], TR[:, q, :], ACT.Sqrt, scale=0.5)
            yield
            for q in qs:
                tt[q.start] = G((tt[q.start],), g.tensor_tensor, TI[:, q, :], TI[:, q, :], TR[:, q, :], ALU.mult)
            for q in qs:
                t = tt[q.start]
                for n in (q.start, q.start + 1):
                    ts = V((t,), v.tensor_tensor_scan, XC[:, n, :], AA[:, n, :], TI[:, n, :], 0.0, ALU.mult, ALU.add)
                yield
                t = (G if q.start % 4 else V)((ts, last["gr"]), (g if q.start % 4 else v).tensor_tensor, XC[:, q, :],
                                              GR[:, q, :], XC[:, q, :], ALU.mult)
                last["yr"] = split_out(t, (YR.h[:, q, :], YR.l[:, q, :], YR.hf[:, q, :]), XC[:, q, :])
                yield

        tC = [None] * 8

        def conv_rnn(i):
            def f(pr, b, t):
                for h in range(2):
                    n = 4 * i + 2 * pr + h
                    r0 = A((t, t_c), a.activation, XC[:, n, :], bk[b][:, h * 256:(h + 1) * 256], ACT.Identity,
                           scale=par("cw", 24 + n), bias=par("cb", n))
                for h in range(2):
                    n = 4 * i + 2 * pr + h
                    ps = bk[b][:, h * 256:(h + 1) * 256]
                    o = XC[:, n, :]
                    r = r0
                    for d in range(1, 4):
                        r = V((r,), v.scalar_tensor_tensor, o[:, d:256], ps[:, 0:256 - d],
                              par("cw", (3 - d) * 8 + n), o[:, d:256], ALU.mult, ALU.add)
                    tC[n] = r
                return (r,)
            return f
        def twice(gen, then, late):
            for _ in range(late):
                yield
            for _ in gen:
                next(gen, None)
                next(then, None)
                yield
            for _ in then:
                pass
        sp.back = twice(params(), toeplitz(), 1)
        for i in range(2):
            pair_T(range(2), HT, tHT, conv_rnn(i), (0, 4))

        for _ in sp.back:
            pass
        t_hb, t_sp, t_lam = small["hb"], small["sp"], small["lam"]
        sp.back = rnn()

        def gelu_g(i):
            def f(pr, b, t):
                n = 4 * i + 2 * pr
                r = A((t,), a.activation, GR[:, n:n + 2, :], two(bk[b][:, :]), ACT.Gelu_apprx_tanh)
                return (r,)
            return f
        for i in range(2):
            pair_T(range(2), HT, (), gelu_g(i), (0, 4))
        last["gr"] = (A.sem, A.n)

        def halves(dst, at=0, free=()):
            def f(pr, b, t):
                src = two(bk[b][:, :])
                for h in range(2):
                    p0 = 64 * h
                    r = A((t, tz, *free), a.activation, dst[p0:p0 + 64, at + 2 * pr:at + 2 * pr + 2, h, :],
                          src[p0:p0 + 64, :, :], ACT.Copy)
                return (r,)
            return f

        def plain(dst, at=0, eng=None, free=()):
            def f(pr, b, t):
                d, s_ = dst[:, at + 2 * pr:at + 2 * pr + 2, :], two(bk[b][:, :])
                if eng is V:
                    return (V((t, *free), v.tensor_copy, d, s_),)
                return (A((t, *free), a.activation, d, s_, ACT.Copy),)
            return f

        def tokmajor(dst, c0, nc_, banks, npieces, k_per, free=()):
            bs = (nextbank(*banks), nextbank(*banks))
            for j in range(npieces):
                wh, wl, tw = sp.take()
                for tb in range(2):
                    for k in range(k_per):
                        kk = j * k_per + k
                        end = tb == 1 and k == k_per - 1
                        q = slice(tb * 128, (tb + 1) * 128)
                        t = mm3(P if end else P.quiet, bk[bs[tb]][:, 0:nc_], HT.h[:, kk, q], HT.l[:, kk, q],
                                wh[:, k, :], wl[:, k, :], start=(kk == 0), stop=(kk == 7), after=(*tw, *bfree[bs[tb]]))
                sp.done(t)
            for tb in range(2):
                r = A((t, *free), a.activation, dst[:, tb, c0:c0 + nc_], bk[bs[tb]][:, 0:nc_], ACT.Copy)
                bfree[bs[tb]] = (r,)
            return r

        pair_T(range(2), HT, (), halves(QD), (0, 4))
        pair_T(range(2), HT, (), plain(KD), (0, 4))
        t_vd = tokmajor(VD, 0, 512, (0, 4), 4, 2)
        t_vf = tokmajor(VF, 0, 512, (0, 4), 4, 2)
        t_kd = (A.sem, A.n)

        for _ in sp.back:
            pass
        t_yr = last["yr"]
        sp.drop()

        b = 4
        for k in range(8):
            P.quiet(((s_wf, 16), *bfree[b]), pe.matmul, bk[b][0:8, 0:256], WF[:, k, :], HT.hf[:, k, :],
                    start=(k == 0), stop=False)
            f = P.quiet if k < 7 else P
            t_fl = f((), pe.matmul, bk[b][0:8, 0:256], WF[:, k, :], HT.lf[:, k, :], start=False, stop=(k == 7))
        s_l = sem("s_l")

        def forget():
            Z, Z2, lf, on = (pg(83 + i, 1)[0:8, 0, :] for i in range(4))
            t = V((t_fl, t_yr), v.tensor_scalar, Z, bk[4][0:8, 0:256], c_fb[0:8, :], None, ALU.add)
            bfree[4] = (t,)
            t = V((t,), v.scalar_tensor_tensor, Z2, Z, -1.0, Z, ALU.mult, ALU.min)
            t = A((t,), a.activation, Z2, Z2, ACT.Exp)
            t = A((t,), a.activation, Z2, Z2, ACT.Ln, bias=1.0)
            t = V((t,), v.tensor_scalar, Z, Z, 0.0, None, ALU.min)
            t = V((t,), v.tensor_tensor, Z, Z, Z2, ALU.subtract)
            V((), v.memset, on, 1.0)
            t = (V.sem, V.n)
            t = V((t,), v.tensor_tensor_scan, lf, on, Z, 0.0, ALU.mult, ALU.add)
            G((t_yr,), g.memset, LH, 0.0)
            tl = G((t_yr,), g.memset, pg(190, 4), 0.0)
            A.dma((tl,), s_l, LH[0:8, :, :], I["sel"])
            V((t, tl), v.tensor_scalar, RH[0:8, 0, :], lf, -8.0, None, ALU.mult)
            last["l"] = V((t, tl), v.tensor_scalar, QC[0:8, 0, :], lf, 8.0, None, ALU.mult)

        def pair_fill(prs, sink, bank):
            for pr in prs:
                piece(bank, 0, 2, 4, HT)
                yield
                t = piece(bank, 1, 2, 4, HT)
                bfree[bank] = sink(pr, bank, t)
                yield

        def tok_fill(dst, c0, key, bank, free=()):
            for j in range(2):
                wh, wl, tw = sp.take()
                for tb in range(2):
                    q = slice(tb * 128, (tb + 1) * 128)
                    for k in range(4):
                        kk = 4 * j + k
                        end = tb == 1 and k == 3
                        t = mm3(P if end else P.quiet, bk[bank][:, tb * 256:(tb + 1) * 256], HT.h[:, kk, q],
                                HT.l[:, kk, q], wh[:, k, :], wl[:, k, :], start=(kk == 0 and tb == 0),
                                stop=(j == 1 and end), after=(*tw, *bfree[bank]))
                sp.done(t)
                if j == 1:
                    avst[key] = A((t, *free), a.activation, dst[:, :, c0:c0 + 256], two(bk[bank][:, :]), ACT.Copy)
                    bfree[bank] = (avst[key],)
                yield

        def gate_fill(npairs, dst, hb, bank, free=()):
            for n in range(0, 2 * npairs, 2):
                t = piece(bank, 0, 2, 4, HT)
                yield
                t = piece(bank, 1, 2, 4, HT)
                for h in range(2):
                    r = A((t, *free), a.activation, dst[:, n + h, :], bk[bank][:, h * 256:(h + 1) * 256], ACT.Tanh,
                          bias=hb[:, n + h:n + h + 1], scale=0.5)
                bfree[bank] = (r,)
                yield

        def run_pipeline(units, filler, order, rate, lags=(0, 1, 2, 3)):
            filled = 0
            for step in range(len(units) + 3):
                for j in order:
                    if j == "f":
                        if filled < rate(step):
                            filled += 1
                            next(filler, None)
                        continue
                    j = int(j)
                    i = step - lags[j]
                    if 0 <= i < len(units):
                        units[i][j]()
            for _ in filler:
                pass

        for h in range(4):
            t_bt = V(((s_b, 16), (s_m, 16)), v.scalar_tensor_tensor, BT[:, h, :], BT[:, h, :], 8.0, cmask[:, :],
                     ALU.mult, ALU.add)
        sfree = [(), (), ()]
        ptfree = [(), ()]
        avst = {}

        def scores_row(ps, bias, S_, st, tok, free):
            return V((tok, *free), v.tensor_tensor_reduce, out=S_, in0=ps, in1=bias, scale=0.125, scalar=-3.0e38,
                     op0=ALU.add, op1=ALU.max, accum_out=c_mx[:, st:st + 1])

        units = []
        for h in range(4):
            i = h

            def s0(h=h, i=i):
                b0 = 0 if i % 2 == 0 else 2
                pa, pb_ = bk[b0], bk[b0 + 1]
                for c in range(2):
                    t0 = P((tz, t_hb, t_kd, *bfree[b0], *bfree[b0 + 1]), pe.matmul, pa[:, c * 128:(c + 1) * 128],
                           QD[:, h, c, 0:128], KD[:, h, 0:128], start=True, stop=True)
                for c in range(2):
                    t0 = P((), pe.matmul, pb_[:, c * 256:(c + 1) * 256],
                           QD[:, h, c, 128:256], KD[:, h, :], start=True, stop=True)
                Sx = SD[i % 3]
                st = 4 * (i % 3)
                fr = sfree[i % 3]
                r = []
                r.append(scores_row(pa[:, 0:128], BT[:, h, 128:256], Sx[:, 0:128], st, t0, (*fr, t_bt)))
                r.append(scores_row(pa[:, 128:256], BT[:, h, 128:256], Sx[:, 128:256], st + 1, t0, ()))
                r.append(scores_row(pb_[:, 0:256], BT[:, h, 0:256], Sx[:, 256:512], st + 2, t0, ()))
                r.append(scores_row(pb_[:, 256:512], BT[:, h, 0:256], Sx[:, 512:768], st + 3, t0, ()))
                bfree[b0] = bfree[b0 + 1] = (r[-1],)
                tn = V((r[-1],), v.tensor_scalar, c_nm[:, st:st + 4], c_mx[:, st:st + 4], -1.0, None, ALU.mult)
                for q, (lo, hi) in enumerate(((0, 128), (128, 256), (256, 512), (512, 768))):
                    te = A((tn,), a.activation, Sx[:, lo:hi], Sx[:, lo:hi], ACT.Exp, bias=c_nm[:, st + q:st + q + 1],
                           accum_out=c_dn[:, st + q:st + q + 1])
                avst[("e", i)] = te

            def s1(h=h, i=i):
                Sx = SD[i % 3]
                st = 4 * (i % 3)
                t = V((avst[("e", i)],), v.reciprocal, c_rc[:, st:st + 4], c_dn[:, st:st + 4])
                for c in (1, 3):
                    tm = V((t, t_lam), v.tensor_scalar, c_rc[:, st + c:st + c + 1], c_rc[:, st + c:st + c + 1],
                           c_lam[:, 3:4], None, ALU.mult)
                for q, (lo, mid, hi) in enumerate(((0, 128, 256), (256, 512, 768))):
                    t = V((tm,), v.tensor_scalar, Sx[:, lo:mid], Sx[:, lo:mid], c_rc[:, st + 2 * q:st + 2 * q + 1], None,
                          ALU.mult)
                    t = V((t,), v.scalar_tensor_tensor, Sx[:, lo:mid], Sx[:, mid:hi],
                          c_rc[:, st + 2 * q + 1:st + 2 * q + 2], Sx[:, lo:mid], ALU.mult, ALU.add)
                avst[("p", i)] = t

            def s2(h=h, i=i):
                Sx, b, pt = SD[i % 3], 4 + i % 2, PTB[i % 2]
                for n, lo in enumerate((0, 256, 384)):
                    t = P((avst[("p", i)], *bfree[b]), pe.transpose, bk[b][:, n * 128:(n + 1) * 128], Sx[:, lo:lo + 128],
                          ident[:, :])
                sfree[i % 3] = (t,)
                t = V((t, t_yr, (s_wf, 16), *ptfree[i % 2]), v.tensor_copy, pt[:, 0:384], bk[b][:, 0:384])
                bfree[b] = (t,)
                avst[("t", i)] = t

            def s3(h=h, i=i):
                pt = PTB[i % 2]
                t = P((avst[("t", i)], t_vd, *bfree[6]), pe.matmul, bk[6][:, 0:128], pt[:, 0:128],
                      VD[:, 0, h * 128:(h + 1) * 128], start=True, stop=True)
                P((), pe.matmul, bk[6][:, 128:256], pt[:, 128:256], VD[:, 0, h * 128:(h + 1) * 128], start=True, stop=False)
                t = P((), pe.matmul, bk[6][:, 128:256], pt[:, 256:384], VD[:, 1, h * 128:(h + 1) * 128], start=False,
                      stop=True)
                ptfree[i % 2] = (t,)
                t = A((t, t_yr), a.activation, O[:, :, h * 128:(h + 1) * 128], two(bk[6][:, 0:256]), ACT.Copy)
                bfree[6] = (t,)
                avst[("o", h)] = t
            units.append([s0, s1, s2, s3])
        unit1 = units[1][0]
        units[1][0] = lambda: (unit1(), forget())
        for h in range(8):
            i = 4 + h

            def s0(h=h, i=i):
                b0 = i % 4
                c, hf = h // 2, h % 2
                w_ = (last["l"], (s_l, 16), avst["qf"], *bfree[b0])
                for lo, n, q0 in ((0, 128, 0), (128, 256, 128)):
                    P.quiet(w_, pe.matmul, bk[b0][:, lo:lo + n], QF[:, c, hf, q0:q0 + 128], KF[:, c, 0:n], start=True,
                            stop=False)
                    P.quiet((), pe.matmul, bk[b0][:, lo:lo + n], LH[:, h, 0:128], RH[:, 0, 0:n], start=False, stop=False)
                    t0 = P((), pe.matmul, bk[b0][:, lo:lo + n], QC[:, 0, q0:q0 + 128], LH[:, h, 0:n], start=False, stop=True)
                Sx, st = SD[i % 3], 4 * (i % 3)
                scores_row(bk[b0][:, 0:128], cmask[:, 128:256], Sx[:, 0:128], st, t0, sfree[i % 3])
                r = scores_row(bk[b0][:, 128:384], cmask[:, 0:256], Sx[:, 128:384], st + 1, t0, ())
                bfree[b0] = (r,)
                tn = V((r,), v.tensor_scalar, c_nm[:, st:st + 2], c_mx[:, st:st + 2], -1.0, None, ALU.mult)
                for q, (lo, hi) in enumerate(((0, 128), (128, 384))):
                    te = A((tn,), a.activation, Sx[:, lo:hi], Sx[:, lo:hi], ACT.Exp, bias=c_nm[:, st + q:st + q + 1],
                           accum_out=c_dn[:, st + q:st + q + 1])
                avst[("e", i)] = te

            def s1(h=h, i=i):
                Sx, st = SD[i % 3], 4 * (i % 3)
                t = V((avst[("e", i)],), v.reciprocal, c_rc[:, st:st + 2], c_dn[:, st:st + 2])
                for q, (lo, hi) in enumerate(((0, 128), (128, 384))):
                    tp = V((t,), v.tensor_scalar, Sx[:, lo:hi], Sx[:, lo:hi], c_rc[:, st + q:st + q + 1], None, ALU.mult)
                avst[("p", i)] = tp

            def s2(h=h, i=i):
                Sx, b, pt = SD[i % 3], 4 + i % 2, PTB[i % 2]
                for n in range(3):
                    t = P((avst[("p", i)], *bfree[b]), pe.transpose, bk[b][:, n * 128:(n + 1) * 128],
                          Sx[:, n * 128:(n + 1) * 128], ident[:, :])
                sfree[i % 3] = (t,)
                t = V((t, *ptfree[i % 2]), v.tensor_copy, pt[:, 0:384], bk[b][:, 0:384])
                bfree[b] = (t,)
                avst[("t", i)] = t

            def s3(h=h, i=i):
                pt, p0 = PTB[i % 2], 64 * (h % 2)
                w_ = bfree[6] if h % 2 == 0 else ()
                o = bk[6][p0:p0 + 64, :]
                P.quiet((avst[("t", i)], t_vf, *w_), pe.matmul, o[:, 0:256], VF[:, 0, h * 64:(h + 1) * 64], pt[:, 0:256],
                        start=True, stop=False)
                t = P((), pe.matmul, o[:, 128:256], VF[:, 1, h * 64:(h + 1) * 64], pt[:, 256:384], start=False, stop=True)
                ptfree[i % 2] = (t,)
                if h % 2:
                    t = split_out(t, (YF.h[:, h // 2, :], YF.l[:, h // 2, :], YF.hf[:, h // 2, :]), bk[6][:, 0:256])
                    bfree[6] = (t,)
                    avst["yf"] = t
            units.append([s0, s1, s2, s3])
        def fill1():
            yield from pair_fill(range(2), halves(QF), 7)
            yield from pair_fill(range(2), plain(KF), 7)
            avst["qf"] = (A.sem, A.n)
            yield from gate_fill(12, GT, c_hb[:, 16:40], 7, free=(t_hb,))
        run_pipeline(units, fill1(), "ff02f13", lambda s: 9 + 2.6 * (s - 3))
        t_gt = (A.sem, A.n)

        O8 = O.rearrange("p b (h d) -> p (b h) d", d=128)
        SQ = pg(140, 8, 128)
        t = V((avst[("o", 3)], (P.sem, P.n)), v.tensor_tensor, SQ, O8, O8, ALU.mult)
        t = V((t,), v.reduce_sum, c_ss, SQ, axis=AX)
        t = V((t,), v.tensor_scalar, c_ss, c_ss, 1.0 / 128, 1e-6, ALU.mult, ALU.add)
        t = A((t,), a.activation, c_ss, c_ss, ACT.Sqrt)
        t = V((t,), v.reciprocal, c_rs, c_ss)
        t = V((t,), v.tensor_tensor, O8, O8, c_rs.rearrange("p (n a) -> p n a", a=1).to_broadcast([128, 8, 128]), ALU.mult)
        for pr in range(2):
            for h in range(2):
                for tb in range(2):
                    tt = P((t, *bfree[pr]), pe.transpose, bk[pr][:, h * 256 + tb * 128:h * 256 + tb * 128 + 128],
                           O[:, tb, (2 * pr + h) * 128:(2 * pr + h + 1) * 128], ident[:, :])
            q = slice(2 * pr, 2 * pr + 2)
            t_yd = split_out(tt, (YD.h[:, q, :], YD.l[:, q, :], YD.hf[:, q, :]), two(bk[pr][:, :]), c_sub)
            bfree[pr] = (t_yd,)

        def merge(M, TMP, GTs, branches, mfree):
            tm, tl = {}, {}
            cnt = 0
            for bi, (npieces, k_per, rhs, toks) in enumerate(branches):
                for n in range(0, 8, 2):
                    b = nextbank(0, 4)
                    t = pair(b, npieces, k_per, rhs, toks)
                    gate, ps, m = GTs[:, bi * 8 + n:bi * 8 + n + 2, :], two(bk[b][:, :]), M.raw[:, n:n + 2, :]
                    if bi == 0:
                        r = tm[n] = V((t, t_gt, *mfree), v.scalar_tensor_tensor, m, gate, 1.0, ps, ALU.add, ALU.mult)
                    else:
                        x = TMP[:, 2 * (cnt % 2):2 * (cnt % 2) + 2, :]
                        cnt += 1
                        r = V((t, *mfree), v.scalar_tensor_tensor, x, gate, 1.0, ps, ALU.add, ALU.mult)
                        tm[n] = V((r, tm[n]), v.tensor_tensor, m, m, x, ALU.add)
                    bfree[b] = (r,)
                    if bi == len(branches) - 1:
                        tl[n] = split_out(tm[n], (M.h[:, n:n + 2, :], M.l[:, n:n + 2, :], M.hf[:, n:n + 2, :]), m)
            return tl

        M1, TMP = Two(120, 128, 8), pg(136, 4)
        tm = merge(M1, TMP, GT, [(2, 4, YR, (t_yr,)), (1, 4, YD, (t_yd,)), (1, 4, YF, (avst["yf"],))],
                   ((P.sem, P.n),))

        tbk = {}

        def project_out(M, tm, X):
            for i in range(2):
                for j in range(4):
                    wh, wl, tw = sp.take()
                    for tb in range(2):
                        b = 4 + 2 * i + tb
                        q = slice(tb * 128, (tb + 1) * 128)
                        for k in range(2):
                            kk = 2 * j + k
                            t = tbk[b] = mm3(P if k == 1 else P.quiet, bk[b][:, :], M.h[:, kk, q], M.l[:, kk, q], wh[:, k, :],
                                    wl[:, k, :], start=(kk == 0), stop=(kk == 7), after=(*tw, tm[2 * j], *bfree[b]))
                    sp.done(t)
                r = []
                for tb in range(2):
                    b = 4 + 2 * i + tb
                    xs = X[:, tb, i * 512:(i + 1) * 512]
                    r.append(V((tbk[b],), v.scalar_tensor_tensor, xs, bk[b][:, :], 0.5, xs, ALU.mult, ALU.add))
                    bfree[b] = (r[tb],)
            return r

        t_x1 = project_out(M1, tm, X)

        s_fg = sem("s_fg")
        slots[2].free = ((P.sem, P.n),)
        stream.open(slots[2], slots[2].free)
        FG = pg(196, 1, 1024)[:, 0, :]
        A.dma(((P.sem, P.n), (V.sem, V.n)), s_fg, FG, I["final_g"].rearrange("(a n) -> a n", a=1).to_broadcast([128, 1024]))
        _, tHT = norm_T(t_x1, "g2", pg(160, 2, 1024), HT, ((P.sem, P.n),))
        AT = Two(96, 118, 22)
        t_ = ((P.sem, P.n), (V.sem, V.n), (A.sem, A.n))
        sp.lend([wbuf(172), wbuf(180), wbuf(188)], t_)
        UU = [pg(140 + 4 * i, 4) for i in range(4)]
        ufree = [()] * 4
        tA = {}
        behind = []

        def flush():
            todo, behind[:] = behind[:], []
            for f in todo:
                f()

        def up_gelu(U, r, tg):
            tg.append(A((r,), a.activation, U[:, 0:2, :], U[:, 0:2, :], ACT.Gelu_apprx_tanh))

        def up_mul(i, U, r, tg):
            m = V((*tg, r), v.tensor_tensor, U[:, 2:4, :], U[:, 0:2, :], U[:, 2:4, :], ALU.mult)
            behind.append(lambda: up_out(i, U, m))

        def up_out(i, U, m):
            x = slice(2 * i, 2 * i + 2)
            r = split_out(m, (AT.h[:, x, :], AT.l[:, x, :], AT.hf[:, x, :]), U[:, 2:4, :])
            ufree[i % 4] = (r,)
            tA[2 * i] = tA[2 * i + 1] = r
        for i in range(11):
            q = i % 4
            U = UU[q]
            for kind in range(2):
                b = nextbank(0, 4)
                t = pair(b, 2, 4, HT, tHT)
                flush()
                for h in range(2):
                    n = kind * 22 + 2 * i + h
                    r0 = A((t, *ufree[q]), a.activation, U[:, 2 * kind + h, :], bk[b][:, h * 256:(h + 1) * 256],
                           ACT.Identity, scale=par("fw", 88 + n), bias=par("fb", n))
                for h in range(2):
                    n = kind * 22 + 2 * i + h
                    ps, o = bk[b][:, h * 256:(h + 1) * 256], U[:, 2 * kind + h, :]
                    r = r0
                    for d in (1, 2):
                        r = V((r,), v.scalar_tensor_tensor, o[:, d:256], ps[:, 0:256 - d], par("fw", (2 - d) * 44 + n),
                              o[:, d:256], ALU.mult, ALU.add)
                bfree[b] = (r,)
                if kind == 0:
                    tg = []
                    behind.append(lambda U=U, r=r, tg=tg: up_gelu(U, r, tg))
            behind.append(lambda i=i, U=U, r=r, tg=tg: up_mul(i, U, r, tg))
        flush()
        flush()
        for kk in range(22):
            wh, wl, tw = sp.take()
            for tb in range(2):
                q = slice(tb * 128, (tb + 1) * 128)
                for hf in range(2):
                    b = 4 + 2 * tb + hf
                    c = slice(hf * 512, (hf + 1) * 512)
                    t = tbk[b] = mm3(P, bk[b][:, :], AT.h[:, kk, q], AT.l[:, kk, q], wh[:, 0, c], wl[:, 0, c],
                            start=(kk == 0), stop=(kk == 21), after=(*tw, tA[kk], *(bfree[b] if kk == 0 else ())))
            sp.done(t)
        def add_banks(t):
            out_ = []
            for tb in range(2):
                for hf in range(2):
                    b = 4 + 2 * tb + hf
                    xs = X[:, tb, hf * 512:(hf + 1) * 512]
                    r = V((t[b],), v.tensor_tensor, xs, xs, bk[b][:, :], ALU.add)
                    bfree[b] = (r,)
                out_.append(r)
            return out_
        r = add_banks(tbk)

        def final_norm(t_in, FGt, t_fg, junk, free):
            t = rstd(t_in, X, junk, free)
            return [V((t, t_fg), v.scalar_tensor_tensor, X[:, b, :], X[:, b, :], c_rs[:, 4 + b:5 + b], FGt, ALU.mult,
                      ALU.mult) for b in range(2)]
        t_x = final_norm(r, FG, (s_fg, 16), pg(160, 2, 1024), ((P.sem, P.n),))

        sp.drop()
        ex_at = [116, 132, 148, 165, 181, 24]
        extra_slots = [Slot(pg(p_, 1, KS)[:, 0, :], sem(f"s_e{i}"), True) for i, p_ in enumerate(ex_at)]
        s_rt, s_io, s_nf = sem("s_rt"), sem("s_io"), sem("s_nf")
        RW = sm[:, 192:448].rearrange("p (k n) -> p k n", k=8)
        IO, ID4 = c_tmp[:, 96:128], c_tmp[:, 64:80]
        t = G((t_lam,), g.memset, RW, 0.0)
        A.dma((t,), s_rt, RW[:, :, 0:16], I["router"][0].rearrange("(k p) n -> p k n", p=128))
        A.dma((t,), s_io, IO, I["iota"])
        t = V((), v.tensor_tensor, ID4, ident[:, 0:16], ident[:, 32:48], ALU.add)
        t = V((t,), v.tensor_tensor, ID4, ID4, ident[:, 64:80], ALU.add)
        t_id4 = V((t,), v.tensor_tensor, ID4, ID4, ident[:, 96:112], ALU.add)
        ex_toks = ()
        btiles = [pg(157, 5, 384)[:, i, :] for i in range(5)]
        s_bt = [sem(f"s_bt{i}") for i in range(5)]
        bcount = [0] * 5

        for l in range(2):
            for i_ in range(3):
                sp.add(f"qka{l}", i_, PAIRS)
            sp.add(f"va{l}", 0, TOKS)
            sp.add(f"vb{l}", 0, [v_flat(j, 4, 256) for j in range(2)])
            for i_ in range(2):
                sp.add(f"qw{l}", i_, PAIRS)
            sp.add(f"kvw{l}", 0, PAIRS)
            for i_ in range(4):
                sp.add(f"gate{l}", i_, PAIRS)
            sp.add(f"bra{l}", 0, [v_rows(pr, 2) for pr in range(4)])
            for i_ in range(2):
                sp.add(f"brb{l}", i_, PAIRS)
            for i_ in range(2):
                sp.add(f"wo{l}", i_, TOKS)
            XN = pg(165, 2, 1024)
            all_now = ((P.sem, P.n), (V.sem, V.n), (A.sem, A.n), (G.sem, G.n), *ex_toks)
            tzz = G(all_now, g.memset, pg(96, 28), 0.0)
            QA = pg(96, 12).rearrange("p (h c) n -> p h c n", c=2)
            QW = pg(108, 16).rearrange("p (h c) n -> p h c n", c=2)
            KA, KW = pg(124, 6), pg(130, 4)
            VA, VW = pg(134, 2, 768), pg(140, 2, 256)
            GL = pg(165, 16)
            OA, OB = Two(181, 183, 2), Two(185, 193, 8)
            SX = [pg(142 + 3 * i, 1, 768)[:, 0, :] for i in range(3)]
            PTL = [pg(151, 1, 768)[:, 0, :], pg(154, 1, 768)[:, 0, :]]
            ML, TMPL = Two(96, 104, 8), pg(112, 4)
            sfree = [(), (), ()]
            ptfree = [(), ()]
            bready, bnext = {}, [0]

            def load_bias(q, toks):
                if bnext[0] < 28:
                    bcount[q] += 16
                    G.dma(toks, s_bt[q], btiles[q], I["bias"][bnext[0]])
                    bready[bnext[0]] = (q, (s_bt[q], bcount[q]))
                    bnext[0] += 1
            for q in range(5):
                load_bias(q, all_now)

            def bias_win(n, qb):
                q, td = bready[n]
                return btiles[q][:, 0:256] if qb else btiles[q][:, 128:384], td

            _, tHT = norm_T(t_x, f"gm{l}", XN, HT, tuple(q for q in all_now if q[0] is not V.sem))
            sp.idle = [(b_, all_now) for b_, _ in sp.idle]
            sp.lend([wbuf(173), wbuf(181), wbuf(189)], all_now)
            tz = tzz

            def qk_sink(i):
                def f(pr, b, t):
                    n = 4 * i + 2 * pr
                    if n < 6:
                        return halves(QA, n - 2 * pr)(pr, b, t)
                    return plain(KA, n - 6 - 2 * pr)(pr, b, t)
                return f
            for i in range(3):
                pair_T(range(2), HT, tHT, qk_sink(i), (0, 4))
            tokmajor(VA, 0, 512, (0, 4), 4, 2, free=all_now)
            t_ka = (A.sem, A.n)
            sp.drop()

            def kw_sink(pr, b, t):
                for c in range(2):
                    for h in range(2):
                        for d in range(2):
                            r = A((t,), a.activation, KW[64 * d:64 * d + 64, 2 * c + h, :],
                                  bk[b][64 * h:64 * h + 64, c * 256:(c + 1) * 256], ACT.Copy)
                return (r,)

            def fill2(l=l, GL=GL, QW=QW, VA=VA, VW=VW, kw_sink=kw_sink):
                yield from tok_fill(VA, 512, "va", 7)
                for i in range(2):
                    yield from pair_fill(range(2), halves(QW, 4 * i), 7)
                yield from pair_fill(range(1), kw_sink, 7)
                avst["qw"] = (A.sem, A.n)
                yield from tok_fill(VW, 0, "vw", 7)
                yield from gate_fill(8, GL, c_hg[:, 16 * l:16 * l + 16], 7)

            units = []
            for h in range(4):
                for qb in range(2):
                    i = 2 * h + qb

                    def s0(h=h, qb=qb, i=i, t_ka=t_ka):
                        b0 = 0 if i % 2 == 0 else 2
                        Sx, st = SX[i % 3], 4 * (i % 3)
                        r = None
                        for gi in range(3):
                            s = gi * 4 + h
                            bb, off = (b0, gi * 256) if gi < 2 else (b0 + 1, 0)
                            t0 = P((t_ka, *bfree[b0], *bfree[b0 + 1]), pe.matmul, bk[bb][:, off:off + 256],
                                   QA[:, s // 2, s % 2, qb * 128:(qb + 1) * 128], KA[:, s // 2, :], start=True, stop=True)
                        for gi in range(3):
                            bb, off = (b0, gi * 256) if gi < 2 else (b0 + 1, 0)
                            bi, td = bias_win(3 * h + gi, qb)
                            r = V((t0, td, *sfree[i % 3]), v.tensor_tensor_reduce, out=Sx[:, gi * 256:(gi + 1) * 256],
                                  in0=bk[bb][:, off:off + 256], in1=bi, scale=0.125, scalar=-3.0e38,
                                  op0=ALU.add, op1=ALU.max, accum_out=c_mx[:, st + gi:st + gi + 1])
                        bfree[b0] = bfree[b0 + 1] = (r,)
                        if qb == 1:
                            for gi in range(3):
                                load_bias(bready[3 * h + gi][0], (r,))
                        r = V((r,), v.reduce_max, c_nm[:, st:st + 1], c_mx[:, st:st + 3], axis=AX, negate=True)
                        te = A((r,), a.activation, Sx[:, 0:768], Sx[:, 0:768], ACT.Exp, bias=c_nm[:, st:st + 1],
                               accum_out=c_dn[:, st:st + 1])
                        avst[("e", i)] = te

                    def s1(i=i):
                        Sx, st = SX[i % 3], 4 * (i % 3)
                        t = V((avst[("e", i)],), v.reciprocal, c_rc[:, st:st + 1], c_dn[:, st:st + 1])
                        avst[("p", i)] = V((t,), v.tensor_scalar, Sx[:, 0:768], Sx[:, 0:768], c_rc[:, st:st + 1], None,
                                           ALU.mult)

                    def s2(i=i):
                        Sx, pt = SX[i % 3], PTL[i % 2]
                        for n in range(6):
                            b = 4 + n // 4
                            t = P((avst[("p", i)], *bfree[4], *bfree[5]), pe.transpose,
                                  bk[b][:, (n % 4) * 128:(n % 4 + 1) * 128], Sx[:, n * 128:(n + 1) * 128], ident[:, :])
                        sfree[i % 3] = (t,)
                        t4 = A((t, *ptfree[i % 2]), a.activation, pt[:, 0:512], bk[4][:, :], ACT.Copy)
                        t5 = V((t, *ptfree[i % 2]), v.tensor_copy, pt[:, 512:768], bk[5][:, 0:256])
                        bfree[4], bfree[5] = (t4,), (t5,)
                        avst[("t", i)] = (t4, t5)

                    def s3(h=h, qb=qb, i=i):
                        pt, p0 = PTL[i % 2], 64 * (h % 2)
                        w_ = bfree[6] if i % 4 == 0 else ()
                        o = bk[6][p0:p0 + 64, qb * 128:(qb + 1) * 128]
                        for n in range(6):
                            s = (n // 2) * 4 + h
                            f = P.quiet if n < 5 else P
                            t = f((*avst[("t", i)], avst["va"], *w_), pe.matmul, o, VA[:, n % 2, s * 64:(s + 1) * 64],
                                  pt[:, n * 128:(n + 1) * 128], start=(n == 0), stop=(n == 5))
                        ptfree[i % 2] = (t,)
                        if i % 4 == 3:
                            t = split_out(t, (OA.h[:, h // 2, :], OA.l[:, h // 2, :], OA.hf[:, h // 2, :]), bk[6][:, 0:256])
                            bfree[6] = (t,)
                            avst["oa"] = t
                    units.append([s0, s1, s2, s3])
            for h in range(16):
                i = 8 + h

                def s0(h=h, i=i, l=l):
                    b0 = i % 4
                    Sx, st = SX[i % 3], 4 * (i % 3)
                    for qb in range(2):
                        t0 = P((avst["qw"], *bfree[b0]), pe.matmul, bk[b0][:, qb * 256:(qb + 1) * 256],
                               QW[:, h // 2, h % 2, qb * 128:(qb + 1) * 128], KW[:, h // 4, :], start=True, stop=True)
                    for qb in range(2):
                        bi, td = bias_win(12 + h, qb)
                        r = V((t0, td, *sfree[i % 3]), v.tensor_tensor_reduce, out=Sx[:, qb * 256:(qb + 1) * 256],
                              in0=bk[b0][:, qb * 256:(qb + 1) * 256], in1=bi, scale=0.125, scalar=-3.0e38,
                              op0=ALU.add, op1=ALU.max, accum_out=c_mx[:, st + qb:st + qb + 1])
                    bfree[b0] = (r,)
                    load_bias(bready[12 + h][0], (r,))
                    sk = c_sink[:, 16 * l + h:16 * l + h + 1]
                    r = V((r,), v.tensor_scalar, c_nm[:, st:st + 2], c_mx[:, st:st + 2], sk, -1.0, ALU.max, ALU.mult)
                    for qb in range(2):
                        A((r,), a.activation, Sx[:, qb * 256:(qb + 1) * 256], Sx[:, qb * 256:(qb + 1) * 256], ACT.Exp,
                          bias=c_nm[:, st + qb:st + qb + 1], accum_out=c_dn[:, st + qb:st + qb + 1])
                    te = A((), a.activation, c_es[:, st:st + 2], c_nm[:, st:st + 2], ACT.Exp, bias=sk)
                    avst[("e", i)] = te

                def s1(i=i):
                    Sx, st = SX[i % 3], 4 * (i % 3)
                    t = V((avst[("e", i)],), v.tensor_tensor, c_dn[:, st:st + 2], c_dn[:, st:st + 2], c_es[:, st:st + 2],
                          ALU.add)
                    t = V((t,), v.reciprocal, c_rc[:, st:st + 2], c_dn[:, st:st + 2])
                    for qb in range(2):
                        tp = V((t,), v.tensor_scalar, Sx[:, qb * 256:(qb + 1) * 256], Sx[:, qb * 256:(qb + 1) * 256],
                               c_rc[:, st + qb:st + qb + 1], None, ALU.mult)
                    avst[("p", i)] = tp

                def s2(i=i):
                    Sx, b, pt = SX[i % 3], 4 + i % 2, PTL[i % 2]
                    for kb in range(2):
                        for qb in range(2):
                            t = P((avst[("p", i)], *bfree[b]), pe.transpose,
                                  bk[b][:, kb * 256 + qb * 128:kb * 256 + qb * 128 + 128],
                                  Sx[:, qb * 256 + kb * 128:qb * 256 + kb * 128 + 128], ident[:, :])
                    sfree[i % 3] = (t,)
                    t = A((t, *ptfree[i % 2]), a.activation, pt[:, 0:512], bk[b][:, :], ACT.Copy)
                    bfree[b] = (t,)
                    avst[("t", i)] = t

                def s3(h=h, i=i):
                    pt, p0 = PTL[i % 2], 64 * (h % 2)
                    w_ = bfree[6] if h % 2 == 0 else ()
                    hk = h // 4
                    for kb in range(2):
                        f = P.quiet if kb < 1 else P
                        t = f((avst[("t", i)], avst["vw"], *w_), pe.matmul, bk[6][p0:p0 + 64, 0:256], VW[:, kb, hk * 64:(hk + 1) * 64],
                              pt[:, kb * 256:(kb + 1) * 256], start=(kb == 0), stop=(kb == 1))
                    ptfree[i % 2] = (t,)
                    if h % 2:
                        t = split_out(t, (OB.h[:, h // 2, :], OB.l[:, h // 2, :], OB.hf[:, h // 2, :]), bk[6][:, 0:256])
                        bfree[6] = (t,)
                        avst["ob"] = t
                units.append([s0, s1, s2, s3])

            def slow(gen, every):
                for _ in gen:
                    for _ in range(every):
                        yield

            run_pipeline(units, fill2(), "01ff23",
                         lambda s: min(2 * (s + 1), 16 + 0.9 * (s - 7)))
            t_gt = (A.sem, A.n)
            t_att = ((P.sem, P.n), (V.sem, V.n), (A.sem, A.n))
            for s_ in extra_slots[0:3]:
                stream.open(s_, t_att)
            tm = merge(ML, TMPL, GL, [(1, 2, OA, (avst["oa"],)), (2, 4, OB, (avst["ob"],))], t_att)
            t_mg = ((P.sem, P.n), (V.sem, V.n))
            for s_ in extra_slots[3:5]:
                stream.open(s_, t_mg)
            t_x1 = project_out(ML, tm, X)
            stream.open(extra_slots[5], ((P.sem, P.n),))
            done = ((P.sem, P.n), (V.sem, V.n), (A.sem, A.n), (G.sem, G.n))

            XN, XH, XL = pg(96, 2, 1024), pr_(104, 2, 1024), pr_(96, 2, 1024)
            HTf = pg(8, 8)
            POr = pr_(40, 2, 512)
            XE = pg(8, 8, 512)
            PG = pg(44, 2, 512)
            GZ = [pg(96, 4), pg(100, 4)]
            LG = pg(112, 1)[:, 0, 160:192]
            AF, WK, MK, AF2 = (pg(p_, 1)[:, 0, :] for p_ in (113, 114, 115, 197))
            TA = pg(198, 1)[:, 0, :]
            YE = [pg(199, 1)[:, 0, :], pg(200, 1)[:, 0, :]]
            HA = [pg(113, 1)[:, 0, :], pg(114, 1)[:, 0, :]]
            tzg = []
            tXN, tHT = norm_T(t_x1, f"gf{l}", XN, HTf, tuple(q for q in done if q[0] is not V.sem))
            t_tr = (P.sem, P.n)
            for k in range(8):
                j = k % 4
                f = P.quiet if k < 7 else P
                t = f((tHT[k // 2], (s_rt, 16 * (l + 1)), *bfree[4]), pe.matmul, bk[4][32 * j:32 * j + 32, 0:256],
                      RW[:, k, :], HTf[:, k, :], start=(k < 4), stop=(k >= 4))
            if l == 0:
                A.dma((t,), s_rt, RW[:, :, 0:16], I["router"][1].rearrange("(k p) n -> p k n", p=128))
            warm(ACT.Exp)
            L2 = LG.rearrange("p (b n) -> p b n", b=2)
            t = V((t,), v.tensor_copy, AF, bk[4][:, 0:256])
            bfree[4] = (t,)
            for tb in range(2):
                t2 = P((t, t_id4, *bfree[7]), pe.matmul, bk[7][:, tb * 16:(tb + 1) * 16],
                       AF[:, tb * 128:(tb + 1) * 128], ID4, start=True, stop=True)
            t = V((t2,), v.tensor_copy, LG, bk[7][:, 0:32])
            bfree[7] = (t,)
            t = V((t,), v.reduce_max, c_nm[:, 0:2], L2, axis=AX, negate=True)
            for tb in range(2):
                te = A((t,), a.activation, L2[:, tb, :], L2[:, tb, :], ACT.Exp, bias=c_nm[:, tb:tb + 1],
                       accum_out=c_dn[:, tb:tb + 1])
            t_xh = A((*tXN, *done), a.activation, XH, XN, ACT.Copy)
            t_xl = G((t_xh, t_tr), g.tensor_tensor, XL, XN, XH.bitcast(F32), ALU.subtract)
            t = V((te,), v.reciprocal, c_rc[:, 0:2], c_dn[:, 0:2])
            for tb in range(2):
                t_lg = V((t,), v.tensor_scalar, L2[:, tb, :], L2[:, tb, :], c_rc[:, tb:tb + 1], None, ALU.mult)
            for tb in range(2):
                t = P((t_lg, *bfree[5]), pe.transpose, bk[5][0:16, tb * 128:(tb + 1) * 128], L2[:, tb, :], ident[:, :])
            af, wk, mk = AF[0:16, :], WK[0:16, :], MK[0:16, :]
            t = V((t,), v.tensor_copy, af, bk[5][0:16, 0:256])
            bfree[5] = (t,)
            src = af
            for r_ in range(4):
                t = V((t,), v.max, c_tmp[0:16, 8 * r_:8 * r_ + 8], src)
                keep((t,), 1, 2)
                t = V((t,), v.match_replace, wk, c_tmp[0:16, 8 * r_:8 * r_ + 8], src, -1.0)
                src = wk
            keep((t,), 1, 2)
            t = V((t,), v.tensor_scalar, mk, wk, 0.0, None, ALU.is_lt)
            keep((t,), 1, 2)
            t = V((t,), v.tensor_scalar, wk, wk, 0.0, 1.0, ALU.mult, ALU.add)
            t = V((t,), v.tensor_tensor_scan, AF2[0:16, :], wk, mk, 0.0, ALU.mult, ALU.add)
            t = V((t,), v.tensor_tensor, mk, mk, AF2[0:16, :], ALU.mult)
            for tb in range(2):
                tt = P((t, *bfree[6]), pe.transpose, bk[6][:, tb * 16:(tb + 1) * 16], mk[:, tb * 128:(tb + 1) * 128],
                       ident[0:16, 0:16])
            t = V((tt,), v.tensor_copy, c_tmp[:, 32:64], bk[6][:, 0:32])
            bfree[6] = (t,)
            iob = IO.rearrange("p (a t) -> p a t", a=1).to_broadcast([128, 16, 32])
            for tb in range(2):
                rk = c_tmp[:, 32 + 16 * tb:48 + 16 * tb].rearrange("p (e a) -> p e a", a=1).to_broadcast([128, 16, 32])
                por = POr[:, tb, :].rearrange("p (e t) -> p e t", t=32)
                t_po = V((t, (s_io, 16)), v.tensor_tensor, por, rk, iob, ALU.is_equal)
            t_xe = []
            def gather(c):
                b = nextbank(1, 4)
                cs = slice(c * 128, (c + 1) * 128)
                for tb in range(2):
                    P.quiet((t_po, t_xh, t_xl, *bfree[b]), pe.matmul, bk[b][:, :], XH[:, tb, cs], POr[:, tb, :],
                            start=(tb == 0), stop=False)
                    f = P.quiet if tb < 1 else P
                    t = f((), pe.matmul, bk[b][:, :], XL[:, tb, cs], POr[:, tb, :], start=False, stop=(tb == 1))
                r = A((t,), a.activation, XE[:, c, :], bk[b][:, :], ACT.Copy, scale=par(f"gf{l}", c)) if c % 2 else \
                    V((t,), v.tensor_scalar, XE[:, c, :], bk[b][:, :], par(f"gf{l}", c), None, ALU.mult)
                bfree[b] = (r,)
                t_xe.append(r)
            for tb in range(2):
                po = POr[:, tb, :].bitcast(F32).rearrange("p (e t) -> p e t", t=32)
                gg = L2[:, tb, :].rearrange("p (e a) -> p e a", a=1).to_broadcast([128, 16, 32])
                t_pg = V((t_po,), v.tensor_tensor, PG[:, tb, :].rearrange("p (e t) -> p e t", t=32), po, gg, ALU.mult)
            yfree = [(), ()]
            gzf = [(), ()]
            haf = [(), ()]

            def expert_up(e, kind, bank):
                for i in range(2):
                    if e == 0 and kind == "eg":
                        for c in range(4 * i, 4 * i + 4):
                            gather(c)
                        if i == 1:
                            tzg.append(G(((P.sem, P.n),), g.memset, pg(96, 8), 0.0))
                    s, td = stream.get(f"{kind}{l}_{e}", i)
                    w = s.ap.rearrange("p (k n) -> p k n", k=4)
                    for k in range(4):
                        for j in range(4):
                            f = P if (k == 3 and j == 3) else P.quiet
                            t = f((td, t_xe[4 * i + k], *bfree[bank]), pe.matmul, bk[bank][32 * j:32 * j + 32, 0:256],
                                  XE[:, 4 * i + k, 32 * e:32 * e + 32], w[:, k, 256 * j:256 * j + 256],
                                  start=(i == 0 and k == 0), stop=(i == 1 and k == 3))
                    stream.done(s, t)
                return t

            def expert_in(e):
                tg = expert_up(e, "eg", 0)
                q = e % 2
                t1 = A((tg, (V.sem, V.n), *haf[q]), a.activation, TA, bk[0][:, 0:256], ACT.Tanh, scale=0.5)
                t2 = V((t1,), v.scalar_tensor_tensor, TA, TA, 1.0, bk[0][:, 0:256], ALU.add, ALU.mult)
                bfree[0] = (t2,)
                tu = expert_up(e, "eu", 1)
                t3 = V((tu, t2), v.scalar_tensor_tensor, TA, bk[1][:, 0:256], 0.5, TA, ALU.mult, ALU.mult)
                bfree[1] = (t3,)
                for c in range(2):
                    t = P((t3, *bfree[2]), pe.transpose, bk[2][:, c * 128:(c + 1) * 128], TA[:, c * 128:(c + 1) * 128],
                          ident[:, :])
                for tb in range(2):
                    tg = P((t_pg,), pe.transpose, bk[2][0:32, 256 + tb * 128:384 + tb * 128],
                           PG[:, tb, 32 * e:32 * e + 32], ident[:, :])
                r = A((tg, *haf[q]), a.activation, HA[q], bk[2][:, 0:256], ACT.Copy)
                for j in range(4):
                    r = A((*tzg, *gzf[q]), a.activation, GZ[q][32 * j:32 * j + 32, j, :],
                          bk[2][0:32, 256:512], ACT.Copy)
                bfree[2] = (r,)
                return r

            def expert_out(e, th):
                q = e % 2
                for i in range(2):
                    s, td = stream.get(f"ed{l}_{e}", i)
                    w = s.ap.rearrange("p (k n) -> p k n", k=4)
                    for k in range(4):
                        kk = 4 * i + k
                        hh = HA[q][:, (kk % 2) * 128 + (kk // 2) * 32:(kk % 2) * 128 + (kk // 2) * 32 + 32]
                        for j in range(4):
                            f = P if (k == 3 and j == 3) else P.quiet
                            t = f((td, th, *bfree[3]), pe.matmul, bk[3][32 * j:32 * j + 32, 0:256], hh,
                                  w[:, k, 256 * j:256 * j + 256], start=(i == 0 and k == 0), stop=(i == 1 and k == 3))
                    stream.done(s, t)
                haf[q] = (t,)
                r = V((t, *yfree[q]), v.tensor_copy, YE[q], bk[3][:, 0:256])
                bfree[3] = (r,)
                for tb in range(2):
                    for j in range(4):
                        b = 4 + 2 * tb + j // 2
                        t = tbk[b] = P((r, *(bfree[b] if e == 0 else ())), pe.matmul, bk[b][:, (j % 2) * 256:(j % 2) * 256 + 256],
                              GZ[q][:, j, tb * 128:(tb + 1) * 128], YE[q], start=(e == 0 and j % 2 == 0),
                              stop=(e == 15), skip_group_check=True)
                yfree[q] = gzf[q] = (t,)
                return t

            for e in range(16):
                th = expert_in(e)
                t = expert_out(e, th)
            t_x = add_banks(tbk)
            toks, _ = stream.take_extras()
            ex_toks = tuple(toks)

        done = ((P.sem, P.n), (V.sem, V.n), (A.sem, A.n), *ex_toks)
        FG = pg(96, 1, 1024)[:, 0, :]
        G.dma(done, s_nf, FG, I["norm_final"].rearrange("(a n) -> a n", a=1).to_broadcast([128, 1024]))
        t = final_norm(t_x, FG, (s_nf, 16), pg(104, 2, 1024), done)
        s_o = sem("s_o")
        for b in range(2):
            S.dma((t[b],), s_o, out.rearrange("(b p) d -> p b d", p=128)[:, b, :], X[:, b, :])
        S.wait((s_o, 32), *t_r)

        block = ctx.enter_context(nc.Block())

        @block.sync
        def _(e):
            S.play()

        @block.scalar
        def _(e):
            A.play()

        @block.vector
        def _(e):
            V.play()

        @block.gpsimd
        def _(e):
            G.play()

        @block.tensor
        def _(e):
            P.play()


def bucket(n):
    if n < 16:
        return max(n, 0)
    return min(31, 16 + int(math.log(n / 16) / math.log(8.0) * 16))


def constants():
    p = np.arange(128)[:, None]
    j = np.arange(384)[None, :]
    d = p + 128 - j
    cmask = np.where(d >= 0, 0.0, 8 * BIG).astype(np.float32)
    bias = []
    for h in range(4):
        for gi in range(3):
            ok = (np.abs(d) <= 64) if gi == 0 else (d % (4 if gi == 1 else 16) == 0)
            bias.append(np.where(ok, -8.0 * np.float32(SLOPES_A[gi * 4 + h]) * np.abs(d), 8 * BIG))
    for h in range(16):
        bias.append(np.where(np.abs(d) <= 128, -8.0 * np.float32(SLOPES_W[h]) * np.abs(d), 8 * BIG))
    bias = np.stack(bias, 0).astype(np.float32)
    onehot = np.zeros((32, 512), np.float32)
    for u in range(512):
        onehot[bucket(255 - u), u] = 1.0
    sel = np.zeros((8, 8, 256), np.float32)
    for h in range(8):
        sel[h, h, :] = 1.0
    iota = np.tile(np.arange(1, 33, dtype=np.float32), (128, 1))
    return dict(ident=np.eye(128, dtype=np.float32), cmask=cmask, onehot=onehot, sel=sel, iota=iota), bias


def cols(w, c0, n):
    k = w.shape[0] // 128
    return w[:, c0:c0 + n].reshape(k, 128, n).transpose(1, 0, 2).reshape(128, k * n)


def rows(w, k0, nk):
    n = w.shape[1]
    return w[k0 * 128:(k0 + nk) * 128, :].reshape(nk, 128, n).transpose(1, 0, 2).reshape(128, nk * n)


def pack(I):
    w = I["w_in"][0]
    d = {}
    for i in range(2):
        d["xrnn", i] = cols(w, 512 * i, 512)
        d["grnn", i] = cols(w, 1024 + 512 * i, 512)
        d["brr", i] = cols(I["w_br_rnn"][0], 512 * i, 512)
        d["wout", i] = cols(I["w_out"][0], 512 * i, 512)
    for i, n in enumerate(("dq", "dk", "dv", "fq", "fk", "fv")):
        d[n, 0] = cols(w, 2048 + 512 * i, 512)
    for i in range(6):
        d["gates", i] = cols(w, 5128 + 512 * i, 512)
    d["brd", 0] = rows(I["w_br_diff"][0], 0, 4)
    d["brf", 0] = rows(I["w_br_fox"][0], 0, 4)
    up = I["ffn_up"][0]
    for i in range(11):
        d["up", i] = cols(np.concatenate([up[:, 256 * i:256 * i + 256], up[:, 2816 + 256 * i:3072 + 256 * i]], 1), 0, 512)
    for i in range(5):
        d["down", i] = rows(I["ffn_down"][0], 4 * i, 4)
    d["down5", 0] = rows(I["ffn_down"][0], 20, 2)
    for l in range(2):
        w = I["w_in_2"][l]
        for i in range(3):
            d[f"qka{l}", i] = cols(w, 512 * i, 512)
        d[f"va{l}", 0] = cols(w, 1536, 512)
        d[f"vb{l}", 0] = cols(w, 2048, 256)
        for i in range(2):
            d[f"qw{l}", i] = cols(w, 2304 + 512 * i, 512)
            d[f"brb{l}", i] = cols(I["w_branch_b_2"][l], 512 * i, 512)
            d[f"wo{l}", i] = cols(I["w_out_2"][l], 512 * i, 512)
        d[f"kvw{l}", 0] = cols(w, 3328, 512)
        for i in range(4):
            d[f"gate{l}", i] = cols(w, 3840 + 512 * i, 512)
        d[f"bra{l}", 0] = rows(I["w_branch_a_2"][l], 0, 2)
        for e in range(16):
            for i in range(2):
                d[f"eg{l}_{e}", i] = rows(I["w_expert_gate_2"][l, e], 4 * i, 4)
                d[f"eu{l}_{e}", i] = rows(I["w_expert_up_2"][l, e], 4 * i, 4)
                d[f"ed{l}_{e}", i] = rows(I["w_expert_down_2"][l, e], 4 * i, 4)
    sl = slab_list()
    out = np.zeros((len(sl), 128, KS), np.float32)
    for n, (name, i, c, _) in enumerate(sl):
        out[n, :, 0:c] = d[name, i]
    return out


def pack_params(I):
    def c(a):
        return np.asarray(a).reshape(-1, 128).T
    out = np.zeros((128, NPV), np.float32)
    for name, arr in (("g1", I["norm1_g"]), ("cw", I["rnn_conv_w"]), ("cb", I["rnn_conv_b"]), ("br", I["rg_b_r"]),
                      ("bi", I["rg_b_i"]), ("ra", I["rg_a"]), ("sub", I["diff_subln_g"]), ("gb", I["gate_b"]),
                      ("g2", I["norm2_g"]), ("fw", I["ffn_conv_w"]), ("fb", I["ffn_conv_b"]),
                      ("gm0", I["norm_mix_2"][0]), ("gm1", I["norm_mix_2"][1]), ("bg0", I["b_gate_2"][0]),
                      ("bg1", I["b_gate_2"][1]), ("gf0", I["norm_ffn_2"][0]), ("gf1", I["norm_ffn_2"][1])):
        at, n = PV[name]
        out[:, at:at + n] = c(arr)
    return out


def kernel(**inputs):
    import concourse.bacc as bacc
    from concourse.bass_utils import run_bass_kernel_spmd

    I = {k: np.asarray(x) for k, x in inputs.items()}
    consts, bias = constants()
    arrays = dict(consts)
    arrays["x"] = np.ascontiguousarray(I["x"][0])
    arrays["pv"] = pack_params(I)
    rg = np.concatenate([I["rg_w_r"][0], I["rg_w_i"][0]], 0)
    arrays["rg"] = rg.transpose(1, 0, 2).reshape(128, 2048)
    arrays["slabs"] = pack(I)
    arrays["bias"] = bias
    arrays["wf"] = np.ascontiguousarray(I["w_in"][0][:, 5120:5128])
    arrays["router"] = I["w_router_2"]
    arrays["rel"] = I["rel_bias"]
    arrays["fb"] = I["fox_b_f"][0]
    arrays["sink"] = I["sink_logit_2"].reshape(32)
    arrays["lq"] = np.concatenate([I[n][0] for n in ("diff_lq1", "diff_lk1", "diff_lq2", "diff_lk2")])
    arrays["final_g"] = I["final_g"]
    arrays["norm_final"] = I["norm_final_2"]
    arrays = {f"in_{k}": np.ascontiguousarray(x) for k, x in arrays.items()}
    nc = bacc.Bacc("TRN2", target_bir_lowering=False, num_devices=1)
    aps = {k[3:]: nc.dram_tensor(k, x.shape, F32, kind="ExternalInput").ap() for k, x in arrays.items()}
    out = nc.dram_tensor("out", [256, 1024], F32, kind="ExternalOutput").ap()
    build(nc, aps, out)
    r = run_bass_kernel_spmd(nc, [arrays], core_ids=[0])
    return r.results[0]["out"].reshape(1, 256, 1024)
```
